# Optimizing a Trainium2 kernel written in Bass

```python
import jax, jax.numpy as jnp
from jax import lax
import numpy as np

D_MODEL = 1024
BATCH = 1
SEQ = 2048
DEPTH = 2

CHUNK = 64
D_MIX = D_MODEL
N_GROUPS = 4
GROUP_W = D_MIX // N_GROUPS
HEAD_DIM = 64
N_HEADS_G = GROUP_W // HEAD_DIM
FOX_BLOCK = 128
SWA_WINDOW = 128
SWA_CHUNKS = SWA_WINDOW // CHUNK
SWA_KV_HEADS = 2
KV_W = SWA_KV_HEADS * HEAD_DIM
RWKV_LORA = 64
RWKV_PRE = 3 * GROUP_W + 2 * RWKV_LORA
CONV_WIDTH = 3
ROPE_THETA = 10000.0
EPS = 1e-6
RWKV_LN_EPS = 64e-5
IN_COLS = (GROUP_W, GROUP_W, GROUP_W, N_HEADS_G, GROUP_W,
           RWKV_PRE, GROUP_W,
           GROUP_W, KV_W, KV_W, GROUP_W,
           GROUP_W, GROUP_W, GROUP_W, GROUP_W)
D_IN = 3 * GROUP_W + N_HEADS_G + GROUP_W + RWKV_PRE + GROUP_W + GROUP_W + 2 * KV_W + GROUP_W + 4 * GROUP_W

kernel_name = "hybrid_fox_rwkv7_swa_shortconv_trunk"

def _split(t, sizes):
    idx = np.cumsum(np.array(sizes))[:-1].tolist()
    return jnp.split(t, idx, axis=-1)

def _rmsnorm(x, g):
    x32 = x.astype(jnp.float32)
    y = x32 * lax.rsqrt(jnp.mean(x32 * x32, axis=-1, keepdims=True) + EPS)
    return (y * g.astype(jnp.float32)).astype(x.dtype)

def _heads(t):
    B, S, W = t.shape
    return t.reshape(B, S, W // HEAD_DIM, HEAD_DIM)

def _rope(t, pos):
    half = t.shape[-1] // 2
    inv = ROPE_THETA ** (-jnp.arange(half, dtype=jnp.float32) / half)
    ang = pos.astype(jnp.float32)[:, None] * inv[None, :]
    cos = jnp.cos(ang)[None, :, None, :].astype(t.dtype)
    sin = jnp.sin(ang)[None, :, None, :].astype(t.dtype)
    t1, t2 = t[..., :half], t[..., half:]
    return jnp.concatenate([t1 * cos - t2 * sin, t2 * cos + t1 * sin], axis=-1)

def _fox_attention(q, k, v, f_logit, b_f, q_norm, k_norm):
    B, S, H, Dh = q.shape
    q = _rmsnorm(q, q_norm)
    k = _rmsnorm(k, k_norm)
    log_f = jax.nn.log_sigmoid((f_logit + b_f).astype(jnp.float32))
    Ft = jnp.cumsum(log_f, axis=1).transpose(0, 2, 1)
    nb = S // FOX_BLOCK
    qb = q.reshape(B, nb, FOX_BLOCK, H, Dh).transpose(1, 0, 2, 3, 4)
    Fb = Ft.reshape(B, H, nb, FOX_BLOCK).transpose(2, 0, 1, 3)
    scale = Dh ** -0.5
    kpos = jnp.arange(S)

    def block(args):
        i, qi, Fi = args
        s = jnp.einsum("bqhd,bkhd->bhqk", qi, k, preferred_element_type=jnp.float32) * scale
        s = s + Fi[..., :, None] - Ft[:, :, None, :]
        qpos = i * FOX_BLOCK + jnp.arange(FOX_BLOCK)
        s = jnp.where(kpos[None, :] <= qpos[:, None], s, -jnp.inf)
        p = jax.nn.softmax(s, axis=-1)
        return jnp.einsum("bhqk,bkhd->bqhd", p.astype(v.dtype), v)

    out = lax.map(block, (jnp.arange(nb), qb, Fb))
    return out.transpose(1, 0, 2, 3, 4).reshape(B, S, H * Dh)

def _rwkv7_time_mix(pre, mu, w0, w_up, a0, a_up, k_k, k_a, r_k, ln_g, ln_b):
    B, S, _ = pre.shape
    f32 = jnp.float32
    shifted = jnp.pad(pre, ((0, 0), (1, 0), (0, 0)))[:, :-1]
    xs = pre + (shifted - pre) * mu
    r, k, v, wd, ad = _split(xs, (GROUP_W, GROUP_W, GROUP_W, RWKV_LORA, RWKV_LORA))
    w = (w0 + jnp.tanh(wd) @ w_up).astype(f32)
    decay = jnp.exp(-jnp.exp(-jax.nn.softplus(-w) - 0.5))
    a = jax.nn.sigmoid((a0 + ad @ a_up).astype(f32))
    kk = _heads(k.astype(f32) * k_k.astype(f32))
    kk = kk / jnp.maximum(jnp.sqrt(jnp.sum(kk * kk, axis=-1, keepdims=True)), 1e-12)
    k_eff = k.astype(f32) * (1.0 + (a - 1.0) * k_a.astype(f32))
    r_h, w_h, k_h, v_h, a_h = (_heads(t) for t in (r.astype(f32), decay, k_eff, v.astype(f32), a))

    def step(state, inp):
        r_t, w_t, k_t, v_t, kk_t, a_t = inp
        sa = jnp.einsum("bhvk,bhk->bhv", state, -kk_t)
        state = (state * w_t[:, :, None, :] + sa[..., None] * (kk_t * a_t)[:, :, None, :]
                 + v_t[..., None] * k_t[:, :, None, :])
        return state, jnp.einsum("bhvk,bhk->bhv", state, r_t)

    seq = tuple(jnp.moveaxis(t, 1, 0) for t in (r_h, w_h, k_h, v_h, kk, a_h))
    state0 = jnp.zeros((B, N_HEADS_G, HEAD_DIM, HEAD_DIM), f32)
    _, y = lax.scan(step, state0, seq)
    y = jnp.moveaxis(y, 0, 1)
    mean = jnp.mean(y, axis=-1, keepdims=True)
    var = jnp.mean((y - mean) ** 2, axis=-1, keepdims=True)
    y = ((y - mean) * lax.rsqrt(var + RWKV_LN_EPS)).reshape(B, S, GROUP_W)
    y = y * ln_g.astype(f32) + ln_b.astype(f32)
    bonus = jnp.sum(r_h * k_h * r_k.astype(f32), axis=-1, keepdims=True) * v_h
    y = y + bonus.reshape(B, S, GROUP_W)
    return y.astype(pre.dtype)

def _swa_attention(q, k, v, sinks, q_norm, k_norm, pos):
    q = _rope(_rmsnorm(q, q_norm), pos)
    k = _rope(_rmsnorm(k, k_norm), pos)
    B, S, Hq, Dh = q.shape
    Hkv = k.shape[2]
    G = Hq // Hkv
    nc = S // CHUNK
    qc = q.reshape(B, nc, CHUNK, Hkv, G, Dh)

    def band(t):
        tc = t.reshape(B, nc, CHUNK, Hkv, Dh)
        padded = jnp.pad(tc, ((0, 0), (SWA_CHUNKS - 1, 0), (0, 0), (0, 0), (0, 0)))
        return jnp.concatenate([padded[:, j:j + nc] for j in range(SWA_CHUNKS)], axis=2)

    kb, vb = band(k), band(v)
    s = jnp.einsum("bcqhgd,bckhd->bchgqk", qc, kb, preferred_element_type=jnp.float32) * (Dh ** -0.5)
    key_chunk = (jnp.arange(nc)[:, None] - (SWA_CHUNKS - 1)
                 + jnp.arange(SWA_CHUNKS * CHUNK)[None, :] // CHUNK)
    s = jnp.where((key_chunk >= 0)[None, :, None, None, None, :], s, -jnp.inf)
    sink = jnp.broadcast_to(sinks.astype(jnp.float32).reshape(1, 1, Hkv, G, 1, 1), s.shape[:-1] + (1,))
    p = jax.nn.softmax(jnp.concatenate([s, sink], axis=-1), axis=-1)[..., :-1]
    out = jnp.einsum("bchgqk,bckhd->bcqhgd", p.astype(v.dtype), vb)
    return out.reshape(B, S, Hq * Dh)

def _short_conv(b_gate, c_gate, x_in, conv_w):
    u = c_gate * x_in
    y = lax.conv_general_dilated(u, conv_w[:, None, :], window_strides=(1,),
                                 padding=[(CONV_WIDTH - 1, 0)],
                                 dimension_numbers=("NWC", "WIO", "NWC"),
                                 feature_group_count=GROUP_W)
    return b_gate * y

def _hybrid_layer(x, pos, norm_g, w_in, fox_b_f, fox_q_norm, fox_k_norm, rwkv_mu, rwkv_w0,
                  rwkv_w_up, rwkv_a0, rwkv_a_up, rwkv_k_k, rwkv_k_a, rwkv_r_k, rwkv_ln_g,
                  rwkv_ln_b, swa_sinks, swa_q_norm, swa_k_norm, conv_w, w_out):
    B, S, _ = x.shape
    h = _rmsnorm(x, norm_g)
    proj = h @ w_in
    (fq, fk, fv, ff, fg, r_pre, rg, sq, sk, sv, sg, cb, cc, cx, cg) = _split(proj, IN_COLS)
    y_fox = _fox_attention(_heads(fq), _heads(fk), _heads(fv), ff, fox_b_f, fox_q_norm, fox_k_norm)
    y_rwkv = _rwkv7_time_mix(r_pre, rwkv_mu, rwkv_w0, rwkv_w_up, rwkv_a0, rwkv_a_up,
                             rwkv_k_k, rwkv_k_a, rwkv_r_k, rwkv_ln_g, rwkv_ln_b)
    y_swa = _swa_attention(_heads(sq), _heads(sk), _heads(sv), swa_sinks, swa_q_norm, swa_k_norm, pos)
    y_conv = _short_conv(cb, cc, cx, conv_w)
    mixed = jnp.concatenate([y_fox * jax.nn.silu(fg), y_rwkv * jax.nn.silu(rg),
                             y_swa * jax.nn.silu(sg), y_conv * jax.nn.silu(cg)], axis=-1)
    return x + mixed @ w_out

def setup_inputs(seed: int = 0) -> dict:
    key = jax.random.key(seed)
    ks = jax.random.split(key, 24)
    f32 = jnp.float32
    L = DEPTH

    def nrm(k, shape, scale):
        return jax.random.normal(k, shape, f32) * scale

    return {
        "x": nrm(ks[0], (BATCH, SEQ, D_MODEL), 1.0),
        "norm_g": 1.0 + nrm(ks[1], (L, D_MODEL), 0.02),
        "w_in": nrm(ks[2], (L, D_MODEL, D_IN), D_MODEL ** -0.5),
        "fox_b_f": 2.0 + nrm(ks[3], (L, N_HEADS_G), 0.5),
        "fox_q_norm": 1.0 + nrm(ks[4], (L, HEAD_DIM), 0.02),
        "fox_k_norm": 1.0 + nrm(ks[5], (L, HEAD_DIM), 0.02),
        "rwkv_mu": jax.random.uniform(ks[6], (L, RWKV_PRE), f32),
        "rwkv_w0": -3.0 + nrm(ks[7], (L, GROUP_W), 0.5),
        "rwkv_w_up": nrm(ks[8], (L, RWKV_LORA, GROUP_W), 0.1 * RWKV_LORA ** -0.5),
        "rwkv_a0": nrm(ks[9], (L, GROUP_W), 0.1),
        "rwkv_a_up": nrm(ks[10], (L, RWKV_LORA, GROUP_W), 0.5 * RWKV_LORA ** -0.5),
        "rwkv_k_k": 0.85 + nrm(ks[11], (L, GROUP_W), 0.05),
        "rwkv_k_a": 1.0 + nrm(ks[12], (L, GROUP_W), 0.05),
        "rwkv_r_k": nrm(ks[13], (L, N_HEADS_G, HEAD_DIM), 0.1),
        "rwkv_ln_g": 1.0 + nrm(ks[14], (L, GROUP_W), 0.02),
        "rwkv_ln_b": nrm(ks[15], (L, GROUP_W), 0.02),
        "swa_sinks": nrm(ks[16], (L, N_HEADS_G), 0.5),
        "swa_q_norm": 1.0 + nrm(ks[17], (L, HEAD_DIM), 0.02),
        "swa_k_norm": 1.0 + nrm(ks[18], (L, HEAD_DIM), 0.02),
        "conv_w": nrm(ks[19], (L, CONV_WIDTH, GROUP_W), CONV_WIDTH ** -0.5),
        "w_out": nrm(ks[20], (L, D_MIX, D_MODEL), D_MIX ** -0.5),
    }

def reference(x, norm_g, w_in, fox_b_f, fox_q_norm, fox_k_norm, rwkv_mu, rwkv_w0, rwkv_w_up,
              rwkv_a0, rwkv_a_up, rwkv_k_k, rwkv_k_a, rwkv_r_k, rwkv_ln_g, rwkv_ln_b,
              swa_sinks, swa_q_norm, swa_k_norm, conv_w, w_out):
    pos = jnp.arange(x.shape[1])
    for l in range(DEPTH):
        x = _hybrid_layer(x, pos, norm_g[l], w_in[l], fox_b_f[l], fox_q_norm[l], fox_k_norm[l],
                          rwkv_mu[l], rwkv_w0[l], rwkv_w_up[l], rwkv_a0[l], rwkv_a_up[l],
                          rwkv_k_k[l], rwkv_k_a[l], rwkv_r_k[l], rwkv_ln_g[l], rwkv_ln_b[l],
                          swa_sinks[l], swa_q_norm[l], swa_k_norm[l], conv_w[l], w_out[l])
    return x


_drawn_inputs = setup_inputs


def setup_inputs(seed=0):
    import zlib

    import numpy as np

    out = dict(_drawn_inputs(seed))
    spreads = {}
    factors = {'fox_q_norm': 8.0,
     'fox_k_norm': 8.0,
     'rwkv_w_up': 8.0,
     'rwkv_a0': 3.029,
     'rwkv_k_k': 4.39,
     'rwkv_ln_g': 7.222,
     'rwkv_ln_b': 6.724,
     'swa_sinks': 8.0,
     'swa_q_norm': 8.0,
     'swa_k_norm': 8.0}
    for name, (base, spread) in spreads.items():
        noise = np.random.default_rng([zlib.crc32(name.encode()), seed]).standard_normal(out[name].shape)
        drawn = base * np.exp(spread * noise) if base else spread * noise
        out[name] = __import__('jax').numpy.asarray(drawn.astype(out[name].dtype))
    for name, factor in factors.items():
        out[name] = (out[name] * factor).astype(out[name].dtype)
    return out
```

```python
import concourse.bass as bass
from concourse import mybir
from contextlib import ExitStack
import numpy as np

F32 = mybir.dt.float32
F32R = mybir.dt.float32r
BF16 = mybir.dt.bfloat16
ALU = mybir.AluOpType
ACT = mybir.ActivationFunctionType
AX = mybir.AxisListType

L, T, DM = 2, 2048, 1024
GW, HD, NH = 256, 64, 4
DIN = 3972
KC = DM // 128
TB = 512
NB = T // TB
NT = T // 128
PAD = 64
CH = 64
R_FQ, R_FK, R_FV, R_FF, R_FG = 0, 256, 512, 768, 772
R_PRE, R_RG, R_SQ, R_SK, R_SV, R_SG = 1028, 1924, 2180, 2436, 2564, 2692
R_CB, R_CC, R_CX, R_CG = 2948, 3204, 3460, 3716
C_NG, C_MU, C_W0, C_A0, C_KK, C_KA, C_RK, C_LG, C_LB = 0, 8, 15, 17, 19, 21, 23, 25, 27
C_GN, C_CW, C_SINK, C_BF, NPAR = 29, 36, 42, 46, 47
EPS, LN_EPS = 1e-6, 64e-5
CDEC = -0.5 * float(np.exp(-0.5))


class Phase:
    def __init__(self, nc, ctx, name):
        self.nc, self.ctx, self.name = nc, ctx, name
        self.sems = []
        ctx.callback(self.close)

    def close(self):
        self.nc.clear_and_free_semaphores(self.sems)
        self.nc.all_engine_barrier(sem_only=True)

    def sb(self, n, shape, dt=F32):
        return self.ctx.enter_context(self.nc.sbuf_tensor(f"{self.name}_{n}", shape, dt))

    def ps(self, n, shape, dt=F32):
        return self.ctx.enter_context(self.nc.psum_tensor(f"{self.name}_{n}", shape, dt))

    def sem(self, n):
        self.sems.append(self.nc.alloc_semaphore(f"{self.name}_{n}"))
        return self.sems[-1]


def lay(t, l):
    v = t[bass.ds(l, 1)]
    return v.rearrange("a p n -> (a p) n")


def phase_transpose(nc, consts, source, target, projT=None):
    with ExitStack() as ctx:
        to_channels = projT is not None
        P = Phase(nc, ctx, "lx" if to_channels else "sx")
        two = range(2)
        ident = P.sb("ident", [128, 128])
        xin, xo = ([P.sb(f"{n}{q}", [128, KC, 128]) for q in two] for n in ("xin", "xo"))
        zero = P.sb("zero", [128, PAD])
        pt = [P.ps(f"pt{q}", [128, KC, 128]) for q in two]
        c_in, z_rdy, z_st = (P.sem(n) for n in ("c_in", "z_rdy", "z_st"))
        x_in, x_free, t_done, t_free, o_rdy, st = ([P.sem(f"{n}{q}") for q in two] for n in ("x_in", "x_free", "t_done", "t_free", "o_rdy", "st"))
        block = ctx.enter_context(nc.Block())

        def tile(x, t, channels):
            if channels:
                return x[:, bass.ds(t * 128, 128)].rearrange("(k p) t -> p k t", p=128)
            return x[bass.ds(t * 128, 128), :].rearrange("p (k c) -> p k c", k=KC)

        @block.sync
        def _(sp):
            sp.dma_start(ident[:], consts[:, 0:128]).then_inc(c_in, 16)

            def load(t, q):
                sp.wait_ge(x_free[q], 1)
                sp.sem_inc(x_free[q], -1)
                sp.dma_start(xin[q][:], tile(source, t, not to_channels)).then_inc(x_in[q], 16)

            def store(t, q):
                sp.wait_ge(o_rdy[q], 1)
                sp.sem_inc(o_rdy[q], -1)
                sp.dma_start(tile(target, t, to_channels), xo[q][:]).then_inc(st[q], 16)

            load(0, 0)
            with sp.Fori(0, NT // 2 - 1) as i:
                for q in two:
                    load(i * 2 + (1 + q), 1 - q)
                    store(i * 2 + q, q)
            load(NT - 1, 1)
            for q in two:
                store(NT - 2 + q, q)
            if to_channels:
                sp.wait_ge(z_rdy, 1)
                for r in range(R_PRE, DIN, 128):
                    sp.dma_start(projT[r:r + 128, 0:PAD], zero[0:min(128, DIN - r), :]).then_inc(z_st, 16)
                sp.wait_ge(z_st, 16 * len(range(R_PRE, DIN, 128)))
            for q in two:
                sp.wait_ge(st[q], 16)

        @block.tensor
        def _(pe):
            pe.wait_ge(c_in, 16)
            with pe.Fori(0, NT // 2) as i:
                for q in two:
                    pe.wait_ge(x_in[q], 16)
                    pe.sem_inc(x_in[q], -16)
                    pe.wait_ge(t_free[q], 1)
                    pe.sem_inc(t_free[q], -1)
                    for k in range(KC):
                        ins = nc.tensor.transpose(pt[q][:, k, :], xin[q][:, k, :], ident[:])
                    ins.then_inc(t_done[q], 1)

        @block.vector
        def _(v):
            if to_channels:
                nc.vector.memset(zero[:], 0.0).then_inc(z_rdy, 1)
            for q in two:
                v.sem_inc(x_free[q], 1)
                v.sem_inc(t_free[q], 1)
                v.sem_inc(st[q], 16)
            with v.Fori(0, NT // 2) as i:
                for q in two:
                    v.wait_ge(t_done[q], 1)
                    v.sem_inc(t_done[q], -1)
                    v.sem_inc(x_free[q], 1)
                    v.wait_ge(st[q], 16)
                    v.sem_inc(st[q], -16)
                    nc.vector.tensor_copy(xo[q][:], pt[q][:]).then_inc(o_rdy[q], 1)
                    v.drain().then_inc(t_free[q], 1)


class Projector:
    def __init__(self, P, nc, l, w_in, h_hi, h_lo, projT):
        self.nc, self.wl, self.h_hi, self.h_lo, self.projT = nc, lay(w_in, l), h_hi, h_lo, projT
        self.raw = P.sb("raw", [128, KC, 128])
        self.w_hi = [P.sb(f"w_hi{q}", [128, KC, 128], F32R) for q in range(2)]
        self.w_lo = [P.sb(f"w_lo{q}", [128, KC, 128], F32R) for q in range(2)]
        self.stage = [P.sb(f"stage{q}", [128, TB]) for q in range(2)]
        self.acc = [P.ps(f"acc{q}", [128, TB]) for q in range(2)]
        self.raw_in, self.raw_free, self.whi_rdy = P.sem("raw_in"), P.sem("raw_free"), P.sem("whi_rdy")
        self.w_rdy, self.w_free, self.acc_rdy, self.acc_free, self.stage_rdy, self.stage_st = (
            [P.sem(f"{n}{q}") for q in range(2)] for n in ("w_rdy", "w_free", "acc_rdy", "acc_free", "stage_rdy", "stage_st"))

    def act_start(self, act):
        act.sem_inc(self.raw_free, 1)
        act.sem_inc(self.w_free[0], 1)
        for q in range(2):
            act.sem_inc(self.acc_free[q], 1)
            act.sem_inc(self.stage_st[q], 16)

    def act_load(self, act, r, m=128):
        act.wait_ge(self.raw_free, 1)
        act.sem_inc(self.raw_free, -1)
        act.dma_start(self.raw[:, :, 0:m], self.wl[:, bass.ds(r, m)].rearrange("(k p) c -> p k c", p=128)).then_inc(self.raw_in, 16)

    def act_split(self, act, q, m=128):
        act.wait_ge(self.raw_in, 16)
        act.sem_inc(self.raw_in, -16)
        act.wait_ge(self.w_free[q], 1)
        act.sem_inc(self.w_free[q], -1)
        self.nc.scalar.activation(self.w_hi[q][:, :, 0:m], self.raw[:, :, 0:m], ACT.Copy).then_inc(self.whi_rdy, 1)

    def pool_weights(self, pool, q, m=128):
        pool.wait_ge(self.whi_rdy, 1)
        pool.sem_inc(self.whi_rdy, -1)
        self.nc.gpsimd.tensor_tensor(self.w_lo[q][:, :, 0:m], self.raw[:, :, 0:m], self.w_hi[q][:, :, 0:m].bitcast(F32), ALU.subtract).then_inc(self.w_rdy[q], 1)
        pool.drain().then_inc(self.raw_free, 1)

    def pe_tile(self, pe, q, m=128):
        M = self.nc.tensor.matmul
        pe.wait_ge(self.w_rdy[q], 1)
        pe.sem_inc(self.w_rdy[q], -1)
        for b in range(NB):
            pe.wait_ge(self.acc_free[b % 2], 1)
            pe.sem_inc(self.acc_free[b % 2], -1)
            cols, acc = slice(b * TB, (b + 1) * TB), self.acc[b % 2][0:m, :]
            for k in range(KC):
                ins = M(acc, self.w_hi[q][:, k, 0:m], self.h_hi[:, k, cols], start=(k == 0), stop=False)
                if b == 0 and k == 0:
                    ins.then_inc(self.w_free[1 - q], 1)
                yield
                M(acc, self.w_hi[q][:, k, 0:m], self.h_lo[:, k, cols], start=False, stop=False)
                yield
                ins = M(acc, self.w_lo[q][:, k, 0:m], self.h_hi[:, k, cols], start=False, stop=(k == KC - 1))
                if k == KC - 1:
                    ins.then_inc(self.acc_rdy[b % 2], 1)
                yield

    def evacuate(self, eng, copy, b, m=128):
        eng.wait_ge(self.acc_rdy[b % 2], 1)
        eng.sem_inc(self.acc_rdy[b % 2], -1)
        eng.wait_ge(self.stage_st[b % 2], 16)
        eng.sem_inc(self.stage_st[b % 2], -16)
        copy(self.stage[b % 2][0:m, :], self.acc[b % 2][0:m, :]).then_inc(self.stage_rdy[b % 2], 1)
        eng.drain().then_inc(self.acc_free[b % 2], 1)

    def sp_store(self, sp, r, b, m=128):
        sp.wait_ge(self.stage_rdy[b % 2], 1)
        sp.sem_inc(self.stage_rdy[b % 2], -1)
        sp.dma_start(self.projT[bass.ds(r, m), PAD + b * TB:PAD + (b + 1) * TB], self.stage[b % 2][0:m, :]).then_inc(self.stage_st[b % 2], 16)


def phase_project(nc, l, xT, w_in, par, consts, projT, h_hi, h_lo):
    with ExitStack() as ctx:
        P = Phase(nc, ctx, "pj")
        pars = P.sb("pars", [128, NPAR])
        ones = P.sb("ones", [128, 128])
        NX, XB = 4, 256
        xb = [P.sb(f"xb{q}", [128, KC, XB]) for q in range(NX)]
        sq, rst = P.sb("sq", [128, KC, XB]), P.sb("rst", [128, XB])
        ss = P.ps("ss", [128, XB])
        names = ("c_in", "sq_rdy", "ss_rdy", "ss_free", "var_rdy", "r_rdy", "h_rdy", "hi_rdy", "h_all")
        s = {n: P.sem(n) for n in names}
        x_in, x_free = ([P.sem(f"{n}{q}") for q in range(NX)] for n in ("x_in", "x_free"))
        J = Projector(P, nc, l, w_in, h_hi, h_lo, projT)
        block = ctx.enter_context(nc.Block())
        HK = KC // 2

        assert (R_RG - R_PRE) % 256 == 128

        def pairs(eng, body):
            with eng.Fori(0, (R_RG - R_PRE) // 256) as i:
                body(i * 256 + R_PRE, i * 256 + (R_PRE + 128), 128, i * 256 + (R_PRE + 256))
            body(R_RG - 128, R_FF, NH, None)

        @block.sync
        def _(sp):
            sp.dma_start(pars[:], lay(par, l)).then_inc(s["c_in"], 16)
            sp.dma_start(ones[:], consts[:, 128:256]).then_inc(s["c_in"], 16)
            for i in range(T // XB):
                sp.wait_ge(x_free[i % NX], 1)
                sp.sem_inc(x_free[i % NX], -1)
                sp.dma_start(xb[i % NX][:], xT[:, i * XB:(i + 1) * XB].rearrange("(k p) t -> p k t", p=128)).then_inc(x_in[i % NX], 16)

            def body(r0, r1, m1, r2):
                for r, m in ((r0, 128), (r1, m1)):
                    for b in range(NB):
                        J.sp_store(sp, r, b, m)
            pairs(sp, body)
            for q in range(2):
                sp.wait_ge(J.stage_st[q], 16)

        @block.scalar
        def _(act):
            A = nc.scalar.activation
            J.act_start(act)

            def square(i):
                act.wait_ge(x_in[i % NX], 16)
                act.sem_inc(x_in[i % NX], -16)
                A(sq[:], xb[i % NX][:], ACT.Square).then_inc(s["sq_rdy"], 1)

            square(0)
            J.act_load(act, R_PRE)
            for i in range(T // XB):
                act.wait_ge(s["var_rdy"], 1)
                act.sem_inc(s["var_rdy"], -1)
                if i + 1 < T // XB:
                    square(i + 1)
                A(rst[:], rst[:], ACT.Ln)
                act.drain()
                A(rst[:], rst[:], ACT.Exp, scale=-0.5).then_inc(s["r_rdy"], 1)
                for c in (0, HK):
                    act.wait_ge(s["h_rdy"], 1)
                    act.sem_inc(s["h_rdy"], -1)
                    A(h_hi[:, c:c + HK, i * XB:(i + 1) * XB], xb[i % NX][:, c:c + HK, :], ACT.Copy).then_inc(s["hi_rdy"], 1)

            def body(r0, r1, m1, r2):
                J.act_split(act, 0)
                J.act_load(act, r1, m1)
                J.act_split(act, 1, m1)
                if r2 is not None:
                    J.act_load(act, r2)
            pairs(act, body)

        @block.gpsimd
        def _(pool):
            for q in range(NX):
                pool.sem_inc(x_free[q], 1)
            for i in range(T // XB):
                for c in (0, HK):
                    dst = slice(i * XB, (i + 1) * XB)
                    pool.wait_ge(s["hi_rdy"], 1)
                    pool.sem_inc(s["hi_rdy"], -1)
                    ins = nc.gpsimd.tensor_tensor(h_lo[:, c:c + HK, dst], xb[i % NX][:, c:c + HK, :], h_hi[:, c:c + HK, dst].bitcast(F32), ALU.subtract)
                ins.then_inc(x_free[i % NX], 1)
            pool.drain().then_inc(s["h_all"], 1)

            def body(r0, r1, m1, r2):
                J.pool_weights(pool, 0)
                J.pool_weights(pool, 1, m1)
            pairs(pool, body)

        @block.tensor
        def _(pe):
            pe.wait_ge(s["c_in"], 32)
            for i in range(T // XB):
                pe.wait_ge(s["sq_rdy"], 1)
                pe.sem_inc(s["sq_rdy"], -1)
                pe.wait_ge(s["ss_free"], 1)
                pe.sem_inc(s["ss_free"], -1)
                for k in range(KC):
                    ins = nc.tensor.matmul(ss[:], ones[:], sq[:, k, :], start=(k == 0), stop=(k == KC - 1))
                ins.then_inc(s["ss_rdy"], 1)
            pe.wait_ge(s["h_all"], 1)

            def body(r0, r1, m1, r2):
                for _ in J.pe_tile(pe, 0):
                    pass
                for _ in J.pe_tile(pe, 1, m1):
                    pass
            pairs(pe, body)

        @block.vector
        def _(v):
            V = nc.vector
            v.wait_ge(s["c_in"], 32)
            v.sem_inc(s["ss_free"], 1)
            for i in range(T // XB):
                x = xb[i % NX]
                v.wait_ge(s["ss_rdy"], 1)
                v.sem_inc(s["ss_rdy"], -1)
                v.drain()
                V.tensor_scalar(rst[:], ss[:], 1.0 / DM, EPS, ALU.mult, ALU.add).then_inc(s["var_rdy"], 1)
                v.drain().then_inc(s["ss_free"], 1)
                v.wait_ge(s["r_rdy"], 1)
                v.sem_inc(s["r_rdy"], -1)
                for k in range(KC):
                    ins = V.scalar_tensor_tensor(x[:, k, :], x[:, k, :], pars[:, C_NG + k:C_NG + k + 1], rst[:], ALU.mult, ALU.mult)
                    if k % HK == HK - 1:
                        ins.then_inc(s["h_rdy"], 1)

            def body(r0, r1, m1, r2):
                for m in (128, m1):
                    for b in range(NB):
                        J.evacuate(v, nc.vector.tensor_copy, b, m)
            pairs(v, body)


PREP_FILL = (("th", 16), ("lora", 24), ("ssk", 20), ("bs", 36))
SCAN_FILL = (("tok", 6), ("mk", 4), ("s3", 5), ("s4", 5), ("s5", 7), ("s6", 6), ("s7", 7), ("s8", 6), ("s9", 7), ("wz", 7), ("g", 8), ("c0", 8), ("c1", 20))
assert sum(n for _, n in PREP_FILL) == sum(n for _, n in SCAN_FILL) == 3 * KC * NB


def units_done(plan, stage):
    unit, before = 3 * KC, 0
    for name, n in plan:
        if name == stage:
            return range(before // unit, (before + n) // unit)
        before += n


def phase_rwkv_prep(nc, l, projT, par, lora, consts, rw, pend, w_in, h_hi, h_lo):
    with ExitStack() as ctx:
        P = Phase(nc, ctx, "rp")
        two = range(2)
        PB = 256
        NU = T // PB
        assert NU == (R_FF + GW) // 128 and NU % 2 == 0
        pars, half = P.sb("pars", [128, NPAR]), P.sb("half", [128, NPAR])
        bones, cmask = P.sb("bones", [128, 128]), P.sb("cmask", [128, PB])
        up = P.sb("up", [128, GW])
        pre = [P.sb(f"pre{q}", [128, 7, PB + 1]) for q in two]
        dif, xs = P.sb("dif", [128, 7, PB]), P.sb("xs", [128, 7, PB])
        lw, ta2, cum, cmp_, pi, kkr, ta, tb, tk_, tr, keff, bv = (P.sb(n, [128, 2, PB]) for n in (
            "lw", "ta2", "cum", "cmp", "pi", "kkr", "ta", "tb", "tk", "tr", "keff", "bv"))
        th, sqk, rk, nrm, pp, pq = dif[0:64, 6, :], dif[:, 0:2, :], dif[:, 2:4, :], dif[:, 4:6, :], lw, cmp_
        pend_sb = P.sb("pend", [128, 2, T // CH])
        pw, pa, pk, pb = (P.ps(n, [128, 2, PB]) for n in ("pw", "pa", "pk", "pb"))
        names = ("c_in", "half_rdy", "xs_rdy", "v_rdy", "v_st", "th_rdy", "lora_rdy", "t_rdy", "cum_rdy", "exp_rdy", "sqk_rdy", "ssk_rdy", "mx_rdy", "nrm_rdy", "rk_rdy", "bs_rdy", "out_rdy", "out_st", "pend_st")
        s = {n: P.sem(n) for n in names}
        p_in, pre_free = ([P.sem(f"{n}{q}") for q in two] for n in ("p_in", "pre_free"))
        J = Projector(P, nc, l, w_in, h_hi, h_lo, projT)
        block = ctx.enter_context(nc.Block())

        def units(eng, body):
            with eng.Fori(0, R_FF // 256 - 1) as i:
                body(i * 2, 0, i * 256, i * 256 + 128)
                body(i * 2 + 1, 1, i * 256 + 128, i * 256 + 256)
            body(NU - 4, 0, R_FF - 256, R_FF - 128)
            body(NU - 3, 1, R_FF - 128, R_FG)
            body(NU - 2, 0, R_FG, R_FG + 128)
            body(NU - 1, 1, R_FG + 128, None)

        @block.sync
        def _(sp):
            sp.dma_start(pars[:], lay(par, l)).then_inc(s["c_in"], 16)
            sp.dma_start(bones[:], consts[:, 256:384]).then_inc(s["c_in"], 16)
            sp.dma_start(cmask[:], consts[:, 384:384 + PB]).then_inc(s["c_in"], 16)
            sp.dma_start(up[:], lay(lora, l)).then_inc(s["c_in"], 16)

            def load(i, q):
                sp.wait_ge(pre_free[q], 1)
                sp.sem_inc(pre_free[q], -1)
                sp.dma_start(pre[q][:], projT[R_PRE:R_PRE + 896, bass.ds(i * PB + (PAD - 1), PB + 1)].rearrange("(k p) t -> p k t", p=128)).then_inc(p_in[q], 16)

            def put(i, n, buf, sem):
                sp.dma_start(rw[n * GW:(n + 1) * GW, bass.ds(i * PB, PB)].rearrange("(k p) t -> p k t", p=128), buf).then_inc(sem, 16)

            def body(i, q, row, follows):
                if follows is not None:
                    load(i + 1, 1 - q)
                sp.wait_ge(s["v_rdy"], 1)
                sp.sem_inc(s["v_rdy"], -1)
                put(i, 4, xs[:, 4:6, :], s["v_st"])
                J.sp_store(sp, row, 0)
                J.sp_store(sp, row, 1)
                sp.wait_ge(s["out_rdy"], 1)
                sp.sem_inc(s["out_rdy"], -1)
                for n, buf in ((0, ta), (1, tr), (2, tb), (3, tk_), (5, bv)):
                    put(i, n, buf[:], s["out_st"])
                J.sp_store(sp, row, 2)
                J.sp_store(sp, row, 3)

            load(0, 0)
            units(sp, body)
            sp.dma_start(pend.rearrange("(k p) c -> p k c", p=128), pend_sb[:]).then_inc(s["pend_st"], 16)
            sp.wait_ge(s["pend_st"], 16)
            sp.wait_ge(s["v_st"], 16)
            sp.wait_ge(s["out_st"], 80)
            for q in two:
                sp.wait_ge(J.stage_st[q], 16)

        @block.vector
        def _(v):
            V = nc.vector
            v.wait_ge(s["c_in"], 64)
            V.tensor_scalar(half[:], pars[:], 0.5, None, ALU.mult).then_inc(s["half_rdy"], 1)
            for q in two:
                v.sem_inc(pre_free[q], 1)
            v.sem_inc(s["v_st"], 16)
            v.sem_inc(s["out_st"], 80)
            v.drain()
            r_, k_, v_ = xs[:, 0:2, :], xs[:, 2:4, :], xs[:, 4:6, :]

            def body(i, q, row, follows):
                x = pre[q]
                v.wait_ge(p_in[q], 16)
                v.sem_inc(p_in[q], -16)
                V.tensor_tensor(dif[:], x[:, :, 0:PB], x[:, :, 1:PB + 1], ALU.subtract)
                v.drain()
                v.wait_ge(s["v_st"], 16)
                v.sem_inc(s["v_st"], -16)
                for j in (6, 2, 3, 0, 1, 4, 5):
                    ins = V.scalar_tensor_tensor(xs[:, j, :], dif[:, j, :], pars[:, C_MU + j:C_MU + j + 1], x[:, j, 1:PB + 1], ALU.mult, ALU.add)
                    if j == 6:
                        ins.then_inc(s["xs_rdy"], 1)
                ins.then_inc(s["v_rdy"], 1)
                v.drain().then_inc(pre_free[q], 1)
                for p in two:
                    V.tensor_scalar(kkr[:, p, :], k_[:, p, :], pars[:, C_KK + p:C_KK + p + 1], None, ALU.mult)
                v.drain()
                V.tensor_tensor(sqk, kkr[:], kkr[:], ALU.mult).then_inc(s["sqk_rdy"], 1)
                v.wait_ge(s["t_rdy"], 1)
                v.sem_inc(s["t_rdy"], -1)
                V.tensor_scalar(lw[:], lw[:], CDEC, CDEC, ALU.mult, ALU.add)
                for p in two:
                    V.tensor_scalar(keff[:, p, :], ta2[:, p, :], -1.0, half[:, C_KA + p:C_KA + p + 1], ALU.add, ALU.mult)
                v.drain()
                for p in two:
                    V.tensor_tensor_scan(cum[:, p, :], cmask[:], lw[:, p, :], 0.0, ALU.mult, ALU.add)
                V.scalar_tensor_tensor(keff[:], keff[:], 1.0, k_, ALU.add, ALU.mult)
                v.drain()
                V.tensor_tensor(cmp_[:], cum[:], lw[:], ALU.subtract).then_inc(s["cum_rdy"], 1)
                for p in two:
                    ins = V.scalar_tensor_tensor(rk[:, p, :], r_[:, p, :], pars[:, C_RK + p:C_RK + p + 1], keff[:, p, :], ALU.mult, ALU.mult)
                ins.then_inc(s["rk_rdy"], 1)
                v.wait_ge(s["ssk_rdy"], 1)
                v.sem_inc(s["ssk_rdy"], -1)
                V.tensor_scalar(nrm, pk[:], 1e-24, None, ALU.max).then_inc(s["mx_rdy"], 1)
                v.wait_ge(s["exp_rdy"], 1)
                v.sem_inc(s["exp_rdy"], -1)
                v.wait_ge(s["out_st"], 80)
                v.sem_inc(s["out_st"], -80)
                V.tensor_tensor(tk_[:], keff[:], pi[:], ALU.mult)
                V.tensor_tensor(tr[:], r_, pp[:], ALU.mult)
                V.tensor_copy(pend_sb[:, :, bass.ds(i * (PB // CH), PB // CH)], pp[:, :, CH - 1::CH])
                v.wait_ge(s["nrm_rdy"], 1)
                v.sem_inc(s["nrm_rdy"], -1)
                V.tensor_tensor(kkr[:], kkr[:], nrm, ALU.mult)
                v.drain()
                V.scalar_tensor_tensor(ta[:], pq[:], -1.0, kkr[:], ALU.mult, ALU.mult)
                V.scalar_tensor_tensor(tb[:], ta2[:], 1.0, kkr[:], ALU.add, ALU.mult)
                v.drain()
                V.scalar_tensor_tensor(tb[:], tb[:], 0.5, pi[:], ALU.mult, ALU.mult)
                v.wait_ge(s["bs_rdy"], 1)
                v.sem_inc(s["bs_rdy"], -1)
                V.tensor_tensor(bv[:], pb[:], v_, ALU.mult).then_inc(s["out_rdy"], 1)
            units(v, body)

        @block.scalar
        def _(act):
            A = nc.scalar.activation
            C = nc.scalar.copy
            J.act_start(act)

            def evac(stage):
                for b in units_done(PREP_FILL, stage):
                    J.evacuate(act, C, b)

            def body(i, q, row, follows):
                if follows is not None:
                    J.act_load(act, follows)
                act.wait_ge(s["xs_rdy"], 1)
                act.sem_inc(s["xs_rdy"], -1)
                A(th, xs[0:64, 6, :], ACT.Tanh).then_inc(s["th_rdy"], 1)
                evac("th")
                act.wait_ge(s["lora_rdy"], 1)
                act.sem_inc(s["lora_rdy"], -1)
                for p in two:
                    A(lw[:, p, :], pw[:, p, :], ACT.Tanh, bias=half[:, C_W0 + p:C_W0 + p + 1], scale=0.5)
                for p in two:
                    ins = A(ta2[:, p, :], pa[:, p, :], ACT.Tanh, bias=half[:, C_A0 + p:C_A0 + p + 1], scale=0.5)
                ins.then_inc(s["t_rdy"], 1)
                evac("lora")
                act.wait_ge(s["cum_rdy"], 1)
                act.sem_inc(s["cum_rdy"], -1)
                A(pi[:], cum[:], ACT.Exp, scale=-1.0)
                A(pq[:], cmp_[:], ACT.Exp)
                A(pp[:], cum[:], ACT.Exp).then_inc(s["exp_rdy"], 1)
                act.wait_ge(s["mx_rdy"], 1)
                act.sem_inc(s["mx_rdy"], -1)
                A(nrm, nrm, ACT.Ln)
                act.drain()
                A(nrm, nrm, ACT.Exp, scale=-0.5).then_inc(s["nrm_rdy"], 1)
                if follows is not None:
                    J.act_split(act, 1 - q)
                evac("ssk")
                evac("bs")

            act.wait_ge(s["half_rdy"], 1)
            J.act_load(act, 0)
            J.act_split(act, 0)
            units(act, body)

        @block.gpsimd
        def _(pool):
            units(pool, lambda i, q, row, follows: J.pool_weights(pool, q))

        @block.tensor
        def _(pe):
            M = nc.tensor.matmul
            pe.wait_ge(s["c_in"], 64)

            def body(i, q, row, follows):
                tile = J.pe_tile(pe, q)

                def fill(stage):
                    for _ in range(dict(PREP_FILL)[stage]):
                        next(tile)

                fill("th")
                pe.wait_ge(s["th_rdy"], 1)
                pe.sem_inc(s["th_rdy"], -1)
                for p in two:
                    M(pw[:, p, :], up[0:64, p * 128:(p + 1) * 128], th, start=True, stop=True)
                for p in two:
                    ins = M(pa[:, p, :], up[64:128, p * 128:(p + 1) * 128], xs[64:128, 6, :], start=True, stop=True)
                ins.then_inc(s["lora_rdy"], 1)
                fill("lora")
                pe.wait_ge(s["sqk_rdy"], 1)
                pe.sem_inc(s["sqk_rdy"], -1)
                for p in two:
                    ins = M(pk[:, p, :], bones[:], sqk[:, p, :], start=True, stop=True)
                ins.then_inc(s["ssk_rdy"], 1)
                fill("ssk")
                pe.wait_ge(s["rk_rdy"], 1)
                pe.sem_inc(s["rk_rdy"], -1)
                for p in two:
                    ins = M(pb[:, p, :], bones[:], rk[:, p, :], start=True, stop=True)
                ins.then_inc(s["bs_rdy"], 1)
                fill("bs")
            units(pe, body)


def phase_rwkv_scan(nc, l, rw, pend, consts, masks, mixT, w_in, projT, h_hi, h_lo):
    with ExitStack() as ctx:
        P = Phase(nc, ctx, "rs")
        two = range(2)
        ident = P.sb("ident", [128, 128])
        mk = P.sb("mk", [128, 6, 128])
        ar = [P.sb(f"ar{e}", [64, NH, 2, 128]) for e in two]
        bt, kt, vt = (P.sb(n, [64, NH, 128]) for n in ("bt", "kt", "vt"))
        pe_all = P.sb("pend", [64, NH, T // CH])
        aq = P.sb("aq", [128, NH, 128])
        bm, km = P.sb("bm", [128, 2, NH, 64]), P.sb("km", [128, 2, NH, 64])
        vm = P.sb("vm", [128, NH, 64])
        D, E1, E2, Dt, p2, p4, p4t, x1 = (P.sb(n, [128, NH, 128]) for n in ("D", "E1", "E2", "Dt", "p2", "p4", "p4t", "x1"))
        p8, xn, yy, wz, m1 = D, p2, p4, Dt, p2[0:64]
        gt = p4t[0:64].rearrange("p h (u t) -> p h u t", u=2)
        px = P.sb("px", [128, NH, 2, 128])
        arb = P.sb("arb", [128, NH, 128])
        ak = P.sb("ak", [128, NH, 2, 128])
        S = P.sb("S", [64, 2, NH, 64])
        yst = P.sb("yst", [64, NH, 128])
        bk = P.ps("bk", [128, 6, 512])
        J = Projector(P, nc, l, w_in, h_hi, h_lo, projT)

        def bank(i, w=128):
            return bk[:, i, 0:NH * w].rearrange("p (h t) -> p h t", h=NH)

        two12 = bk[:, 1:3, :].rearrange("p b (h u t) -> p (b h) u t", h=2, u=2)
        two45 = bk[:, 4:6, :].rearrange("p b (h u t) -> p (b h) u t", h=2, u=2)
        sems = ("c_in", "tok", "n_rdy", "mb", "mk", "tok_ev", "d_rdy", "ak_rdy", "p2_m", "p2t_m", "p2_a", "p2_d", "s3a", "s3d", "p4_a", "p4t_d", "x2_d", "s4a", "s4d", "p8_a", "x3_d",
                "s5", "x4", "s6a", "s6d", "x4_a", "y_d", "s7", "x5", "s8a", "s8d", "x5_a", "y2_d", "s9", "x6", "q_m", "q_a", "wz_m", "wz_d", "g_m", "g_d", "s_m", "s_d", "s2_m", "s2_d", "y_m", "y_a", "y_st", "y_ev", "i_ok")
        s = {n: P.sem(n) for n in sems}
        i_in, in_free = [P.sem(f"i_in{e}") for e in two], [P.sem(f"in_free{e}") for e in two]
        b_free = P.sem("b_free")
        block = ctx.enter_context(nc.Block())
        rh = rw.rearrange("(n h c) t -> n c h t", h=NH, c=64)
        assert R_RG + NT * 128 == DIN

        def tiles(eng, body):
            with eng.Fori(0, NT // 2) as i:
                for e in two:
                    body(i * 2 + e, i * 256 + (R_RG + e * 128), e)

        @block.sync
        def _(sp):
            sp.dma_start(ident[:], consts[:, 0:128]).then_inc(s["c_in"], 16)
            sp.dma_start(mk[:], masks.rearrange("p (k t) -> p k t", t=128)[:, 0:6, :]).then_inc(s["c_in"], 16)
            sp.dma_start(pe_all[:], pend.rearrange("(h c) n -> c h n", c=64)).then_inc(s["c_in"], 16)

            def load(t, e):
                sp.wait_ge(in_free[e], 1)
                sp.sem_inc(in_free[e], -1)
                cols = bass.ds(t * 128, 128)
                sp.dma_start(ar[e][:, :, 0, :], rh[0, :, :, cols]).then_inc(i_in[e], 16)
                sp.dma_start(ar[e][:, :, 1, :], rh[1, :, :, cols]).then_inc(i_in[e], 16)
                sp.wait_ge(b_free, 1)
                sp.sem_inc(b_free, -1)
                sp.dma_start(bt[:], rh[2, :, :, cols]).then_inc(i_in[e], 16)
                sp.dma_start(kt[:], rh[3, :, :, cols]).then_inc(i_in[e], 16)
                sp.dma_start(vt[:], rh[4, :, :, cols]).then_inc(i_in[e], 16)

            def store(t, row, e):
                for b in range(NB):
                    if b == NB - 1:
                        sp.wait_ge(s["y_a"], 1)
                        sp.sem_inc(s["y_a"], -1)
                        sp.dma_start(mixT[GW:2 * GW, bass.ds(t * 128, 128)].rearrange("(h c) t -> c h t", c=64), yst[:]).then_inc(s["y_st"], 16)
                    J.sp_store(sp, row, b)

            load(0, 0)
            with sp.Fori(0, NT // 2 - 1) as i:
                for e in two:
                    load(i * 2 + (1 + e), 1 - e)
                    store(i * 2 + e, i * 256 + (R_RG + e * 128), e)
            load(NT - 1, 1)
            for e in two:
                store(NT - 2 + e, DIN - 256 + 128 * e, e)
            sp.wait_ge(s["y_st"], 16)
            for q in two:
                sp.wait_ge(J.stage_st[q], 16)

        @block.gpsimd
        def _(pool):
            tiles(pool, lambda t, row, e: J.pool_weights(pool, e))

        @block.tensor
        def _(pe):
            pe.wait_ge(s["c_in"], 48)
            pe.wait_ge(s["i_ok"], 1)
            M, Tr = nc.tensor.matmul, nc.tensor.transpose

            def body(t, row, e):
                tile = J.pe_tile(pe, e)

                def fill(stage):
                    for _ in range(dict(SCAN_FILL)[stage]):
                        next(tile)

                a_, b_, k_, v_ = ar[e], bt, kt, vt
                pe.wait_ge(i_in[e], 80)
                pe.sem_inc(i_in[e], -80)
                for h in range(NH):
                    N_ = M(bank(0)[:, h, :], a_[:, h, 0, :], b_[:, h, :], start=True, stop=True)
                N_.then_inc(s["n_rdy"], 1)
                for h in range(NH):
                    N_ = M(two12[:, h], b_[:, h, :], a_[:, h], start=True, stop=True)
                N_.then_inc(s["mb"], 1)
                pe.wait_ge(s["y_ev"], 1)
                pe.sem_inc(s["y_ev"], -1)
                for h in range(NH):
                    Tr(bk[:, 3, h * 64:(h + 1) * 64], a_[:, h, 0, :], ident[0:64, 0:64])
                    Tr(bk[:, 3, 256 + h * 64:256 + (h + 1) * 64], b_[:, h, :], ident[0:64, 0:64])
                for h in range(NH):
                    Tr(bk[:, 4, h * 64:(h + 1) * 64], k_[:, h, :], ident[0:64, 0:64])
                    N_ = Tr(bk[:, 4, 256 + h * 64:256 + (h + 1) * 64], v_[:, h, :], ident[0:64, 0:64])
                N_.then_inc(s["tok"], 1)
                fill("tok")
                pe.wait_ge(s["d_rdy"], 1)
                pe.sem_inc(s["d_rdy"], -1)
                for h in range(NH):
                    N_ = M(bank(0)[:, h, :], Dt[:, h, :], D[:, h, :], start=True, stop=True)
                N_.then_inc(s["p2_m"], 1)
                pe.wait_ge(s["tok_ev"], 1)
                pe.sem_inc(s["tok_ev"], -1)
                for h in range(NH):
                    N_ = M(bank(3)[:, h, :], D[:, h, :], Dt[:, h, :], start=True, stop=True)
                N_.then_inc(s["p2t_m"], 1)
                pe.wait_ge(s["s2_d"], 1)
                pe.sem_inc(s["s2_d"], -1)
                for h in range(NH):
                    N_ = M(two45[:, h], k_[:, h, :], a_[:, h], start=True, stop=True)
                N_.then_inc(s["mk"], 1)
                fill("mk")
                pe.wait_ge(s["p2_a"], 1)
                pe.sem_inc(s["p2_a"], -1)
                pe.wait_ge(s["p2_d"], 1)
                pe.sem_inc(s["p2_d"], -1)
                for h in range(NH):
                    N_ = M(bank(0)[:, h, :], px[:, h, 0, :], p2[:, h, :], start=True, stop=True)
                N_.then_inc(s["s3a"], 1)
                for h in range(NH):
                    N_ = M(two12[:, h], p2[:, h, :], px[:, h], start=True, stop=True)
                N_.then_inc(s["s3d"], 1)
                fill("s3")
                pe.wait_ge(s["p4_a"], 1)
                pe.sem_inc(s["p4_a"], -1)
                pe.wait_ge(s["p4t_d"], 1)
                pe.sem_inc(s["p4t_d"], -1)
                for h in range(NH):
                    N_ = M(bank(3)[:, h, :], p4t[:, h, :], p4[:, h, :], start=True, stop=True)
                N_.then_inc(s["s4a"], 1)
                pe.wait_ge(s["x2_d"], 1)
                pe.sem_inc(s["x2_d"], -1)
                for h in range(NH):
                    N_ = M(bank(0)[:, h, :], p4[:, h, :], x1[:, h, :], start=True, stop=True)
                N_.then_inc(s["s4d"], 1)
                fill("s4")
                pe.wait_ge(s["ak_rdy"], 1)
                pe.sem_inc(s["ak_rdy"], -1)
                for h in range(NH):
                    N_ = M(bank(4, 64)[:, h, :], ak[:, h, 0, :], vm[:, h, :], start=True, stop=True)
                N_.then_inc(s["q_m"], 1)
                pe.wait_ge(s["p8_a"], 1)
                pe.sem_inc(s["p8_a"], -1)
                pe.wait_ge(s["x3_d"], 1)
                pe.sem_inc(s["x3_d"], -1)
                for h in range(NH):
                    N_ = M(bank(1)[:, h, :], p8[:, h, :], x1[:, h, :], start=True, stop=True)
                N_.then_inc(s["s5"], 1)
                fill("s5")
                for xr, sa, sd, xa, yd, E, sx, f1, f2 in (("x4", "s6a", "s6d", "x4_a", "y_d", E1, "s7", "s6", "s7"), ("x5", "s8a", "s8d", "x5_a", "y2_d", E2, "s9", "s8", "s9")):
                    pe.wait_ge(s[xr], 1)
                    pe.sem_inc(s[xr], -1)
                    for h in range(NH):
                        N_ = Tr(bank(2)[:, h, :], x1[:, h, :], ident[:])
                    N_.then_inc(s[sa], 1)
                    for h in range(NH):
                        N_ = M(bank(3)[:, h, :], E[:, h, :], x1[:, h, :], start=True, stop=True)
                    N_.then_inc(s[sd], 1)
                    fill(f1)
                    pe.wait_ge(s[xa], 1)
                    pe.sem_inc(s[xa], -1)
                    pe.wait_ge(s[yd], 1)
                    pe.sem_inc(s[yd], -1)
                    for h in range(NH):
                        N_ = M(bank(1)[:, h, :], xn[:, h, :], yy[:, h, :], start=True, stop=True)
                    N_.then_inc(s[sx], 1)
                    fill(f2)
                pe.wait_ge(s["x6"], 1)
                pe.sem_inc(s["x6"], -1)
                pe.wait_ge(s["q_a"], 1)
                pe.sem_inc(s["q_a"], -1)
                for h in range(NH):
                    N_ = M(bank(2)[:, h, :], x1[:, h, :], aq[:, h, :], start=True, stop=True)
                N_.then_inc(s["wz_m"], 1)
                fill("wz")
                pe.wait_ge(s["wz_d"], 1)
                pe.sem_inc(s["wz_d"], -1)
                for h in range(NH):
                    M(bk[0:64, 0, h * 128:(h + 1) * 128].rearrange("p (u t) -> p u t", u=2), wz[:, h, 0:64], bm[:, :, h, :], start=True, stop=True)
                for h in range(NH):
                    N_ = M(bk[0:64, 1, h * 128:(h + 1) * 128], wz[:, h, 0:64], arb[:, h, :], start=True, stop=True)
                N_.then_inc(s["g_m"], 1)
                fill("g")
                pe.wait_ge(s["g_d"], 1)
                pe.sem_inc(s["g_d"], -1)
                for h in range(NH):
                    o = bk[0:64, 5, h * 64:(h + 1) * 64]
                    M(o, bm[:, 0, h, :], wz[:, h, 64:128], start=True, stop=False)
                    M(o, km[:, 0, h, :], vm[:, h, :], start=False, stop=False)
                    N_ = M(o, gt[:, h, 0, :], S[:, 0, h, :], start=False, stop=True)
                N_.then_inc(s["s_m"], 1)
                fill("c0")
                pe.wait_ge(s["s_d"], 1)
                pe.sem_inc(s["s_d"], -1)
                for h in range(NH):
                    o = bk[0:64, 4, h * 128:(h + 1) * 128]
                    M(o, wz[:, h, 64:128], arb[:, h, :], start=True, stop=False)
                    M(o, vm[:, h, :], ak[:, h, 1, :], start=False, stop=False)
                    M(o[:, 0:64], S[:, 0, h, :], m1[:, h, 0:64], start=False, stop=False)
                    N_ = M(o[:, 64:128], S[:, 1, h, :], m1[:, h, 64:128], start=False, stop=True)
                N_.then_inc(s["y_m"], 1)
                for h in range(NH):
                    o = bk[0:64, 5, h * 64:(h + 1) * 64]
                    M(o, bm[:, 1, h, :], wz[:, h, 64:128], start=True, stop=False)
                    M(o, km[:, 1, h, :], vm[:, h, :], start=False, stop=False)
                    N_ = M(o, gt[:, h, 1, :], S[:, 1, h, :], start=False, stop=True)
                N_.then_inc(s["s2_m"], 1)
                fill("c1")
            tiles(pe, body)

        def mask(i):
            return mk[:, i:i + 1, :].to_broadcast([128, NH, 128])

        @block.vector
        def _(v):
            v.wait_ge(s["c_in"], 48)
            V = nc.vector
            V.memset(S[:], 0.0)
            V.memset(bm[:], 0.0)
            V.memset(km[:], 0.0)
            v.drain().then_inc(s["s2_d"], 1)
            for e in two:
                v.sem_inc(in_free[e], 1)
            v.sem_inc(b_free, 1)
            v.drain().then_inc(s["i_ok"], 2)

            def body(t, row, e):
                v.wait_ge(s["n_rdy"], 1)
                v.sem_inc(s["n_rdy"], -1)
                V.tensor_tensor(D[:], bank(0), mask(0), ALU.mult)
                v.wait_ge(s["mb"], 1)
                v.sem_inc(s["mb"], -1)
                V.tensor_tensor(Dt[:], two12[:, :, 0, :], mask(3), ALU.mult)
                V.tensor_tensor(E1[:], bank(0), mask(1), ALU.mult)
                V.tensor_tensor(E2[:], bank(0), mask(2), ALU.mult).then_inc(s["d_rdy"], 1)
                v.drain()
                V.tensor_tensor(px[:, :, 1, :], Dt[:], ident[:].rearrange("p (o t) -> p o t", o=1).to_broadcast([128, NH, 128]), ALU.add)
                V.tensor_tensor(arb[:], two12[:, :, 1, :], mask(5), ALU.mult)
                v.wait_ge(s["p2t_m"], 1)
                v.sem_inc(s["p2t_m"], -1)
                V.tensor_copy(px[:, :, 0, :], bank(3)).then_inc(s["p2_d"], 1)
                v.wait_ge(s["mk"], 1)
                v.sem_inc(s["mk"], -1)
                V.tensor_tensor(ak[:, :, 0, :], two45[:, :, 0, :], mask(4), ALU.mult).then_inc(b_free, 1)
                v.wait_ge(s["s3d"], 1)
                v.sem_inc(s["s3d"], -1)
                V.tensor_copy(p4t[:], two12[:, :, 0, :]).then_inc(s["p4t_d"], 1)
                V.tensor_tensor(x1[:], two12[:, :, 1, :], px[:, :, 1, :], ALU.add).then_inc(s["x2_d"], 1)
                V.tensor_tensor(ak[:, :, 1, :], two45[:, :, 1, :], mask(5), ALU.mult).then_inc(s["ak_rdy"], 1)
                v.drain()
                for m, b_, r in (("s4d", 0, "x3_d"), ("s5", 1, "x4")):
                    v.wait_ge(s[m], 1)
                    v.sem_inc(s[m], -1)
                    V.tensor_tensor(x1[:], bank(b_), x1[:], ALU.add)
                    v.drain().then_inc(s[r], 1)
                for sd, yd, sx, r in (("s6d", "y_d", "s7", "x5"), ("s8d", "y2_d", "s9", "x6")):
                    v.wait_ge(s[sd], 1)
                    v.sem_inc(s[sd], -1)
                    V.tensor_copy(yy[:], bank(3)).then_inc(s[yd], 1)
                    v.wait_ge(s[sx], 1)
                    v.sem_inc(s[sx], -1)
                    V.tensor_tensor(x1[:], bank(1), x1[:], ALU.add)
                    v.drain().then_inc(s[r], 1)
                v.wait_ge(s["wz_m"], 1)
                v.sem_inc(s["wz_m"], -1)
                V.tensor_copy(wz[:], bank(2)).then_inc(s["wz_d"], 1)
                v.wait_ge(s["g_m"], 1)
                v.sem_inc(s["g_m"], -1)
                V.tensor_tensor(gt.rearrange("p h u t -> p (h u) t"), bk[0:64, 0, :].rearrange("p (h t) -> p h t", t=64),
                                ident[0:64, 0:64].rearrange("p (o t) -> p o t", o=1).to_broadcast([64, 2 * NH, 64]), ALU.add)
                V.tensor_tensor(m1, bk[0:64, 1, :].rearrange("p (h t) -> p h t", h=NH), ar[e][:, :, 1, :], ALU.add).then_inc(s["g_d"], 1)
                v.drain().then_inc(in_free[e], 1)
                for c, m in ((0, "s_m"), (1, "s2_m")):
                    v.wait_ge(s[m], 1)
                    v.sem_inc(s[m], -1)
                    V.tensor_tensor(S[:, 1 - c], bk[0:64, 5, 0:NH * 64].rearrange("p (h t) -> p h t", h=NH),
                                    pe_all[:, :, bass.ds(t * 2 + c, 1)].to_broadcast([64, NH, 64]), ALU.mult)
                    v.drain().then_inc(s["s_d" if c == 0 else "s2_d"], 1)
            tiles(v, body)

        @block.scalar
        def _(act):
            J.act_start(act)
            act.wait_ge(s["i_ok"], 2)
            act.sem_inc(s["y_st"], 16)
            act.sem_inc(s["y_ev"], 1)
            C = nc.scalar.copy

            def evac(stage):
                for b in units_done(SCAN_FILL, stage):
                    J.evacuate(act, C, b)

            def body(t, nxt, e):
                if nxt is not None:
                    J.act_load(act, nxt)
                act.wait_ge(s["tok"], 1)
                act.sem_inc(s["tok"], -1)
                b3 = bk[:, 3, :].rearrange("p (u h c) -> p u h c", u=2, h=NH)
                b4 = bk[:, 4, :].rearrange("p (u h c) -> p u h c", u=2, h=NH)
                C(aq[:, :, 0:64], b3[:, 0])
                for c in two:
                    C(bm[64 * c:64 * c + 64, c], b3[64 * c:64 * c + 64, 1])
                    C(km[64 * c:64 * c + 64, c], b4[64 * c:64 * c + 64, 0])
                C(vm[:], b4[:, 1])
                act.drain().then_inc(s["tok_ev"], 1)
                evac("tok")
                act.wait_ge(s["p2_m"], 1)
                act.sem_inc(s["p2_m"], -1)
                C(p2[:], bank(0)).then_inc(s["p2_a"], 1)
                evac("mk")
                act.wait_ge(s["s3a"], 1)
                act.sem_inc(s["s3a"], -1)
                C(p4[:], bank(0)).then_inc(s["p4_a"], 1)
                evac("s3")
                act.wait_ge(s["s4a"], 1)
                act.sem_inc(s["s4a"], -1)
                C(p8[:], bank(3)).then_inc(s["p8_a"], 1)
                evac("s4")
                act.wait_ge(s["q_m"], 1)
                act.sem_inc(s["q_m"], -1)
                C(aq[:, :, 64:128], bank(4, 64)).then_inc(s["q_a"], 1)
                evac("s5")
                if nxt is not None:
                    J.act_split(act, 1 - e)
                for sa, xa, f1, f2 in (("s6a", "x4_a", "s6", "s7"), ("s8a", "x5_a", "s8", "s9")):
                    act.wait_ge(s[sa], 1)
                    act.sem_inc(s[sa], -1)
                    C(xn[:], bank(2)).then_inc(s[xa], 1)
                    evac(f1)
                    evac(f2)
                evac("wz")
                evac("g")
                evac("c0")
                act.wait_ge(s["y_m"], 1)
                act.sem_inc(s["y_m"], -1)
                act.wait_ge(s["y_st"], 16)
                act.sem_inc(s["y_st"], -16)
                C(yst[:], bk[0:64, 4, :].rearrange("p (h t) -> p h t", h=NH)).then_inc(s["y_a"], 1)
                act.drain().then_inc(s["y_ev"], 1)
                evac("c1")

            J.act_load(act, R_RG)
            J.act_split(act, 0)
            with act.Fori(0, NT // 2 - 1) as i:
                for e in two:
                    body(i * 2 + e, i * 256 + (R_RG + (1 + e) * 128), e)
            body(NT - 2, DIN - 128, 0)
            body(NT - 1, None, 1)


def phase_head_norm(nc, l, projT, par, consts, rope, fa):
    with ExitStack() as ctx:
        P = Phase(nc, ctx, "hn")
        pars, gsc = P.sb("pars", [128, NPAR]), P.sb("gsc", [128, 7])
        bones, perm = P.sb("bones", [128, 128]), P.sb("perm", [128, 128])
        cs = P.sb("cs", [128, 2, T])
        NX = 3
        x = [P.sb(f"x{q}", [128, T]) for q in range(NX)]
        sq, rs, sw = (P.sb(n, [128, T]) for n in ("sq", "rs", "sw"))
        f, g, one, F4 = P.sb("f", [4, T]), P.sb("g", [4, T]), P.sb("one", [4, T]), P.sb("F4", [4, 4, T])
        ss, pr = P.ps("ss", [128, T]), P.ps("pr", [128, T])
        names = ("c_in", "rope_in", "f_in", "z_rdy", "e_rdy", "F_rdy", "F_st", "sq_rdy", "ss_rdy", "ss_free", "v_rdy", "r_rdy", "y_rdy", "sw_rdy", "o_rdy")
        s = {n: P.sem(n) for n in names}
        x_in, st = ([P.sem(f"{n}{q}") for q in range(NX)] for n in ("x_in", "st"))
        block = ctx.enter_context(nc.Block())
        tiles = [(r * 128, False) for r in range(4)] + [(R_SQ + r * 128, True) for r in range(3)]
        last = len(tiles) - 1

        @block.sync
        def _(sp):
            sp.dma_start(pars[:], lay(par, l)).then_inc(s["c_in"], 16)
            sp.dma_start(bones[:], consts[:, 256:384]).then_inc(s["c_in"], 16)
            sp.dma_start(perm[:], consts[:, 896:1024]).then_inc(s["c_in"], 16)
            sp.dma_start(f[:], projT[R_FF:R_FF + 4, PAD:PAD + T]).then_inc(s["f_in"], 16)

            def load(j):
                sp.wait_ge(st[j % NX], 16)
                sp.sem_inc(st[j % NX], -16)
                sp.dma_start(x[j % NX][:], projT[tiles[j][0]:tiles[j][0] + 128, PAD:PAD + T]).then_inc(x_in[j % NX], 16)

            load(0)
            load(1)
            sp.dma_start(cs[:], rope.rearrange("p (k t) -> p k t", k=2)).then_inc(s["rope_in"], 16)
            for j, (row, rot) in enumerate(tiles):
                if j + 2 <= last:
                    load(j + 2)
                sp.wait_ge(s["o_rdy"], 1)
                sp.sem_inc(s["o_rdy"], -1)
                sp.dma_start(projT[row:row + 128, PAD:PAD + T], x[j % NX][:]).then_inc(st[j % NX], 16)
                if j == 2:
                    sp.wait_ge(s["F_rdy"], 1)
                    sp.sem_inc(s["F_rdy"], -1)
                    sp.dma_start(fa.rearrange("(h k) t -> h k t", k=4), F4[:]).then_inc(s["F_st"], 16)
            for q in range(NX):
                sp.wait_ge(st[q], 16)
            sp.wait_ge(s["F_st"], 16)

        @block.scalar
        def _(act):
            A = nc.scalar.activation
            for q in range(NX):
                act.sem_inc(st[q], 16)

            def square(j):
                act.wait_ge(x_in[j % NX], 16)
                act.sem_inc(x_in[j % NX], -16)
                A(sq[:], x[j % NX][:], ACT.Square).then_inc(s["sq_rdy"], 1)

            square(0)
            act.wait_ge(s["z_rdy"], 1)
            act.sem_inc(s["z_rdy"], -1)
            A(g[:], g[:], ACT.Exp, scale=-1.0)
            act.drain()
            A(g[:], g[:], ACT.Ln, bias=1.0).then_inc(s["e_rdy"], 1)
            for j in range(len(tiles)):
                act.wait_ge(s["v_rdy"], 1)
                act.sem_inc(s["v_rdy"], -1)
                if j < last:
                    square(j + 1)
                A(rs[:], rs[:], ACT.Ln)
                act.drain()
                A(rs[:], rs[:], ACT.Exp, scale=-0.5).then_inc(s["r_rdy"], 1)

        @block.tensor
        def _(pe):
            def rotate(pe, j):
                pe.wait_ge(s["y_rdy"], 1)
                pe.sem_inc(s["y_rdy"], -1)
                for c in range(NB):
                    ins = nc.tensor.matmul(pr[:, c * TB:(c + 1) * TB], perm[:], x[j % NX][:, c * TB:(c + 1) * TB], start=True, stop=True)
                ins.then_inc(s["sw_rdy"], 1)

            pe.wait_ge(s["c_in"], 48)
            for j, (row, rot) in enumerate(tiles):
                pe.wait_ge(s["sq_rdy"], 1)
                pe.sem_inc(s["sq_rdy"], -1)
                pe.wait_ge(s["ss_free"], 1)
                pe.sem_inc(s["ss_free"], -1)
                for c in range(NB):
                    ins = nc.tensor.matmul(ss[:, c * TB:(c + 1) * TB], bones[:], sq[:, c * TB:(c + 1) * TB], start=True, stop=True)
                ins.then_inc(s["ss_rdy"], 1)
                if j > 0 and tiles[j - 1][1]:
                    rotate(pe, j - 1)
            rotate(pe, last)

        @block.vector
        def _(v):
            V = nc.vector
            v.wait_ge(s["c_in"], 48)
            v.sem_inc(s["ss_free"], 1)
            V.tensor_copy(gsc[:], pars[:, C_GN:C_GN + 7])
            v.drain()
            for c in (0, 4):
                V.tensor_scalar(gsc[:, c:c + 2], gsc[:, c:c + 2], HD ** -0.5, None, ALU.mult)
            v.wait_ge(s["f_in"], 16)
            v.sem_inc(s["f_in"], -16)
            V.tensor_scalar(f[:], f[:], pars[0:4, C_BF:C_BF + 1], None, ALU.add)
            v.drain()
            V.scalar_tensor_tensor(g[:], f[:], -1.0, f[:], ALU.mult, ALU.max).then_inc(s["z_rdy"], 1)

            def forget_gate():
                V.memset(one[:], 1.0)
                V.memset(F4[:, 1:3, :], 1.0)
                v.wait_ge(s["e_rdy"], 1)
                v.sem_inc(s["e_rdy"], -1)
                V.scalar_tensor_tensor(f[:], f[:], 0.0, g[:], ALU.min, ALU.subtract)
                v.drain()
                V.tensor_tensor_scan(F4[:, 0, :], one[:], f[:], 0.0, ALU.mult, ALU.add)
                v.drain()
                V.tensor_scalar(F4[:, 3, :], F4[:, 0, :], -1.0, None, ALU.mult).then_inc(s["F_rdy"], 1)

            def variance():
                v.wait_ge(s["ss_rdy"], 1)
                v.sem_inc(s["ss_rdy"], -1)
                V.tensor_scalar(rs[:], ss[:], 1.0 / HD, EPS, ALU.mult, ALU.add).then_inc(s["v_rdy"], 1)
                v.drain().then_inc(s["ss_free"], 1)

            variance()
            for j, (row, rot) in enumerate(tiles):
                y = x[j % NX]
                v.wait_ge(s["r_rdy"], 1)
                v.sem_inc(s["r_rdy"], -1)
                ins = V.scalar_tensor_tensor(y[:], y[:], gsc[:, j:j + 1], rs[:], ALU.mult, ALU.mult)
                if rot:
                    ins.then_inc(s["y_rdy"], 1)
                    if j == 4:
                        v.wait_ge(s["rope_in"], 16)
                        v.sem_inc(s["rope_in"], -16)
                else:
                    ins.then_inc(s["o_rdy"], 1)
                v.drain()
                if j < last:
                    variance()
                if j == 0:
                    forget_gate()
                if rot:
                    v.wait_ge(s["sw_rdy"], 1)
                    v.sem_inc(s["sw_rdy"], -1)
                    V.tensor_tensor(sw[:], pr[:], cs[:, 1, :], ALU.mult)
                    V.tensor_tensor(y[:], y[:], cs[:, 0, :], ALU.mult)
                    v.drain()
                    V.tensor_tensor(y[:], y[:], sw[:], ALU.add).then_inc(s["o_rdy"], 1)


def phase_fox(nc, l, projT, fa, consts, mixT):
    with ExitStack() as ctx:
        P = Phase(nc, ctx, "fx")
        ident, cm = P.sb("ident", [128, 128]), P.sb("cm", [128, 128])
        identb, cmb = P.sb("identb", [128, 128], BF16), P.sb("cmb", [128, 128], BF16)
        two = range(2)
        q2, k2 = ([P.sb(f"{n}{e}", [66, T]) for e in two] for n in ("qs", "ks"))
        v2 = [P.sb(f"vc{e}", [64, T]) for e in two]
        vs = P.sb("vs", [128, NT, HD])
        UK = 8
        prob = [P.sb(f"prob{q}", [128, UK * 128]) for q in range(3)]
        pts = [P.sb(f"pts{q}", [128, UK, 128]) for q in range(2)]
        nm, ls, sc, nr, lr = (P.sb(n, [128, 4, 2]) for n in ("nm", "ls", "sc", "nr", "lr"))
        on = P.sb("on", [128, 2, HD])
        yo = P.sb("yo", [64, T])
        S = P.ps("S", [128, 2, UK * 128])
        pt = [P.ps(f"pt{q}", [128, 4, 128]) for q in range(2)]
        O, OT = P.ps("O", [128, 512]), P.ps("OT", [64, 512])
        names = ("c_in", "cb_rdy", "v_tr", "v_ev", "s_rdy", "m_rdy", "d_rdy", "sc_rdy", "o_rdy", "o_free", "on_rdy", "ot_rdy", "yo_rdy", "yo_st", "ot_free")
        s = {n: P.sem(n) for n in names}
        pt_rdy = [P.sem(f"pt_rdy{q}") for q in range(2)]
        pt_ev = [P.sem(f"pt_ev{q}") for q in range(2)]
        h_in, in_free = ([P.sem(f"{n}{e}") for e in two] for n in ("h_in", "in_free"))
        p_rdy, ls_rdy = P.sem("p_rdy"), P.sem("ls_rdy")
        block = ctx.enter_context(nc.Block())

        units = []
        for t in range(NT):
            parts = [(0, t + 1)] if t < UK else [(0, UK), (UK, t + 1)]
            units += [(t, p, a, b, p == len(parts) - 1) for p, (a, b) in enumerate(parts)]
        NU = len(units)
        assert NU % 6 == 0

        def groups(u):
            t, p, a, b, last = units[u]
            return [(g, a + 4 * g, min(a + 4 * g + 4, b)) for g in range((b - a + 3) // 4)]

        @block.sync
        def _(sp):
            sp.dma_start(ident[:], consts[:, 0:128]).then_inc(s["c_in"], 16)
            sp.dma_start(cm[:], consts[:, 1024:1152]).then_inc(s["c_in"], 16)

            def load(h, e):
                sp.wait_ge(in_free[e], 1)
                sp.sem_inc(in_free[e], -1)
                tok = slice(PAD, PAD + T)
                sp.dma_start(v2[e][:], projT[bass.ds(h * HD + R_FV, HD), tok]).then_inc(h_in[e], 16)
                sp.dma_start(q2[e][0:64, :], projT[bass.ds(h * HD, HD), tok]).then_inc(h_in[e], 16)
                sp.dma_start(k2[e][0:64, :], projT[bass.ds(h * HD + R_FK, HD), tok]).then_inc(h_in[e], 16)
                sp.dma_start(q2[e][64:66, :], fa[bass.ds(h * 4, 2), :]).then_inc(h_in[e], 16)
                sp.dma_start(k2[e][64:66, :], fa[bass.ds(h * 4 + 2, 2), :]).then_inc(h_in[e], 16)

            def store(h):
                sp.wait_ge(s["yo_rdy"], 1)
                sp.sem_inc(s["yo_rdy"], -1)
                sp.dma_start(mixT[bass.ds(h * HD, HD), :], yo[:]).then_inc(s["yo_st"], 16)

            load(0, 0)
            with sp.Fori(0, NH // 2 - 1) as i:
                for e in two:
                    load(i * 2 + (1 + e), 1 - e)
                    store(i * 2 + e)
            load(NH - 1, 1)
            store(NH - 2)
            store(NH - 1)
            sp.wait_ge(s["yo_st"], 16)

        @block.tensor
        def _(pe):
            M, Tr = nc.tensor.matmul, nc.tensor.transpose
            pe.wait_ge(s["c_in"], 32)
            pe.wait_ge(s["cb_rdy"], 1)

            def qk(u, qs, ks):
                t, p, a, b, last = units[u]
                n = (b - a) * 128
                for c in range(0, n, 512):
                    w = min(512, n - c)
                    ins = M(S[:, u % 2, c:c + w], qs[:, t * 128:(t + 1) * 128], ks[:, a * 128 + c:a * 128 + c + w], start=True, stop=(c + w < n or not last))
                if last:
                    ins = M(S[:, u % 2, n - 128:n], identb[:], cmb[:], start=False, stop=True)
                ins.then_inc(s["s_rdy"], 1)

            def transpose_p(u):
                for g, j0, j1 in groups(u):
                    a = units[u][2]
                    for j in range(j0, j1):
                        ins = Tr(pt[g][:, j - j0, :], prob[u % 3][:, (j - a) * 128:(j - a + 1) * 128], ident[:])
                    ins.then_inc(pt_rdy[g], 1)

            def pv(u):
                t, p, a, b, last = units[u]
                if p == 0:
                    pe.wait_ge(s["o_free"], 1)
                    pe.sem_inc(s["o_free"], -1)
                for g, j0, j1 in groups(u):
                    for j in range(j0, j1):
                        ins = M(O[:, p * HD:(p + 1) * HD], pts[u % 2][:, j - a, :], vs[:, j, :], start=(j == a), stop=(j == b - 1))
                if last:
                    ins.then_inc(s["o_rdy"], 1)

            def out_t(t):
                pe.wait_ge(s["on_rdy"], 1)
                pe.sem_inc(s["on_rdy"], -1)
                pe.wait_ge(s["ot_free"], 1)
                pe.sem_inc(s["ot_free"], -1)
                Tr(OT[:, 0:128], on[:, t % 2, :], ident[:]).then_inc(s["ot_rdy"], 1)

            def head(qs, ks, vc, h_in):
                pe.wait_ge(h_in, 80)
                pe.sem_inc(h_in, -80)
                for j in range(NT):
                    ins = Tr(S[:, 0, j * HD:(j + 1) * HD], vc[:, j * 128:(j + 1) * 128], ident[0:64, 0:64])
                ins.then_inc(s["v_tr"], 1)
                pe.wait_ge(s["v_ev"], 1)
                pe.sem_inc(s["v_ev"], -1)
                qk(0, qs, ks)
                qk(1, qs, ks)
                for u in range(NU):
                    pe.wait_ge(p_rdy, 1)
                    pe.sem_inc(p_rdy, -1)
                    if u + 2 < NU:
                        qk(u + 2, qs, ks)
                    if u > 1 and units[u - 2][4]:
                        out_t(units[u - 2][0])
                    if u > 0:
                        for g, j0, j1 in groups(u - 1):
                            pe.wait_ge(pt_ev[g], 1)
                            pe.sem_inc(pt_ev[g], -1)
                    transpose_p(u)
                    if u > 0:
                        pv(u - 1)
                if units[NU - 2][4]:
                    out_t(units[NU - 2][0])
                for g, j0, j1 in groups(NU - 1):
                    pe.wait_ge(pt_ev[g], 1)
                    pe.sem_inc(pt_ev[g], -1)
                pv(NU - 1)
                out_t(units[NU - 1][0])

            with pe.Fori(0, NH // 2) as i:
                for e in two:
                    head(q2[e], k2[e], v2[e], h_in[e])

        @block.vector
        def _(v):
            V = nc.vector
            v.wait_ge(s["c_in"], 32)
            V.tensor_copy(identb[:], ident[:])
            V.tensor_copy(cmb[:], cm[:])
            v.drain().then_inc(s["cb_rdy"], 1)
            for e in two:
                v.sem_inc(in_free[e], 1)
            v.sem_inc(s["o_free"], 1)

            def row_max(u):
                t, p, a, b, last = units[u]
                v.wait_ge(s["s_rdy"], 1)
                v.sem_inc(s["s_rdy"], -1)
                V.tensor_reduce(nm[:, t % 4, p:p + 1], S[:, u % 2, 0:(b - a) * 128], AX.X, ALU.max, negate=True).then_inc(s["m_rdy"], 1)
                if p == 1:
                    v.drain()
                    V.tensor_tensor(nr[:, t % 4, 0:1], nm[:, t % 4, 0:1], nm[:, t % 4, 1:2], ALU.min)
                    v.drain()
                    V.tensor_scalar(nr[:, t % 4, :], nm[:, t % 4, :], nr[:, t % 4, 0:1], -1.0, ALU.subtract, ALU.mult).then_inc(s["d_rdy"], 1)

            def out_row(t):
                q = t % 4
                v.wait_ge(ls_rdy, 1)
                v.sem_inc(ls_rdy, -1)
                v.wait_ge(s["o_rdy"], 1)
                v.sem_inc(s["o_rdy"], -1)
                if t < UK:
                    V.reciprocal(lr[:, q, 0:1], ls[:, q, 0:1])
                    v.drain()
                    V.tensor_scalar(on[:, t % 2, :], O[:, 0:HD], lr[:, q, 0:1], None, ALU.mult).then_inc(s["on_rdy"], 1)
                else:
                    v.wait_ge(s["sc_rdy"], 1)
                    v.sem_inc(s["sc_rdy"], -1)
                    V.tensor_tensor(lr[:, q, :], ls[:, q, :], sc[:, q, :], ALU.mult)
                    v.drain()
                    V.tensor_tensor(lr[:, q, 0:1], lr[:, q, 0:1], lr[:, q, 1:2], ALU.add)
                    v.drain()
                    V.reciprocal(lr[:, q, 0:1], lr[:, q, 0:1])
                    v.drain()
                    V.tensor_scalar(sc[:, q, :], sc[:, q, :], lr[:, q, 0:1], None, ALU.mult)
                    v.drain()
                    V.tensor_scalar(on[:, t % 2, :], O[:, 0:HD], sc[:, q, 0:1], None, ALU.mult)
                    v.drain()
                    V.scalar_tensor_tensor(on[:, t % 2, :], O[:, HD:2 * HD], sc[:, q, 1:2], on[:, t % 2, :], ALU.mult, ALU.add).then_inc(s["on_rdy"], 1)
                v.drain().then_inc(s["o_free"], 1)

            def head(e):
                v.wait_ge(s["v_tr"], 1)
                v.sem_inc(s["v_tr"], -1)
                V.tensor_copy(vs[:], S[:, 0, 0:NT * HD].rearrange("p (j c) -> p j c", j=NT)).then_inc(s["v_ev"], 1)
                row_max(0)
                for u in range(NU):
                    if u + 1 < NU:
                        row_max(u + 1)
                    g, j0, j1 = groups(u)[0]
                    v.wait_ge(pt_rdy[g], 1)
                    v.sem_inc(pt_rdy[g], -1)
                    V.tensor_copy(pts[u % 2][:, 0:j1 - j0, :], pt[g][:, 0:j1 - j0, :]).then_inc(pt_ev[g], 1)
                    if u > 0 and units[u - 1][4]:
                        out_row(units[u - 1][0])
                out_row(NT - 1)
                v.drain().then_inc(in_free[e], 1)

            with v.Fori(0, NH // 2) as i:
                for e in two:
                    head(e)

        @block.scalar
        def _(act):
            A = nc.scalar.activation
            act.sem_inc(s["yo_st"], 16)
            act.sem_inc(s["ot_free"], 1)

            def exps(u):
                t, p, a, b, last = units[u]
                act.wait_ge(s["m_rdy"], 1)
                act.sem_inc(s["m_rdy"], -1)
                n = (b - a) * 128
                A(prob[u % 3][:, 0:n], S[:, u % 2, 0:n], ACT.Exp, bias=nm[:, t % 4, p:p + 1], accum_out=ls[:, t % 4, p:p + 1])
                act.drain().then_inc(p_rdy, 1)
                if last:
                    if p == 1:
                        act.wait_ge(s["d_rdy"], 1)
                        act.sem_inc(s["d_rdy"], -1)
                        A(sc[:, t % 4, :], nr[:, t % 4, :], ACT.Exp).then_inc(s["sc_rdy"], 1)
                    act.drain().then_inc(ls_rdy, 1)

            def out_ev(t):
                act.wait_ge(s["ot_rdy"], 1)
                act.sem_inc(s["ot_rdy"], -1)
                nc.scalar.copy(yo[:, t * 128:(t + 1) * 128], OT[:, 0:128]).then_inc(s["ot_free"], 1)

            with act.Fori(0, NH) as h:
                exps(0)
                act.wait_ge(s["yo_st"], 16)
                act.sem_inc(s["yo_st"], -16)
                for u in range(NU):
                    if u + 1 < NU:
                        exps(u + 1)
                    for g, j0, j1 in groups(u)[1:]:
                        act.wait_ge(pt_rdy[g], 1)
                        act.sem_inc(pt_rdy[g], -1)
                        nc.scalar.copy(pts[u % 2][:, 4 * g:4 * g + j1 - j0, :], pt[g][:, 0:j1 - j0, :]).then_inc(pt_ev[g], 1)
                    if u > 1 and units[u - 2][4]:
                        out_ev(units[u - 2][0])
                if units[NU - 2][4]:
                    out_ev(units[NU - 2][0])
                out_ev(NT - 1)
                act.drain().then_inc(s["yo_rdy"], 1)


def phase_swa(nc, l, projT, par, consts, masks, mixT):
    with ExitStack() as ctx:
        P = Phase(nc, ctx, "sw")
        KW = 192
        ident, pars = P.sb("ident", [128, 128]), P.sb("pars", [128, NPAR])
        mks = P.sb("mks", [128, 2, KW])
        cur = P.sb("cur", [128, KW])
        two = range(2)
        q, k, vc = ([P.sb(f"{n}{e}", [64, w, c]) for e in two] for n, w, c in (("q", NH, 128), ("k", 2, KW), ("vc", 2, KW)))
        va, vb = [P.sb(f"va{e}", [128, 2, HD]) for e in two], [P.sb(f"vb{e}", [64, 2, HD]) for e in two]
        sc, pb = ([P.sb(f"{n}{e}", [128, NH, KW]) for e in two] for n in ("sc", "pb"))
        mx, nm, es, ls = ([P.sb(f"{n}{e}", [128, NH]) for e in two] for n in ("mx", "nm", "es", "ls"))
        pa_t, pb_t = P.sb("pa_t", [128, NH, 128]), P.sb("pb_t", [64, NH, 128])
        on, yo = [P.sb(f"on{e}", [128, NH * HD]) for e in two], [P.sb(f"yo{e}", [128, 2, 128]) for e in two]
        S = P.ps("S", [128, 2, 512])
        TA, TB_, O, V_, OT = P.ps("TA", [128, 512]), P.ps("TB", [64, 512]), P.ps("O", [128, 512]), P.ps("V", [128, 512]), P.ps("OT", [128, 512])
        names = ("c_in", "s_rdy", "s_free", "v_tr", "v_ev", "m_rdy", "p_rdy", "t_rdy", "tt_rdy", "ta_d", "tb_a", "o_rdy", "on_rdy", "ot_rdy", "ot_free")
        s = {n: P.sem(n) for n in names}
        s_in, in_free, yo_rdy, yo_st = ([P.sem(f"{n}{e}") for e in two] for n in ("in", "in_free", "yo_rdy", "yo_st"))
        block = ctx.enter_context(nc.Block())

        def loop(eng, first, body):
            first()
            body(0, 0, True, before=False)
            body(1, 1, True)
            with eng.Fori(1, NT // 2 - 1) as i:
                body(i * 2, 0, True)
                body(i * 2 + 1, 1, True)
            body(NT - 2, 0, True)
            body(NT - 1, 1, False)

        @block.sync
        def _(sp):
            sp.dma_start(ident[:], consts[:, 0:128]).then_inc(s["c_in"], 16)
            sp.dma_start(pars[:], lay(par, l)).then_inc(s["c_in"], 16)
            sp.dma_start(mks[:], masks[:, 768:768 + 2 * KW].rearrange("p (k t) -> p k t", k=2)).then_inc(s["c_in"], 16)

            def load(t, e):
                sp.wait_ge(in_free[e], 1)
                sp.sem_inc(in_free[e], -1)
                sp.dma_start(q[e][:], projT[R_SQ:R_SQ + GW, bass.ds(t * 128 + PAD, 128)].rearrange("(h c) t -> c h t", c=64)).then_inc(s_in[e], 16)
                sp.dma_start(k[e][:], projT[R_SK:R_SK + 128, bass.ds(t * 128 + (PAD - CH), KW)].rearrange("(h c) t -> c h t", c=64)).then_inc(s_in[e], 16)
                sp.dma_start(vc[e][:], projT[R_SV:R_SV + 128, bass.ds(t * 128 + (PAD - CH), KW)].rearrange("(h c) t -> c h t", c=64)).then_inc(s_in[e], 16)

            def store(t, e):
                sp.wait_ge(yo_rdy[e], 1)
                sp.sem_inc(yo_rdy[e], -1)
                sp.dma_start(mixT[2 * GW:3 * GW, bass.ds(t * 128, 128)].rearrange("(k p) t -> p k t", p=128), yo[e][:]).then_inc(yo_st[e], 16)

            load(0, 0)
            load(1, 1)
            with sp.Fori(0, NT // 2 - 1) as i:
                for e in two:
                    load(i * 2 + (2 + e), e)
                    store(i * 2 + e, e)
            for e in two:
                store(NT - 2 + e, e)
            for e in two:
                sp.wait_ge(yo_st[e], 16)

        @block.tensor
        def _(pe):
            M, Tr = nc.tensor.matmul, nc.tensor.transpose
            pe.wait_ge(s["c_in"], 48)

            def scores(e, first=False):
                pe.wait_ge(s_in[e], 48)
                pe.sem_inc(s_in[e], -48)
                pe.wait_ge(s["s_free"], 1)
                pe.sem_inc(s["s_free"], -1)
                for h in range(NH):
                    ins = M(S[:, h // 2, (h % 2) * KW:(h % 2 + 1) * KW], q[e][:, h, :], k[e][:, h // 2, :], start=True, stop=True)
                ins.then_inc(s["s_rdy"], 1)
                if not first:
                    pe.wait_ge(s["v_ev"], 1)
                    pe.sem_inc(s["v_ev"], -1)
                for g in two:
                    Tr(V_[:, g * HD:(g + 1) * HD], vc[e][:, g, 0:128], ident[0:64, 0:64])
                for g in two:
                    ins = Tr(V_[0:64, 128 + g * HD:128 + (g + 1) * HD], vc[e][:, g, 128:KW], ident[0:64, 0:64])
                ins.then_inc(s["v_tr"], 1)

            def out_t(e):
                pe.wait_ge(s["on_rdy"], 1)
                pe.sem_inc(s["on_rdy"], -1)
                pe.wait_ge(s["ot_free"], 1)
                pe.sem_inc(s["ot_free"], -1)
                for p in two:
                    ins = Tr(OT[:, p * 128:(p + 1) * 128], on[e][:, p * 128:(p + 1) * 128], ident[:])
                ins.then_inc(s["ot_rdy"], 1)

            def body(t, e, nxt, before=True):
                if nxt:
                    scores(1 - e)
                if before:
                    out_t(1 - e)
                pe.wait_ge(s["p_rdy"], 1)
                pe.sem_inc(s["p_rdy"], -1)
                for h in range(NH):
                    ins = Tr(TA[:, h * 128:(h + 1) * 128], pb[e][:, h, 0:128], ident[:])
                ins.then_inc(s["t_rdy"], 1)
                for h in range(NH):
                    ins = Tr(TB_[:, h * 128:(h + 1) * 128], pb[e][:, h, 128:KW], ident[:])
                ins.then_inc(s["tt_rdy"], 1)
                if not nxt:
                    pe.wait_ge(s["v_ev"], 1)
                    pe.sem_inc(s["v_ev"], -1)
                pe.wait_ge(s["ta_d"], 1)
                pe.sem_inc(s["ta_d"], -1)
                pe.wait_ge(s["tb_a"], 1)
                pe.sem_inc(s["tb_a"], -1)
                for h in range(NH):
                    M(O[:, h * HD:(h + 1) * HD], pa_t[:, h, :], va[e][:, h // 2, :], start=True, stop=False)
                    ins = M(O[:, h * HD:(h + 1) * HD], pb_t[:, h, :], vb[e][:, h // 2, :], start=False, stop=True)
                ins.then_inc(s["o_rdy"], 1)
            loop(pe, lambda: scores(0, True), body)
            out_t(1)

        @block.vector
        def _(v):
            V = nc.vector
            v.wait_ge(s["c_in"], 48)
            V.tensor_copy(cur[:], mks[:, 0, :])
            for e in two:
                v.sem_inc(in_free[e], 1)
            v.sem_inc(s["s_free"], 1)
            v.drain()
            sink = pars[:, C_SINK:C_SINK + NH]

            def maxima(e):
                v.wait_ge(s["s_rdy"], 1)
                v.sem_inc(s["s_rdy"], -1)
                V.tensor_tensor(sc[e][:].rearrange("p (b h) k -> p b h k", b=2), S[:, :, 0:2 * KW].rearrange("p b (h k) -> p b h k", h=2),
                                cur[:].rearrange("p (a b k) -> p a b k", a=1, b=1).to_broadcast([128, 2, 2, KW]), ALU.add)
                v.drain().then_inc(s["s_free"], 1)
                V.tensor_copy(cur[:], mks[:, 1, :])
                V.tensor_reduce(mx[e][:], sc[e][:], AX.X, ALU.max)
                v.drain()
                V.tensor_tensor(mx[e][:], mx[e][:], sink, ALU.max)
                v.drain()
                V.tensor_scalar(nm[e][:], mx[e][:], -1.0, None, ALU.mult)
                V.tensor_tensor(es[e][:], sink, mx[e][:], ALU.subtract)
                v.drain().then_inc(s["m_rdy"], 1)
                v.wait_ge(s["v_tr"], 1)
                v.sem_inc(s["v_tr"], -1)
                V.tensor_copy(va[e][:], V_[:, 0:128].rearrange("p (g c) -> p g c", g=2)).then_inc(in_free[e], 1)
                V.tensor_copy(vb[e][:], V_[0:64, 128:256].rearrange("p (g c) -> p g c", g=2))
                v.drain().then_inc(s["v_ev"], 1)

            def body(t, e, nxt, before=True):
                if nxt:
                    maxima(1 - e)
                v.wait_ge(s["t_rdy"], 1)
                v.sem_inc(s["t_rdy"], -1)
                V.tensor_copy(pa_t[:], TA[:].rearrange("p (h q) -> p h q", h=NH)).then_inc(s["ta_d"], 1)
                V.tensor_tensor(ls[e][:], ls[e][:], es[e][:], ALU.add)
                v.drain()
                V.reciprocal(ls[e][:], ls[e][:])
                v.drain()
                v.wait_ge(s["o_rdy"], 1)
                v.sem_inc(s["o_rdy"], -1)
                V.tensor_tensor(on[e][:].rearrange("p (h c) -> p h c", h=NH), O[:, 0:NH * HD].rearrange("p (h c) -> p h c", h=NH),
                                ls[e][:].rearrange("p (h o) -> p h o", o=1).to_broadcast([128, NH, HD]), ALU.mult).then_inc(s["on_rdy"], 1)
            loop(v, lambda: maxima(0), body)

        @block.scalar
        def _(act):
            A = nc.scalar.activation
            for e in two:
                act.sem_inc(yo_st[e], 16)
            act.sem_inc(s["ot_free"], 1)

            def out_ev(e):
                act.wait_ge(s["ot_rdy"], 1)
                act.sem_inc(s["ot_rdy"], -1)
                act.wait_ge(yo_st[e], 16)
                act.sem_inc(yo_st[e], -16)
                nc.scalar.copy(yo[e][:], OT[:, 0:256].rearrange("p (k q) -> p k q", k=2)).then_inc(yo_rdy[e], 1)
                act.drain().then_inc(s["ot_free"], 1)

            def exps(e):
                act.wait_ge(s["m_rdy"], 1)
                act.sem_inc(s["m_rdy"], -1)
                A(es[e][:], es[e][:], ACT.Exp)
                for h in range(NH):
                    A(pb[e][:, h, :], sc[e][:, h, :], ACT.Exp, bias=nm[e][:, h:h + 1], accum_out=ls[e][:, h:h + 1])
                act.drain().then_inc(s["p_rdy"], 1)

            def body(t, e, nxt, before=True):
                if before:
                    out_ev(1 - e)
                if nxt:
                    exps(1 - e)
                act.wait_ge(s["tt_rdy"], 1)
                act.sem_inc(s["tt_rdy"], -1)
                nc.scalar.copy(pb_t[:], TB_[:].rearrange("p (h q) -> p h q", h=NH)).then_inc(s["tb_a"], 1)
            loop(act, lambda: exps(0), body)
            out_ev(1)


def phase_out(nc, l, projT, rw, w_out, par, consts, mixT, xT):
    with ExitStack() as ctx:
        P = Phase(nc, ctx, "ou")
        two = range(2)
        pars, bones = P.sb("pars", [128, NPAR]), P.sb("bones", [128, 128])
        wo_hi, wo_lo = P.sb("wo_hi", [128, KC, DM], F32R), P.sb("wo_lo", [128, KC, DM], F32R)
        raw = [P.sb(f"raw{q}", [128, TB]) for q in two]
        y = [P.sb(f"y{q}", [128, KC, TB]) for q in two]
        g = P.sb("g", [128, KC, TB])
        cv = [P.sb(f"cv{q}", [128, 3, 2, TB + 2]) for q in two]
        bv = [P.sb(f"bv{q}", [128, 2, TB]) for q in two]
        th, sq = P.sb("th", [128, KC, TB]), P.sb("sq", [128, 2, TB])
        m_hi, m_lo = P.sb("m_hi", [128, KC, TB], F32R), P.sb("m_lo", [128, KC, TB], F32R)
        stage = [P.sb(f"stage{q}", [128, TB]) for q in two]
        pm, pv = P.ps("pm", [128, 2, TB]), P.ps("pv", [128, 2, TB])
        NA = 4
        acc = [P.ps(f"acc{q}", [128, TB]) for q in range(NA)]
        names = ("c_in", "w_all", "th_rdy", "u_rdy", "pm_rdy", "sq_rdy", "pv_rdy", "v_rdy", "r_rdy", "mix_rdy", "hi_rdy", "lo_rdy", "m_free", "g_in", "g_free")
        s = {n: P.sem(n) for n in names}
        acc_rdy, acc_free = ([P.sem(f"{n}{q}") for q in range(NA)] for n in ("acc_rdy", "acc_free"))
        raw_in, raw_free, rhi, y_in, y_free, stage_in, stage_rdy, stage_st = (
            [P.sem(f"{n}{q}") for q in two] for n in ("raw_in", "raw_free", "rhi", "y_in", "y_free", "stage_in", "stage_rdy", "stage_st"))
        block = ctx.enter_context(nc.Block())
        wl = lay(w_out, l)
        assert NB % 2 == 0 and DM == 2 * TB

        def blocks(eng, body):
            with eng.Fori(0, NB // 2 - 1) as i:
                for q in two:
                    body(i * 2 + q, q, True, True)
            body(NB - 2, 0, True, False)
            body(NB - 1, 1, False, False)

        def weight(w, k, q):
            return w[:, bass.ds(k, 1), q * TB:(q + 1) * TB].rearrange("p a n -> p (a n)")

        @block.sync
        def _(sp):
            sp.dma_start(pars[:], lay(par, l)).then_inc(s["c_in"], 16)
            sp.dma_start(bones[:], consts[:, 256:384]).then_inc(s["c_in"], 16)

            def load_block(i, q):
                cols = bass.ds(i * TB, TB)
                sp.wait_ge(y_free[q], 1)
                sp.sem_inc(y_free[q], -1)
                sp.dma_start(y[q][:, 0:6, :], mixT[0:768, cols].rearrange("(k p) t -> p k t", p=128)).then_inc(y_in[q], 16)
                sp.dma_start(bv[q][:], rw[5 * GW:6 * GW, cols].rearrange("(k p) t -> p k t", p=128)).then_inc(y_in[q], 16)
                for n, r in enumerate((R_CB, R_CC, R_CX)):
                    sp.dma_start(cv[q][:, n], projT[r:r + GW, bass.ds(i * TB + (PAD - 2), TB + 2)].rearrange("(k p) t -> p k t", p=128)).then_inc(y_in[q], 16)

            def load_gates(i):
                sp.wait_ge(s["g_free"], 1)
                sp.sem_inc(s["g_free"], -1)
                for n, r in enumerate((R_FG, R_RG, R_SG, R_CG)):
                    sp.dma_start(g[:, 2 * n:2 * n + 2, :], projT[r:r + GW, bass.ds(i * TB + PAD, TB)].rearrange("(k p) t -> p k t", p=128)).then_inc(s["g_in"], 16)

            load_block(0, 0)
            load_gates(0)
            with sp.Fori(0, KC) as k:
                for q in two:
                    sp.wait_ge(raw_free[q], 1)
                    sp.sem_inc(raw_free[q], -1)
                    sp.dma_start(raw[q][:], wl[bass.ds(k * 128, 128), q * TB:(q + 1) * TB]).then_inc(raw_in[q], 16)
            load_block(1, 1)

            def body(i, q, follows, load):
                cols = bass.ds(i * TB, TB)
                if follows:
                    load_gates(i + 1)
                for d in range(KC):
                    e = d % 2
                    sp.wait_ge(stage_st[e], 16)
                    sp.sem_inc(stage_st[e], -16)
                    sp.dma_start(stage[e][:], xT[d * 128:(d + 1) * 128, cols]).then_inc(stage_in[e], 16)
                    if d == 2 and load:
                        load_block(i + 2, q)
                    if d > 0:
                        sp.wait_ge(stage_rdy[1 - e], 1)
                        sp.sem_inc(stage_rdy[1 - e], -1)
                        sp.dma_start(xT[(d - 1) * 128:d * 128, cols], stage[1 - e][:]).then_inc(stage_st[1 - e], 16)
                sp.wait_ge(stage_rdy[1], 1)
                sp.sem_inc(stage_rdy[1], -1)
                sp.dma_start(xT[(KC - 1) * 128:KC * 128, cols], stage[1][:]).then_inc(stage_st[1], 16)
            blocks(sp, body)
            for q in two:
                sp.wait_ge(stage_st[q], 16)

        @block.scalar
        def _(act):
            A = nc.scalar.activation

            def gates():
                act.wait_ge(s["g_in"], 64)
                act.sem_inc(s["g_in"], -64)
                A(th[:], g[:], ACT.Tanh, scale=0.5).then_inc(s["th_rdy"], 1)
                act.wait_ge(s["v_rdy"], 1)
                act.sem_inc(s["v_rdy"], -1)
                A(sq[:], sq[:], ACT.Ln)
                act.drain()
                A(sq[:], sq[:], ACT.Exp, scale=-0.5).then_inc(s["r_rdy"], 1)

            act.sem_inc(s["g_free"], 1)
            with act.Fori(0, KC) as k:
                for q in two:
                    act.wait_ge(raw_in[q], 16)
                    act.sem_inc(raw_in[q], -16)
                    A(weight(wo_hi, k, q), raw[q][:], ACT.Copy).then_inc(rhi[q], 1)
            gates()

            def body(i, q, follows, load):
                act.wait_ge(s["mix_rdy"], 1)
                act.sem_inc(s["mix_rdy"], -1)
                if follows:
                    act.sem_inc(s["g_free"], 1)
                act.wait_ge(s["m_free"], 1)
                act.sem_inc(s["m_free"], -1)
                for c in range(0, KC, 2):
                    A(m_hi[:, c:c + 2, :], y[q][:, c:c + 2, :], ACT.Copy).then_inc(s["hi_rdy"], 1)
                if follows:
                    gates()
            blocks(act, body)

        @block.gpsimd
        def _(pool):
            for q in two:
                pool.sem_inc(y_free[q], 1)
                pool.sem_inc(raw_free[q], 1)
            with pool.Fori(0, KC) as k:
                for q in two:
                    pool.wait_ge(rhi[q], 1)
                    pool.sem_inc(rhi[q], -1)
                    nc.gpsimd.tensor_tensor(weight(wo_lo, k, q), raw[q][:], weight(wo_hi, k, q).bitcast(F32), ALU.subtract).then_inc(raw_free[q], 1)
            pool.drain().then_inc(s["w_all"], 1)

            def body(i, q, follows, load):
                for c in range(0, KC, 2):
                    pool.wait_ge(s["hi_rdy"], 1)
                    pool.sem_inc(s["hi_rdy"], -1)
                    nc.gpsimd.tensor_tensor(m_lo[:, c:c + 2, :], y[q][:, c:c + 2, :], m_hi[:, c:c + 2, :].bitcast(F32), ALU.subtract).then_inc(s["lo_rdy"], 1)
                pool.drain().then_inc(y_free[q], 1)
            blocks(pool, body)

        @block.tensor
        def _(pe):
            M = nc.tensor.matmul
            pe.wait_ge(s["c_in"], 32)

            def head_sums(q):
                pe.wait_ge(s["u_rdy"], 1)
                pe.sem_inc(s["u_rdy"], -1)
                for p in two:
                    ins = M(pm[:, p, :], bones[:], y[q][:, 2 + p, :], start=True, stop=True)
                ins.then_inc(s["pm_rdy"], 1)

            def head_squares():
                pe.wait_ge(s["sq_rdy"], 1)
                pe.sem_inc(s["sq_rdy"], -1)
                for p in two:
                    ins = M(pv[:, p, :], bones[:], sq[:, p, :], start=True, stop=True)
                ins.then_inc(s["pv_rdy"], 1)

            head_sums(0)
            head_squares()
            pe.sem_inc(s["m_free"], 1)
            pe.wait_ge(s["w_all"], 1)

            def body(i, q, follows, load):
                for d in range(KC):
                    a = acc[d % NA]
                    cs = slice(d * 128, (d + 1) * 128)
                    pe.wait_ge(acc_free[d % NA], 1)
                    pe.sem_inc(acc_free[d % NA], -1)
                    for k in range(KC):
                        if d == 0 and k % 2 == 0:
                            pe.wait_ge(s["lo_rdy"], 1)
                            pe.sem_inc(s["lo_rdy"], -1)
                        M(a[:], wo_hi[:, k, cs], m_hi[:, k, :], start=(k == 0), stop=False)
                        M(a[:], wo_hi[:, k, cs], m_lo[:, k, :], start=False, stop=False)
                        ins = M(a[:], wo_lo[:, k, cs], m_hi[:, k, :], start=False, stop=(k == KC - 1))
                    ins.then_inc(acc_rdy[d % NA], 1)
                    if d == 0 and follows:
                        head_sums(1 - q)
                    if d == 2 and follows:
                        head_squares()
                pe.drain().then_inc(s["m_free"], 1)
            blocks(pe, body)

        @block.vector
        def _(v):
            V = nc.vector
            v.wait_ge(s["c_in"], 32)
            for q in two:
                v.sem_inc(stage_st[q], 16)
            for q in range(NA):
                v.sem_inc(acc_free[q], 1)

            def add_x(d):
                e = d % 2
                v.wait_ge(acc_rdy[d % NA], 1)
                v.sem_inc(acc_rdy[d % NA], -1)
                v.wait_ge(stage_in[e], 16)
                v.sem_inc(stage_in[e], -16)
                V.tensor_tensor(stage[e][:], acc[d % NA][:], stage[e][:], ALU.add).then_inc(stage_rdy[e], 1)
                v.drain().then_inc(acc_free[d % NA], 1)

            def mix(q, between):
                y_, g_, cv_ = y[q], g, cv[q]
                v.wait_ge(y_in[q], 80)
                v.sem_inc(y_in[q], -80)
                v.drain().then_inc(s["u_rdy"], 1)
                V.tensor_tensor(cv_[:, 1], cv_[:, 1], cv_[:, 2], ALU.mult)
                v.drain()
                for p in two:
                    V.tensor_scalar(y_[:, 6 + p, :], cv_[:, 1, p, 2:TB + 2], pars[:, C_CW + 4 + p:C_CW + 5 + p], None, ALU.mult)
                for w in (1, 0):
                    v.drain()
                    for p in two:
                        V.scalar_tensor_tensor(y_[:, 6 + p, :], cv_[:, 1, p, w:TB + w], pars[:, C_CW + 2 * w + p:C_CW + 2 * w + p + 1], y_[:, 6 + p, :], ALU.mult, ALU.add)
                v.wait_ge(s["pm_rdy"], 1)
                v.sem_inc(s["pm_rdy"], -1)
                V.scalar_tensor_tensor(y_[:, 2:4, :], pm[:], -1.0 / HD, y_[:, 2:4, :], ALU.mult, ALU.add)
                v.drain()
                V.tensor_tensor(sq[:], y_[:, 2:4, :], y_[:, 2:4, :], ALU.mult).then_inc(s["sq_rdy"], 1)
                between(0)
                V.tensor_tensor(y_[:, 6:8, :], y_[:, 6:8, :], cv_[:, 0, :, 2:TB + 2], ALU.mult)
                between(1)
                v.wait_ge(s["pv_rdy"], 1)
                v.sem_inc(s["pv_rdy"], -1)
                V.tensor_scalar(sq[:], pv[:], 1.0 / HD, LN_EPS, ALU.mult, ALU.add).then_inc(s["v_rdy"], 1)
                between(2)
                v.wait_ge(s["th_rdy"], 1)
                v.sem_inc(s["th_rdy"], -1)
                V.scalar_tensor_tensor(g_[:, 0:4, :], th[:, 0:4, :], 1.0, g_[:, 0:4, :], ALU.add, ALU.mult)
                V.scalar_tensor_tensor(g_[:, 4:8, :], th[:, 4:8, :], 1.0, g_[:, 4:8, :], ALU.add, ALU.mult)
                between(3)
                v.wait_ge(s["r_rdy"], 1)
                v.sem_inc(s["r_rdy"], -1)
                V.tensor_tensor(y_[:, 2:4, :], y_[:, 2:4, :], sq[:], ALU.mult)
                v.drain()
                for p in two:
                    V.tensor_scalar(y_[:, 2 + p, :], y_[:, 2 + p, :], pars[:, C_LG + p:C_LG + p + 1], pars[:, C_LB + p:C_LB + p + 1], ALU.mult, ALU.add)
                v.drain()
                V.tensor_tensor(y_[:, 2:4, :], y_[:, 2:4, :], bv[q][:], ALU.add)
                between(4)
                v.drain()
                V.scalar_tensor_tensor(y_[:, 0:4, :], g_[:, 0:4, :], 0.5, y_[:, 0:4, :], ALU.mult, ALU.mult)
                between(5)
                V.scalar_tensor_tensor(y_[:, 4:8, :], g_[:, 4:8, :], 0.5, y_[:, 4:8, :], ALU.mult, ALU.mult).then_inc(s["mix_rdy"], 1)
                between(6)
                between(7)

            mix(0, lambda d: None)

            def body(i, q, follows, load):
                if follows:
                    mix(1 - q, add_x)
                else:
                    for d in range(KC):
                        add_x(d)
            blocks(v, body)


def hybrid_trunk(nc, x, w_in, w_out, par, lora, consts, masks, rope, out, layers=L, debug=None):
    def dram(n, shape):
        return nc.dram_tensor(n, shape, F32, kind="ExternalOutput" if debug else "Internal").ap()

    xT, mixT = dram("xT", (DM, T)), dram("mixT", (DM, T))
    projT = dram("projT", (DIN, PAD + T))
    rw, pend, fa = dram("rw", (6 * GW, T)), dram("pend", (GW, T // CH)), dram("fa", (4 * NH, T))
    phase_transpose(nc, consts, x, xT, projT)
    with nc.Fori(0, layers) as l:
        with nc.sbuf_tensor("h_hi", [128, KC, T], F32R) as h_hi, nc.sbuf_tensor("h_lo", [128, KC, T], F32R) as h_lo:
            phase_project(nc, l, xT, w_in, par, consts, projT, h_hi, h_lo)
            phase_rwkv_prep(nc, l, projT, par, lora, consts, rw, pend, w_in, h_hi, h_lo)
            phase_rwkv_scan(nc, l, rw, pend, consts, masks, mixT, w_in, projT, h_hi, h_lo)
        phase_head_norm(nc, l, projT, par, consts, rope, fa)
        phase_fox(nc, l, projT, fa, consts, mixT)
        phase_swa(nc, l, projT, par, consts, masks, mixT)
        phase_out(nc, l, projT, rw, w_out, par, consts, mixT, xT)
    phase_transpose(nc, consts, xT, out)


def constants():
    i = np.arange(128)
    eye = np.eye(128)
    same = lambda n: (i[:, None] // n) == (i[None, :] // n)
    reset = np.tile(np.where(np.arange(TB) % CH == 0, 0.0, 1.0), (128, 1))
    perm = np.zeros((128, 128))
    perm[i, i ^ 32] = 1.0
    causal = np.where(i[None, :] <= i[:, None], 0.0, -1e30)
    consts = np.concatenate([eye, np.ones((128, 128)), same(64), reset, perm, causal], 1)
    low = i[None, :] < i[:, None]
    m = [low & same(16), low & same(32) & ~same(16), low & same(64) & ~same(32), (low & same(16)).T, (low & same(64)).T, ((low | (eye > 0)) & same(64)).T]
    k = np.arange(192)
    win = (k[None, :] // 64 == i[:, None] // 64) | (k[None, :] // 64 == i[:, None] // 64 + 1)
    w1 = np.where(win, 0.0, -1e30)
    w0 = np.where(win & (k[None, :] >= 64), 0.0, -1e30)
    masks = np.concatenate([a.astype(np.float32) for a in m] + [w0, w1], 1)
    half = HD // 2
    inv = np.float32(10000.0) ** (-np.arange(half, dtype=np.float32) / np.float32(half))
    ang = np.arange(T, dtype=np.float32)[None, :] * inv[:, None].astype(np.float32)
    cos, sin = np.cos(ang), np.sin(ang)
    rope = np.concatenate([np.tile(np.concatenate([cos, cos]), (2, 1)), np.tile(np.concatenate([-sin, sin]), (2, 1))], 1)
    return [np.ascontiguousarray(a, dtype=np.float32) for a in (consts, masks, rope)]


def pack_parameters(a):
    def cols(n):
        v = a[n].reshape(L, -1, 128)
        return v.transpose(0, 2, 1)

    def twice(n):
        return np.concatenate([a[n], a[n]], 1)[:, :, None]

    bf = np.zeros((L, 128, 1), a["fox_b_f"].dtype)
    bf[:, 0:NH, 0] = a["fox_b_f"]
    parts = [cols(n) for n in ("norm_g", "rwkv_mu", "rwkv_w0", "rwkv_a0", "rwkv_k_k", "rwkv_k_a", "rwkv_r_k", "rwkv_ln_g", "rwkv_ln_b")]
    parts += [twice("fox_q_norm")] * 2 + [twice("fox_k_norm")] * 2 + [twice("swa_q_norm")] * 2 + [twice("swa_k_norm")]
    parts += [cols("conv_w"), np.repeat(a["swa_sinks"][:, None, :], 128, 1), bf]
    return np.ascontiguousarray(np.concatenate(parts, 2))


LAYERS, DEBUG = L, None


def kernel(**inputs):
    import concourse.bacc as bacc
    from concourse.bass_utils import run_bass_kernel_spmd as run

    a = {n: np.ascontiguousarray(v) for n, v in inputs.items()}
    consts, masks, rope = constants()
    feeds = {
        "x": a["x"].reshape(T, DM), "w_in": a["w_in"], "w_out": a["w_out"], "par": pack_parameters(a),
        "lora": np.ascontiguousarray(np.concatenate([a["rwkv_w_up"], a["rwkv_a_up"]], 1)),
        "consts": consts, "masks": masks, "rope": rope,
    }
    nc = bacc.Bacc("TRN2", target_bir_lowering=False, num_devices=1)
    args = [nc.dram_tensor(n, v.shape, F32, kind="ExternalInput").ap() for n, v in feeds.items()]
    args.append(nc.dram_tensor("out", (T, DM), F32, kind="ExternalOutput").ap())
    hybrid_trunk(nc, *args, layers=LAYERS, debug=DEBUG)
    r = run(nc, [feeds], core_ids=[0])
    return r.results[0]["out"].reshape(1, T, DM)
```

```python
import concourse.bass as bass
from concourse import mybir
from contextlib import ExitStack
import numpy as np

F32 = mybir.dt.float32
F32R = mybir.dt.float32r
BF16 = mybir.dt.bfloat16
ALU = mybir.AluOpType
ACT = mybir.ActivationFunctionType
AX = mybir.AxisListType

L, T, DM = 2, 2048, 1024
GW, HD, NH = 256, 64, 4
DIN = 3972
KC = DM // 128
TB = 512
NB = T // TB
NT = T // 128
PAD = 64
CH = 64
R_FQ, R_FK, R_FV, R_FF, R_FG = 0, 256, 512, 768, 772
R_PRE, R_RG, R_SQ, R_SK, R_SV, R_SG = 1028, 1924, 2180, 2436, 2564, 2692
R_CB, R_CC, R_CX, R_CG = 2948, 3204, 3460, 3716
C_NG, C_MU, C_W0, C_A0, C_KK, C_KA, C_RK, C_LG, C_LB = 0, 8, 15, 17, 19, 21, 23, 25, 27
C_GN, C_CW, C_SINK, C_BF, NPAR = 29, 36, 42, 46, 47
C_GATHER = 1152
C_SPREAD = C_GATHER + 7 * 14
NCONST = C_SPREAD + 7 * 128
EPS, LN_EPS = 1e-6, 64e-5
CDEC = -0.5 * float(np.exp(-0.5))


class Phase:
    def __init__(self, nc, ctx, name):
        self.nc, self.ctx, self.name = nc, ctx, name
        self.sems = []
        ctx.callback(self.close)

    def close(self):
        self.nc.clear_and_free_semaphores(self.sems)
        self.nc.all_engine_barrier(sem_only=True)

    def sb(self, n, shape, dt=F32):
        return self.ctx.enter_context(self.nc.sbuf_tensor(f"{self.name}_{n}", shape, dt))

    def ps(self, n, shape, dt=F32):
        return self.ctx.enter_context(self.nc.psum_tensor(f"{self.name}_{n}", shape, dt))

    def sem(self, n):
        self.sems.append(self.nc.alloc_semaphore(f"{self.name}_{n}"))
        return self.sems[-1]


def lay(t, l):
    v = t[bass.ds(l, 1)]
    return v.rearrange("a p n -> (a p) n")


def phase_transpose(nc, consts, source, target, projT=None):
    with ExitStack() as ctx:
        to_channels = projT is not None
        P = Phase(nc, ctx, "lx" if to_channels else "sx")
        two = range(2)
        ident = P.sb("ident", [128, 128])
        xin, xo = ([P.sb(f"{n}{q}", [128, KC, 128]) for q in two] for n in ("xin", "xo"))
        zero = P.sb("zero", [128, PAD])
        pt = [P.ps(f"pt{q}", [128, KC, 128]) for q in two]
        c_in, z_rdy, z_st = (P.sem(n) for n in ("c_in", "z_rdy", "z_st"))
        x_in, x_free, t_done, t_free, o_rdy, st = ([P.sem(f"{n}{q}") for q in two] for n in ("x_in", "x_free", "t_done", "t_free", "o_rdy", "st"))
        block = ctx.enter_context(nc.Block())

        def tile(x, t, channels):
            if channels:
                return x[:, bass.ds(t * 128, 128)].rearrange("(k p) t -> p k t", p=128)
            return x[bass.ds(t * 128, 128), :].rearrange("p (k c) -> p k c", k=KC)

        @block.sync
        def _(sp):
            sp.dma_start(ident[:], consts[:, 0:128]).then_inc(c_in, 16)

            def load(t, q):
                sp.wait_ge(x_free[q], 1)
                sp.sem_inc(x_free[q], -1)
                sp.dma_start(xin[q][:], tile(source, t, not to_channels)).then_inc(x_in[q], 16)

            def store(t, q):
                sp.wait_ge(o_rdy[q], 1)
                sp.sem_inc(o_rdy[q], -1)
                sp.dma_start(tile(target, t, to_channels), xo[q][:]).then_inc(st[q], 16)

            load(0, 0)
            with sp.Fori(0, NT // 2 - 1) as i:
                for q in two:
                    load(i * 2 + (1 + q), 1 - q)
                    store(i * 2 + q, q)
            load(NT - 1, 1)
            for q in two:
                store(NT - 2 + q, q)
            if to_channels:
                sp.wait_ge(z_rdy, 1)
                for r in range(R_PRE, DIN, 128):
                    sp.dma_start(projT[r:r + 128, 0:PAD], zero[0:min(128, DIN - r), :]).then_inc(z_st, 16)
                sp.wait_ge(z_st, 16 * len(range(R_PRE, DIN, 128)))
            for q in two:
                sp.wait_ge(st[q], 16)

        @block.tensor
        def _(pe):
            pe.wait_ge(c_in, 16)
            with pe.Fori(0, NT // 2) as i:
                for q in two:
                    pe.wait_ge(x_in[q], 16)
                    pe.sem_inc(x_in[q], -16)
                    pe.wait_ge(t_free[q], 1)
                    pe.sem_inc(t_free[q], -1)
                    for k in range(KC):
                        ins = nc.tensor.transpose(pt[q][:, k, :], xin[q][:, k, :], ident[:])
                    ins.then_inc(t_done[q], 1)

        @block.vector
        def _(v):
            if to_channels:
                nc.vector.memset(zero[:], 0.0).then_inc(z_rdy, 1)
            for q in two:
                v.sem_inc(x_free[q], 1)
                v.sem_inc(t_free[q], 1)
                v.sem_inc(st[q], 16)
            with v.Fori(0, NT // 2) as i:
                for q in two:
                    v.wait_ge(t_done[q], 1)
                    v.sem_inc(t_done[q], -1)
                    v.sem_inc(x_free[q], 1)
                    v.wait_ge(st[q], 16)
                    v.sem_inc(st[q], -16)
                    nc.vector.tensor_copy(xo[q][:], pt[q][:]).then_inc(o_rdy[q], 1)
                    v.drain().then_inc(t_free[q], 1)


class Projector:
    def __init__(self, P, nc, l, w_in, h_hi, h_lo, projT):
        self.nc, self.wl, self.h_hi, self.h_lo, self.projT = nc, lay(w_in, l), h_hi, h_lo, projT
        self.raw = P.sb("raw", [128, KC, 128])
        self.w_hi = [P.sb(f"w_hi{q}", [128, KC, 128], F32R) for q in range(2)]
        self.w_lo = [P.sb(f"w_lo{q}", [128, KC, 128], F32R) for q in range(2)]
        self.stage = [P.sb(f"stage{q}", [128, TB]) for q in range(2)]
        self.acc = [P.ps(f"acc{q}", [128, TB]) for q in range(2)]
        self.raw_in, self.raw_free, self.whi_rdy = P.sem("raw_in"), P.sem("raw_free"), P.sem("whi_rdy")
        self.w_rdy, self.w_free, self.acc_rdy, self.acc_free, self.stage_rdy, self.stage_st = (
            [P.sem(f"{n}{q}") for q in range(2)] for n in ("w_rdy", "w_free", "acc_rdy", "acc_free", "stage_rdy", "stage_st"))

    def act_start(self, act, first=0):
        act.sem_inc(self.raw_free, 1)
        act.sem_inc(self.w_free[first], 1)
        for q in range(2):
            act.sem_inc(self.acc_free[q], 1)
            act.sem_inc(self.stage_st[q], 16)

    def act_load(self, act, r, m=128):
        act.wait_ge(self.raw_free, 1)
        act.sem_inc(self.raw_free, -1)
        act.dma_start(self.raw[:, :, 0:m], self.wl[:, bass.ds(r, m)].rearrange("(k p) c -> p k c", p=128)).then_inc(self.raw_in, 16)

    def act_split(self, act, q, m=128):
        act.wait_ge(self.raw_in, 16)
        act.sem_inc(self.raw_in, -16)
        act.wait_ge(self.w_free[q], 1)
        act.sem_inc(self.w_free[q], -1)
        self.nc.scalar.activation(self.w_hi[q][:, :, 0:m], self.raw[:, :, 0:m], ACT.Copy).then_inc(self.whi_rdy, 1)

    def pool_weights(self, pool, q, m=128):
        pool.wait_ge(self.whi_rdy, 1)
        pool.sem_inc(self.whi_rdy, -1)
        self.nc.gpsimd.tensor_tensor(self.w_lo[q][:, :, 0:m], self.raw[:, :, 0:m], self.w_hi[q][:, :, 0:m].bitcast(F32), ALU.subtract).then_inc(self.w_rdy[q], 1)
        pool.drain().then_inc(self.raw_free, 1)

    def pe_tile(self, pe, q, m=128):
        M = self.nc.tensor.matmul
        pe.wait_ge(self.w_rdy[q], 1)
        pe.sem_inc(self.w_rdy[q], -1)
        for b in range(NB):
            pe.wait_ge(self.acc_free[b % 2], 1)
            pe.sem_inc(self.acc_free[b % 2], -1)
            cols, acc = slice(b * TB, (b + 1) * TB), self.acc[b % 2][0:m, :]
            for k in range(KC):
                ins = M(acc, self.w_hi[q][:, k, 0:m], self.h_hi[:, k, cols], start=(k == 0), stop=False)
                if b == 0 and k == 0:
                    ins.then_inc(self.w_free[1 - q], 1)
                yield
                M(acc, self.w_hi[q][:, k, 0:m], self.h_lo[:, k, cols], start=False, stop=False)
                yield
                ins = M(acc, self.w_lo[q][:, k, 0:m], self.h_hi[:, k, cols], start=False, stop=(k == KC - 1))
                if k == KC - 1:
                    ins.then_inc(self.acc_rdy[b % 2], 1)
                yield

    def evacuate(self, eng, copy, b, m=128):
        eng.wait_ge(self.acc_rdy[b % 2], 1)
        eng.sem_inc(self.acc_rdy[b % 2], -1)
        eng.wait_ge(self.stage_st[b % 2], 16)
        eng.sem_inc(self.stage_st[b % 2], -16)
        copy(self.stage[b % 2][0:m, :], self.acc[b % 2][0:m, :]).then_inc(self.stage_rdy[b % 2], 1)
        eng.drain().then_inc(self.acc_free[b % 2], 1)

    def sp_store(self, sp, r, b, m=128):
        sp.wait_ge(self.stage_rdy[b % 2], 1)
        sp.sem_inc(self.stage_rdy[b % 2], -1)
        sp.dma_start(self.projT[bass.ds(r, m), PAD + b * TB:PAD + (b + 1) * TB], self.stage[b % 2][0:m, :]).then_inc(self.stage_st[b % 2], 16)


def phase_project(nc, l, xT, w_in, par, consts, projT, h_hi, h_lo):
    with ExitStack() as ctx:
        P = Phase(nc, ctx, "pj")
        pars = P.sb("pars", [128, NPAR])
        ones = P.sb("ones", [128, 128])
        NX, XB = 4, 256
        xb = [P.sb(f"xb{q}", [128, KC, XB]) for q in range(NX)]
        sq, rst = P.sb("sq", [128, KC, XB]), P.sb("rst", [128, XB])
        ss = P.ps("ss", [128, XB])
        names = ("c_in", "sq_rdy", "ss_rdy", "ss_free", "var_rdy", "r_rdy", "h_rdy", "hi_rdy", "h_blk")
        s = {n: P.sem(n) for n in names}
        x_in, x_free = ([P.sem(f"{n}{q}") for q in range(NX)] for n in ("x_in", "x_free"))
        J = Projector(P, nc, l, w_in, h_hi, h_lo, projT)
        block = ctx.enter_context(nc.Block())
        HK = KC // 2
        NBX = T // XB
        assert (R_RG - R_PRE) % 256 == 128 and TB == 2 * XB

        def tiles(eng, body):
            with eng.Fori(0, (R_RG - R_PRE) // 256) as i:
                for q in range(2):
                    body(i * 256 + (R_PRE + 128 * q), q, i * 256 + (R_PRE + 128 * (q + 1)))
            body(R_RG - 128, 0, None)

        @block.sync
        def _(sp):
            sp.dma_start(pars[:], lay(par, l)).then_inc(s["c_in"], 16)
            sp.dma_start(ones[:], consts[:, 128:256]).then_inc(s["c_in"], 16)
            for i in range(NBX):
                sp.wait_ge(x_free[i % NX], 1)
                sp.sem_inc(x_free[i % NX], -1)
                sp.dma_start(xb[i % NX][:], xT[:, i * XB:(i + 1) * XB].rearrange("(k p) t -> p k t", p=128)).then_inc(x_in[i % NX], 16)

            for b in range(NB):
                J.sp_store(sp, R_FF, b, NH)

            def body(row, q, follows):
                for b in range(NB):
                    J.sp_store(sp, row, b)
            tiles(sp, body)
            for q in range(2):
                sp.wait_ge(J.stage_st[q], 16)

        @block.scalar
        def _(act):
            A = nc.scalar.activation
            J.act_start(act, 1)

            def square(i):
                act.wait_ge(x_in[i % NX], 16)
                act.sem_inc(x_in[i % NX], -16)
                A(sq[:], xb[i % NX][:], ACT.Square).then_inc(s["sq_rdy"], 1)

            square(0)
            J.act_load(act, R_FF, NH)
            for i in range(NBX):
                act.wait_ge(s["var_rdy"], 1)
                act.sem_inc(s["var_rdy"], -1)
                if i + 1 < NBX:
                    square(i + 1)
                A(rst[:], rst[:], ACT.Ln)
                act.drain()
                A(rst[:], rst[:], ACT.Exp, scale=-0.5).then_inc(s["r_rdy"], 1)
                for c in (0, HK):
                    act.wait_ge(s["h_rdy"], 1)
                    act.sem_inc(s["h_rdy"], -1)
                    A(h_hi[:, c:c + HK, i * XB:(i + 1) * XB], xb[i % NX][:, c:c + HK, :], ACT.Copy).then_inc(s["hi_rdy"], 1)
                if i == 0:
                    J.act_split(act, 1, NH)
                if i == 1:
                    J.act_load(act, R_PRE)

            def body(row, q, follows):
                J.act_split(act, q)
                if follows is not None:
                    J.act_load(act, follows)
            tiles(act, body)

        @block.gpsimd
        def _(pool):
            for q in range(NX):
                pool.sem_inc(x_free[q], 1)
            for i in range(NBX):
                for c in (0, HK):
                    dst = slice(i * XB, (i + 1) * XB)
                    pool.wait_ge(s["hi_rdy"], 1)
                    pool.sem_inc(s["hi_rdy"], -1)
                    ins = nc.gpsimd.tensor_tensor(h_lo[:, c:c + HK, dst], xb[i % NX][:, c:c + HK, :], h_hi[:, c:c + HK, dst].bitcast(F32), ALU.subtract)
                ins.then_inc(x_free[i % NX], 1)
                if i % 2 == 1:
                    pool.drain().then_inc(s["h_blk"], 1)
                if i == 0:
                    J.pool_weights(pool, 1, NH)
            tiles(pool, lambda row, q, follows: J.pool_weights(pool, q))

        @block.tensor
        def _(pe):
            pe.wait_ge(s["c_in"], 32)
            gates = J.pe_tile(pe, 1, NH)

            def gate_block():
                pe.wait_ge(s["h_blk"], 1)
                pe.sem_inc(s["h_blk"], -1)
                for _ in range(3 * KC):
                    next(gates)

            for i in range(NBX):
                pe.wait_ge(s["sq_rdy"], 1)
                pe.sem_inc(s["sq_rdy"], -1)
                pe.wait_ge(s["ss_free"], 1)
                pe.sem_inc(s["ss_free"], -1)
                for k in range(KC):
                    ins = nc.tensor.matmul(ss[:], ones[:], sq[:, k, :], start=(k == 0), stop=(k == KC - 1))
                ins.then_inc(s["ss_rdy"], 1)
                if i % 2 == 1 and i > 1:
                    gate_block()
            gate_block()

            def body(row, q, follows):
                for _ in J.pe_tile(pe, q):
                    pass
            tiles(pe, body)

        @block.vector
        def _(v):
            V = nc.vector
            v.wait_ge(s["c_in"], 32)
            v.sem_inc(s["ss_free"], 1)
            for i in range(NBX):
                x = xb[i % NX]
                v.wait_ge(s["ss_rdy"], 1)
                v.sem_inc(s["ss_rdy"], -1)
                v.drain()
                V.tensor_scalar(rst[:], ss[:], 1.0 / DM, EPS, ALU.mult, ALU.add).then_inc(s["var_rdy"], 1)
                v.drain().then_inc(s["ss_free"], 1)
                v.wait_ge(s["r_rdy"], 1)
                v.sem_inc(s["r_rdy"], -1)
                for k in range(KC):
                    ins = V.scalar_tensor_tensor(x[:, k, :], x[:, k, :], pars[:, C_NG + k:C_NG + k + 1], rst[:], ALU.mult, ALU.mult)
                    if k % HK == HK - 1:
                        ins.then_inc(s["h_rdy"], 1)
                if i % 2 == 0 and i > 2:
                    J.evacuate(v, V.tensor_copy, i // 2 - 2, NH)
            for b in range(NB - 2, NB):
                J.evacuate(v, V.tensor_copy, b, NH)

            def body(row, q, follows):
                for b in range(NB):
                    J.evacuate(v, V.tensor_copy, b)
            tiles(v, body)


PREP_FILL = (("th", 16), ("lora", 24), ("ssk", 20), ("bs", 36))
SCAN_FILL = (("tok", 6), ("mk", 4), ("s3", 5), ("s4", 5), ("s5", 7), ("s6", 6), ("s7", 7), ("s8", 6), ("s9", 7), ("wz", 7), ("g", 8), ("c0", 8), ("c1", 20))
assert sum(n for _, n in PREP_FILL) == sum(n for _, n in SCAN_FILL) == 3 * KC * NB


def units_done(plan, stage):
    unit, before = 3 * KC, 0
    for name, n in plan:
        if name == stage:
            return range(before // unit, (before + n) // unit)
        before += n


def phase_rwkv_prep(nc, l, projT, par, lora, consts, rw, pend, w_in, h_hi, h_lo):
    with ExitStack() as ctx:
        P = Phase(nc, ctx, "rp")
        two = range(2)
        PB = 256
        NU = T // PB
        assert NU == (R_FF + GW) // 128 and NU % 2 == 0
        pars, half = P.sb("pars", [128, NPAR]), P.sb("half", [128, NPAR])
        bones, cmask = P.sb("bones", [128, 128]), P.sb("cmask", [128, PB])
        up = P.sb("up", [128, GW])
        pre = [P.sb(f"pre{q}", [128, 7, PB + 1]) for q in two]
        dif, xs = P.sb("dif", [128, 7, PB]), P.sb("xs", [128, 7, PB])
        lw, ta2, cum, cmp_, pi, kkr, ta, tb, tk_, tr, keff, bv = (P.sb(n, [128, 2, PB]) for n in (
            "lw", "ta2", "cum", "cmp", "pi", "kkr", "ta", "tb", "tk", "tr", "keff", "bv"))
        th, sqk, rk, nrm, pp, pq = dif[0:64, 6, :], dif[:, 0:2, :], dif[:, 2:4, :], dif[:, 4:6, :], lw, cmp_
        pend_sb = P.sb("pend", [128, 2, T // CH])
        pw, pa, pk, pb = (P.ps(n, [128, 2, PB]) for n in ("pw", "pa", "pk", "pb"))
        names = ("c_in", "half_rdy", "xs_rdy", "v_rdy", "v_st", "th_rdy", "lora_rdy", "t_rdy", "cum_rdy", "exp_rdy", "sqk_rdy", "ssk_rdy", "mx_rdy", "nrm_rdy", "rk_rdy", "bs_rdy", "out_rdy", "out_st", "pend_st")
        s = {n: P.sem(n) for n in names}
        p_in, pre_free = ([P.sem(f"{n}{q}") for q in two] for n in ("p_in", "pre_free"))
        J = Projector(P, nc, l, w_in, h_hi, h_lo, projT)
        block = ctx.enter_context(nc.Block())

        def units(eng, body):
            with eng.Fori(0, R_FF // 256 - 1) as i:
                body(i * 2, 0, i * 256, i * 256 + 128)
                body(i * 2 + 1, 1, i * 256 + 128, i * 256 + 256)
            body(NU - 4, 0, R_FF - 256, R_FF - 128)
            body(NU - 3, 1, R_FF - 128, R_FG)
            body(NU - 2, 0, R_FG, R_FG + 128)
            body(NU - 1, 1, R_FG + 128, None)

        @block.sync
        def _(sp):
            sp.dma_start(pars[:], lay(par, l)).then_inc(s["c_in"], 16)
            sp.dma_start(bones[:], consts[:, 256:384]).then_inc(s["c_in"], 16)
            sp.dma_start(cmask[:], consts[:, 384:384 + PB]).then_inc(s["c_in"], 16)
            sp.dma_start(up[:], lay(lora, l)).then_inc(s["c_in"], 16)

            def load(i, q):
                sp.wait_ge(pre_free[q], 1)
                sp.sem_inc(pre_free[q], -1)
                sp.dma_start(pre[q][:], projT[R_PRE:R_PRE + 896, bass.ds(i * PB + (PAD - 1), PB + 1)].rearrange("(k p) t -> p k t", p=128)).then_inc(p_in[q], 16)

            def put(i, n, buf, sem):
                sp.dma_start(rw[n * GW:(n + 1) * GW, bass.ds(i * PB, PB)].rearrange("(k p) t -> p k t", p=128), buf).then_inc(sem, 16)

            def body(i, q, row, follows):
                if follows is not None:
                    load(i + 1, 1 - q)
                sp.wait_ge(s["v_rdy"], 1)
                sp.sem_inc(s["v_rdy"], -1)
                put(i, 4, xs[:, 4:6, :], s["v_st"])
                J.sp_store(sp, row, 0)
                J.sp_store(sp, row, 1)
                sp.wait_ge(s["out_rdy"], 1)
                sp.sem_inc(s["out_rdy"], -1)
                for n, buf in ((0, ta), (1, tr), (2, tb), (3, tk_), (5, bv)):
                    put(i, n, buf[:], s["out_st"])
                J.sp_store(sp, row, 2)
                J.sp_store(sp, row, 3)

            load(0, 0)
            units(sp, body)
            sp.dma_start(pend.rearrange("(k p) c -> p k c", p=128), pend_sb[:]).then_inc(s["pend_st"], 16)
            sp.wait_ge(s["pend_st"], 16)
            sp.wait_ge(s["v_st"], 16)
            sp.wait_ge(s["out_st"], 80)
            for q in two:
                sp.wait_ge(J.stage_st[q], 16)

        @block.vector
        def _(v):
            V = nc.vector
            v.wait_ge(s["c_in"], 64)
            V.tensor_scalar(half[:], pars[:], 0.5, None, ALU.mult).then_inc(s["half_rdy"], 1)
            for q in two:
                v.sem_inc(pre_free[q], 1)
            v.sem_inc(s["v_st"], 16)
            v.sem_inc(s["out_st"], 80)
            v.drain()
            r_, k_, v_ = xs[:, 0:2, :], xs[:, 2:4, :], xs[:, 4:6, :]

            def body(i, q, row, follows):
                x = pre[q]
                v.wait_ge(p_in[q], 16)
                v.sem_inc(p_in[q], -16)
                V.tensor_tensor(dif[:], x[:, :, 0:PB], x[:, :, 1:PB + 1], ALU.subtract)
                v.drain()
                v.wait_ge(s["v_st"], 16)
                v.sem_inc(s["v_st"], -16)
                for j in (6, 2, 3, 0, 1, 4, 5):
                    ins = V.scalar_tensor_tensor(xs[:, j, :], dif[:, j, :], pars[:, C_MU + j:C_MU + j + 1], x[:, j, 1:PB + 1], ALU.mult, ALU.add)
                    if j == 6:
                        ins.then_inc(s["xs_rdy"], 1)
                ins.then_inc(s["v_rdy"], 1)
                v.drain().then_inc(pre_free[q], 1)
                for p in two:
                    V.tensor_scalar(kkr[:, p, :], k_[:, p, :], pars[:, C_KK + p:C_KK + p + 1], None, ALU.mult)
                v.drain()
                V.tensor_tensor(sqk, kkr[:], kkr[:], ALU.mult).then_inc(s["sqk_rdy"], 1)
                v.wait_ge(s["t_rdy"], 1)
                v.sem_inc(s["t_rdy"], -1)
                V.tensor_scalar(lw[:], lw[:], CDEC, CDEC, ALU.mult, ALU.add)
                for p in two:
                    V.tensor_scalar(keff[:, p, :], ta2[:, p, :], -1.0, half[:, C_KA + p:C_KA + p + 1], ALU.add, ALU.mult)
                v.drain()
                for p in two:
                    V.tensor_tensor_scan(cum[:, p, :], cmask[:], lw[:, p, :], 0.0, ALU.mult, ALU.add)
                V.scalar_tensor_tensor(keff[:], keff[:], 1.0, k_, ALU.add, ALU.mult)
                v.drain()
                V.tensor_tensor(cmp_[:], cum[:], lw[:], ALU.subtract).then_inc(s["cum_rdy"], 1)
                for p in two:
                    ins = V.scalar_tensor_tensor(rk[:, p, :], r_[:, p, :], pars[:, C_RK + p:C_RK + p + 1], keff[:, p, :], ALU.mult, ALU.mult)
                ins.then_inc(s["rk_rdy"], 1)
                v.wait_ge(s["ssk_rdy"], 1)
                v.sem_inc(s["ssk_rdy"], -1)
                V.tensor_scalar(nrm, pk[:], 1e-24, None, ALU.max).then_inc(s["mx_rdy"], 1)
                v.wait_ge(s["exp_rdy"], 1)
                v.sem_inc(s["exp_rdy"], -1)
                v.wait_ge(s["out_st"], 80)
                v.sem_inc(s["out_st"], -80)
                V.tensor_tensor(tk_[:], keff[:], pi[:], ALU.mult)
                V.tensor_tensor(tr[:], r_, pp[:], ALU.mult)
                V.tensor_copy(pend_sb[:, :, bass.ds(i * (PB // CH), PB // CH)], pp[:, :, CH - 1::CH])
                v.wait_ge(s["nrm_rdy"], 1)
                v.sem_inc(s["nrm_rdy"], -1)
                V.tensor_tensor(kkr[:], kkr[:], nrm, ALU.mult)
                v.drain()
                V.scalar_tensor_tensor(ta[:], pq[:], -1.0, kkr[:], ALU.mult, ALU.mult)
                V.scalar_tensor_tensor(tb[:], ta2[:], 1.0, kkr[:], ALU.add, ALU.mult)
                v.drain()
                V.scalar_tensor_tensor(tb[:], tb[:], 0.5, pi[:], ALU.mult, ALU.mult)
                v.wait_ge(s["bs_rdy"], 1)
                v.sem_inc(s["bs_rdy"], -1)
                V.tensor_tensor(bv[:], pb[:], v_, ALU.mult).then_inc(s["out_rdy"], 1)
            units(v, body)

        @block.scalar
        def _(act):
            A = nc.scalar.activation
            C = nc.scalar.copy
            J.act_start(act)

            def evac(stage):
                for b in units_done(PREP_FILL, stage):
                    J.evacuate(act, C, b)

            def body(i, q, row, follows):
                if follows is not None:
                    J.act_load(act, follows)
                act.wait_ge(s["xs_rdy"], 1)
                act.sem_inc(s["xs_rdy"], -1)
                A(th, xs[0:64, 6, :], ACT.Tanh).then_inc(s["th_rdy"], 1)
                evac("th")
                act.wait_ge(s["lora_rdy"], 1)
                act.sem_inc(s["lora_rdy"], -1)
                for p in two:
                    A(lw[:, p, :], pw[:, p, :], ACT.Tanh, bias=half[:, C_W0 + p:C_W0 + p + 1], scale=0.5)
                for p in two:
                    ins = A(ta2[:, p, :], pa[:, p, :], ACT.Tanh, bias=half[:, C_A0 + p:C_A0 + p + 1], scale=0.5)
                ins.then_inc(s["t_rdy"], 1)
                evac("lora")
                act.wait_ge(s["cum_rdy"], 1)
                act.sem_inc(s["cum_rdy"], -1)
                A(pi[:], cum[:], ACT.Exp, scale=-1.0)
                A(pq[:], cmp_[:], ACT.Exp)
                A(pp[:], cum[:], ACT.Exp).then_inc(s["exp_rdy"], 1)
                act.wait_ge(s["mx_rdy"], 1)
                act.sem_inc(s["mx_rdy"], -1)
                A(nrm, nrm, ACT.Ln)
                act.drain()
                A(nrm, nrm, ACT.Exp, scale=-0.5).then_inc(s["nrm_rdy"], 1)
                if follows is not None:
                    J.act_split(act, 1 - q)
                evac("ssk")
                evac("bs")

            act.wait_ge(s["half_rdy"], 1)
            J.act_load(act, 0)
            J.act_split(act, 0)
            units(act, body)

        @block.gpsimd
        def _(pool):
            units(pool, lambda i, q, row, follows: J.pool_weights(pool, q))

        @block.tensor
        def _(pe):
            M = nc.tensor.matmul
            pe.wait_ge(s["c_in"], 64)

            def body(i, q, row, follows):
                tile = J.pe_tile(pe, q)

                def fill(stage):
                    for _ in range(dict(PREP_FILL)[stage]):
                        next(tile)

                fill("th")
                pe.wait_ge(s["th_rdy"], 1)
                pe.sem_inc(s["th_rdy"], -1)
                for p in two:
                    M(pw[:, p, :], up[0:64, p * 128:(p + 1) * 128], th, start=True, stop=True)
                for p in two:
                    ins = M(pa[:, p, :], up[64:128, p * 128:(p + 1) * 128], xs[64:128, 6, :], start=True, stop=True)
                ins.then_inc(s["lora_rdy"], 1)
                fill("lora")
                pe.wait_ge(s["sqk_rdy"], 1)
                pe.sem_inc(s["sqk_rdy"], -1)
                for p in two:
                    ins = M(pk[:, p, :], bones[:], sqk[:, p, :], start=True, stop=True)
                ins.then_inc(s["ssk_rdy"], 1)
                fill("ssk")
                pe.wait_ge(s["rk_rdy"], 1)
                pe.sem_inc(s["rk_rdy"], -1)
                for p in two:
                    ins = M(pb[:, p, :], bones[:], rk[:, p, :], start=True, stop=True)
                ins.then_inc(s["bs_rdy"], 1)
                fill("bs")
            units(pe, body)


def phase_rwkv_scan(nc, l, rw, pend, consts, masks, mixT, w_in, projT, h_hi, h_lo):
    with ExitStack() as ctx:
        P = Phase(nc, ctx, "rs")
        two = range(2)
        ident = P.sb("ident", [128, 128])
        mk = P.sb("mk", [128, 6, 128])
        ar = [P.sb(f"ar{e}", [64, NH, 2, 128]) for e in two]
        bt, kt, vt = (P.sb(n, [64, NH, 128]) for n in ("bt", "kt", "vt"))
        pe_all = P.sb("pend", [64, NH, T // CH])
        aq = P.sb("aq", [128, NH, 128])
        bm, km = P.sb("bm", [128, 2, NH, 64]), P.sb("km", [128, 2, NH, 64])
        vm = P.sb("vm", [128, NH, 64])
        D, E1, E2, Dt, p2, p4, p4t, x1 = (P.sb(n, [128, NH, 128]) for n in ("D", "E1", "E2", "Dt", "p2", "p4", "p4t", "x1"))
        p8, xn, yy, wz, m1 = D, p2, p4, Dt, p2[0:64]
        gt = p4t[0:64].rearrange("p h (u t) -> p h u t", u=2)
        px = P.sb("px", [128, NH, 2, 128])
        arb = P.sb("arb", [128, NH, 128])
        ak = P.sb("ak", [128, NH, 2, 128])
        S = P.sb("S", [64, 2, NH, 64])
        yst = P.sb("yst", [64, NH, 128])
        bk = P.ps("bk", [128, 6, 512])
        J = Projector(P, nc, l, w_in, h_hi, h_lo, projT)

        def bank(i, w=128):
            return bk[:, i, 0:NH * w].rearrange("p (h t) -> p h t", h=NH)

        two12 = bk[:, 1:3, :].rearrange("p b (h u t) -> p (b h) u t", h=2, u=2)
        two45 = bk[:, 4:6, :].rearrange("p b (h u t) -> p (b h) u t", h=2, u=2)
        sems = ("c_in", "tok", "n_rdy", "mb", "mk", "tok_ev", "d_rdy", "ak_rdy", "p2_m", "p2t_m", "p2_a", "p2_d", "s3a", "s3d", "p4_a", "p4t_d", "x2_d", "s4a", "s4d", "p8_a", "x3_d",
                "s5", "x4", "s6a", "s6d", "x4_a", "y_d", "s7", "x5", "s8a", "s8d", "x5_a", "y2_d", "s9", "x6", "q_m", "q_a", "wz_m", "wz_d", "g_m", "g_d", "s_m", "s_d", "s2_m", "s2_d", "y_m", "y_a", "y_st", "y_ev", "i_ok")
        s = {n: P.sem(n) for n in sems}
        i_in, in_free = [P.sem(f"i_in{e}") for e in two], [P.sem(f"in_free{e}") for e in two]
        b_free = P.sem("b_free")
        block = ctx.enter_context(nc.Block())
        rh = rw.rearrange("(n h c) t -> n c h t", h=NH, c=64)
        assert R_RG + NT * 128 == DIN

        def tiles(eng, body):
            with eng.Fori(0, NT // 2) as i:
                for e in two:
                    body(i * 2 + e, i * 256 + (R_RG + e * 128), e)

        @block.sync
        def _(sp):
            sp.dma_start(ident[:], consts[:, 0:128]).then_inc(s["c_in"], 16)
            sp.dma_start(mk[:], masks.rearrange("p (k t) -> p k t", t=128)[:, 0:6, :]).then_inc(s["c_in"], 16)
            sp.dma_start(pe_all[:], pend.rearrange("(h c) n -> c h n", c=64)).then_inc(s["c_in"], 16)

            def load(t, e):
                sp.wait_ge(in_free[e], 1)
                sp.sem_inc(in_free[e], -1)
                cols = bass.ds(t * 128, 128)
                sp.dma_start(ar[e][:, :, 0, :], rh[0, :, :, cols]).then_inc(i_in[e], 16)
                sp.dma_start(ar[e][:, :, 1, :], rh[1, :, :, cols]).then_inc(i_in[e], 16)
                sp.wait_ge(b_free, 1)
                sp.sem_inc(b_free, -1)
                sp.dma_start(bt[:], rh[2, :, :, cols]).then_inc(i_in[e], 16)
                sp.dma_start(kt[:], rh[3, :, :, cols]).then_inc(i_in[e], 16)
                sp.dma_start(vt[:], rh[4, :, :, cols]).then_inc(i_in[e], 16)

            def store(t, row, e):
                for b in range(NB):
                    if b == NB - 1:
                        sp.wait_ge(s["y_a"], 1)
                        sp.sem_inc(s["y_a"], -1)
                        sp.dma_start(mixT[GW:2 * GW, bass.ds(t * 128, 128)].rearrange("(h c) t -> c h t", c=64), yst[:]).then_inc(s["y_st"], 16)
                    J.sp_store(sp, row, b)

            load(0, 0)
            with sp.Fori(0, NT // 2 - 1) as i:
                for e in two:
                    load(i * 2 + (1 + e), 1 - e)
                    store(i * 2 + e, i * 256 + (R_RG + e * 128), e)
            load(NT - 1, 1)
            for e in two:
                store(NT - 2 + e, DIN - 256 + 128 * e, e)
            sp.wait_ge(s["y_st"], 16)
            for q in two:
                sp.wait_ge(J.stage_st[q], 16)

        @block.gpsimd
        def _(pool):
            tiles(pool, lambda t, row, e: J.pool_weights(pool, e))

        @block.tensor
        def _(pe):
            pe.wait_ge(s["c_in"], 48)
            pe.wait_ge(s["i_ok"], 1)
            M, Tr = nc.tensor.matmul, nc.tensor.transpose

            def body(t, row, e):
                tile = J.pe_tile(pe, e)

                def fill(stage):
                    for _ in range(dict(SCAN_FILL)[stage]):
                        next(tile)

                a_, b_, k_, v_ = ar[e], bt, kt, vt
                pe.wait_ge(i_in[e], 80)
                pe.sem_inc(i_in[e], -80)
                for h in range(NH):
                    N_ = M(bank(0)[:, h, :], a_[:, h, 0, :], b_[:, h, :], start=True, stop=True)
                N_.then_inc(s["n_rdy"], 1)
                for h in range(NH):
                    N_ = M(two12[:, h], b_[:, h, :], a_[:, h], start=True, stop=True)
                N_.then_inc(s["mb"], 1)
                pe.wait_ge(s["y_ev"], 1)
                pe.sem_inc(s["y_ev"], -1)
                for h in range(NH):
                    Tr(bk[:, 3, h * 64:(h + 1) * 64], a_[:, h, 0, :], ident[0:64, 0:64])
                    Tr(bk[:, 3, 256 + h * 64:256 + (h + 1) * 64], b_[:, h, :], ident[0:64, 0:64])
                for h in range(NH):
                    Tr(bk[:, 4, h * 64:(h + 1) * 64], k_[:, h, :], ident[0:64, 0:64])
                    N_ = Tr(bk[:, 4, 256 + h * 64:256 + (h + 1) * 64], v_[:, h, :], ident[0:64, 0:64])
                N_.then_inc(s["tok"], 1)
                fill("tok")
                pe.wait_ge(s["d_rdy"], 1)
                pe.sem_inc(s["d_rdy"], -1)
                for h in range(NH):
                    N_ = M(bank(0)[:, h, :], Dt[:, h, :], D[:, h, :], start=True, stop=True)
                N_.then_inc(s["p2_m"], 1)
                pe.wait_ge(s["tok_ev"], 1)
                pe.sem_inc(s["tok_ev"], -1)
                for h in range(NH):
                    N_ = M(bank(3)[:, h, :], D[:, h, :], Dt[:, h, :], start=True, stop=True)
                N_.then_inc(s["p2t_m"], 1)
                pe.wait_ge(s["s2_d"], 1)
                pe.sem_inc(s["s2_d"], -1)
                for h in range(NH):
                    N_ = M(two45[:, h], k_[:, h, :], a_[:, h], start=True, stop=True)
                N_.then_inc(s["mk"], 1)
                fill("mk")
                pe.wait_ge(s["p2_a"], 1)
                pe.sem_inc(s["p2_a"], -1)
                pe.wait_ge(s["p2_d"], 1)
                pe.sem_inc(s["p2_d"], -1)
                for h in range(NH):
                    N_ = M(bank(0)[:, h, :], px[:, h, 0, :], p2[:, h, :], start=True, stop=True)
                N_.then_inc(s["s3a"], 1)
                for h in range(NH):
                    N_ = M(two12[:, h], p2[:, h, :], px[:, h], start=True, stop=True)
                N_.then_inc(s["s3d"], 1)
                fill("s3")
                pe.wait_ge(s["p4_a"], 1)
                pe.sem_inc(s["p4_a"], -1)
                pe.wait_ge(s["p4t_d"], 1)
                pe.sem_inc(s["p4t_d"], -1)
                for h in range(NH):
                    N_ = M(bank(3)[:, h, :], p4t[:, h, :], p4[:, h, :], start=True, stop=True)
                N_.then_inc(s["s4a"], 1)
                pe.wait_ge(s["x2_d"], 1)
                pe.sem_inc(s["x2_d"], -1)
                for h in range(NH):
                    N_ = M(bank(0)[:, h, :], p4[:, h, :], x1[:, h, :], start=True, stop=True)
                N_.then_inc(s["s4d"], 1)
                fill("s4")
                pe.wait_ge(s["ak_rdy"], 1)
                pe.sem_inc(s["ak_rdy"], -1)
                for h in range(NH):
                    N_ = M(bank(4, 64)[:, h, :], ak[:, h, 0, :], vm[:, h, :], start=True, stop=True)
                N_.then_inc(s["q_m"], 1)
                pe.wait_ge(s["p8_a"], 1)
                pe.sem_inc(s["p8_a"], -1)
                pe.wait_ge(s["x3_d"], 1)
                pe.sem_inc(s["x3_d"], -1)
                for h in range(NH):
                    N_ = M(bank(1)[:, h, :], p8[:, h, :], x1[:, h, :], start=True, stop=True)
                N_.then_inc(s["s5"], 1)
                fill("s5")
                for xr, sa, sd, xa, yd, E, sx, f1, f2 in (("x4", "s6a", "s6d", "x4_a", "y_d", E1, "s7", "s6", "s7"), ("x5", "s8a", "s8d", "x5_a", "y2_d", E2, "s9", "s8", "s9")):
                    pe.wait_ge(s[xr], 1)
                    pe.sem_inc(s[xr], -1)
                    for h in range(NH):
                        N_ = Tr(bank(2)[:, h, :], x1[:, h, :], ident[:])
                    N_.then_inc(s[sa], 1)
                    for h in range(NH):
                        N_ = M(bank(3)[:, h, :], E[:, h, :], x1[:, h, :], start=True, stop=True)
                    N_.then_inc(s[sd], 1)
                    fill(f1)
                    pe.wait_ge(s[xa], 1)
                    pe.sem_inc(s[xa], -1)
                    pe.wait_ge(s[yd], 1)
                    pe.sem_inc(s[yd], -1)
                    for h in range(NH):
                        N_ = M(bank(1)[:, h, :], xn[:, h, :], yy[:, h, :], start=True, stop=True)
                    N_.then_inc(s[sx], 1)
                    fill(f2)
                pe.wait_ge(s["x6"], 1)
                pe.sem_inc(s["x6"], -1)
                pe.wait_ge(s["q_a"], 1)
                pe.sem_inc(s["q_a"], -1)
                for h in range(NH):
                    N_ = M(bank(2)[:, h, :], x1[:, h, :], aq[:, h, :], start=True, stop=True)
                N_.then_inc(s["wz_m"], 1)
                fill("wz")
                pe.wait_ge(s["wz_d"], 1)
                pe.sem_inc(s["wz_d"], -1)
                for h in range(NH):
                    M(bk[0:64, 0, h * 128:(h + 1) * 128].rearrange("p (u t) -> p u t", u=2), wz[:, h, 0:64], bm[:, :, h, :], start=True, stop=True)
                for h in range(NH):
                    N_ = M(bk[0:64, 1, h * 128:(h + 1) * 128], wz[:, h, 0:64], arb[:, h, :], start=True, stop=True)
                N_.then_inc(s["g_m"], 1)
                fill("g")
                pe.wait_ge(s["g_d"], 1)
                pe.sem_inc(s["g_d"], -1)
                for h in range(NH):
                    o = bk[0:64, 5, h * 64:(h + 1) * 64]
                    M(o, bm[:, 0, h, :], wz[:, h, 64:128], start=True, stop=False)
                    M(o, km[:, 0, h, :], vm[:, h, :], start=False, stop=False)
                    N_ = M(o, gt[:, h, 0, :], S[:, 0, h, :], start=False, stop=True)
                N_.then_inc(s["s_m"], 1)
                fill("c0")
                pe.wait_ge(s["s_d"], 1)
                pe.sem_inc(s["s_d"], -1)
                for h in range(NH):
                    o = bk[0:64, 4, h * 128:(h + 1) * 128]
                    M(o, wz[:, h, 64:128], arb[:, h, :], start=True, stop=False)
                    M(o, vm[:, h, :], ak[:, h, 1, :], start=False, stop=False)
                    M(o[:, 0:64], S[:, 0, h, :], m1[:, h, 0:64], start=False, stop=False)
                    N_ = M(o[:, 64:128], S[:, 1, h, :], m1[:, h, 64:128], start=False, stop=True)
                N_.then_inc(s["y_m"], 1)
                for h in range(NH):
                    o = bk[0:64, 5, h * 64:(h + 1) * 64]
                    M(o, bm[:, 1, h, :], wz[:, h, 64:128], start=True, stop=False)
                    M(o, km[:, 1, h, :], vm[:, h, :], start=False, stop=False)
                    N_ = M(o, gt[:, h, 1, :], S[:, 1, h, :], start=False, stop=True)
                N_.then_inc(s["s2_m"], 1)
                fill("c1")
            tiles(pe, body)

        def mask(i):
            return mk[:, i:i + 1, :].to_broadcast([128, NH, 128])

        @block.vector
        def _(v):
            v.wait_ge(s["c_in"], 48)
            V = nc.vector
            V.memset(S[:], 0.0)
            V.memset(bm[:], 0.0)
            V.memset(km[:], 0.0)
            v.drain().then_inc(s["s2_d"], 1)
            for e in two:
                v.sem_inc(in_free[e], 1)
            v.sem_inc(b_free, 1)
            v.drain().then_inc(s["i_ok"], 2)

            def body(t, row, e):
                v.wait_ge(s["n_rdy"], 1)
                v.sem_inc(s["n_rdy"], -1)
                V.tensor_tensor(D[:], bank(0), mask(0), ALU.mult)
                v.wait_ge(s["mb"], 1)
                v.sem_inc(s["mb"], -1)
                V.tensor_tensor(Dt[:], two12[:, :, 0, :], mask(3), ALU.mult)
                V.tensor_tensor(E1[:], bank(0), mask(1), ALU.mult)
                V.tensor_tensor(E2[:], bank(0), mask(2), ALU.mult).then_inc(s["d_rdy"], 1)
                v.drain()
                V.tensor_tensor(px[:, :, 1, :], Dt[:], ident[:].rearrange("p (o t) -> p o t", o=1).to_broadcast([128, NH, 128]), ALU.add)
                V.tensor_tensor(arb[:], two12[:, :, 1, :], mask(5), ALU.mult)
                v.wait_ge(s["p2t_m"], 1)
                v.sem_inc(s["p2t_m"], -1)
                V.tensor_copy(px[:, :, 0, :], bank(3)).then_inc(s["p2_d"], 1)
                v.wait_ge(s["mk"], 1)
                v.sem_inc(s["mk"], -1)
                V.tensor_tensor(ak[:, :, 0, :], two45[:, :, 0, :], mask(4), ALU.mult).then_inc(b_free, 1)
                v.wait_ge(s["s3d"], 1)
                v.sem_inc(s["s3d"], -1)
                V.tensor_copy(p4t[:], two12[:, :, 0, :]).then_inc(s["p4t_d"], 1)
                V.tensor_tensor(x1[:], two12[:, :, 1, :], px[:, :, 1, :], ALU.add).then_inc(s["x2_d"], 1)
                V.tensor_tensor(ak[:, :, 1, :], two45[:, :, 1, :], mask(5), ALU.mult).then_inc(s["ak_rdy"], 1)
                v.drain()
                for m, b_, r in (("s4d", 0, "x3_d"), ("s5", 1, "x4")):
                    v.wait_ge(s[m], 1)
                    v.sem_inc(s[m], -1)
                    V.tensor_tensor(x1[:], bank(b_), x1[:], ALU.add)
                    v.drain().then_inc(s[r], 1)
                for sd, yd, sx, r in (("s6d", "y_d", "s7", "x5"), ("s8d", "y2_d", "s9", "x6")):
                    v.wait_ge(s[sd], 1)
                    v.sem_inc(s[sd], -1)
                    V.tensor_copy(yy[:], bank(3)).then_inc(s[yd], 1)
                    v.wait_ge(s[sx], 1)
                    v.sem_inc(s[sx], -1)
                    V.tensor_tensor(x1[:], bank(1), x1[:], ALU.add)
                    v.drain().then_inc(s[r], 1)
                v.wait_ge(s["wz_m"], 1)
                v.sem_inc(s["wz_m"], -1)
                V.tensor_copy(wz[:], bank(2)).then_inc(s["wz_d"], 1)
                v.wait_ge(s["g_m"], 1)
                v.sem_inc(s["g_m"], -1)
                V.tensor_tensor(gt.rearrange("p h u t -> p (h u) t"), bk[0:64, 0, :].rearrange("p (h t) -> p h t", t=64),
                                ident[0:64, 0:64].rearrange("p (o t) -> p o t", o=1).to_broadcast([64, 2 * NH, 64]), ALU.add)
                V.tensor_tensor(m1, bk[0:64, 1, :].rearrange("p (h t) -> p h t", h=NH), ar[e][:, :, 1, :], ALU.add).then_inc(s["g_d"], 1)
                v.drain().then_inc(in_free[e], 1)
                for c, m in ((0, "s_m"), (1, "s2_m")):
                    v.wait_ge(s[m], 1)
                    v.sem_inc(s[m], -1)
                    V.tensor_tensor(S[:, 1 - c], bk[0:64, 5, 0:NH * 64].rearrange("p (h t) -> p h t", h=NH),
                                    pe_all[:, :, bass.ds(t * 2 + c, 1)].to_broadcast([64, NH, 64]), ALU.mult)
                    v.drain().then_inc(s["s_d" if c == 0 else "s2_d"], 1)
            tiles(v, body)

        @block.scalar
        def _(act):
            J.act_start(act)
            act.wait_ge(s["i_ok"], 2)
            act.sem_inc(s["y_st"], 16)
            act.sem_inc(s["y_ev"], 1)
            C = nc.scalar.copy

            def evac(stage):
                for b in units_done(SCAN_FILL, stage):
                    J.evacuate(act, C, b)

            def body(t, nxt, e):
                if nxt is not None:
                    J.act_load(act, nxt)
                act.wait_ge(s["tok"], 1)
                act.sem_inc(s["tok"], -1)
                b3 = bk[:, 3, :].rearrange("p (u h c) -> p u h c", u=2, h=NH)
                b4 = bk[:, 4, :].rearrange("p (u h c) -> p u h c", u=2, h=NH)
                C(aq[:, :, 0:64], b3[:, 0])
                for c in two:
                    C(bm[64 * c:64 * c + 64, c], b3[64 * c:64 * c + 64, 1])
                    C(km[64 * c:64 * c + 64, c], b4[64 * c:64 * c + 64, 0])
                C(vm[:], b4[:, 1])
                act.drain().then_inc(s["tok_ev"], 1)
                evac("tok")
                act.wait_ge(s["p2_m"], 1)
                act.sem_inc(s["p2_m"], -1)
                C(p2[:], bank(0)).then_inc(s["p2_a"], 1)
                evac("mk")
                act.wait_ge(s["s3a"], 1)
                act.sem_inc(s["s3a"], -1)
                C(p4[:], bank(0)).then_inc(s["p4_a"], 1)
                evac("s3")
                act.wait_ge(s["s4a"], 1)
                act.sem_inc(s["s4a"], -1)
                C(p8[:], bank(3)).then_inc(s["p8_a"], 1)
                evac("s4")
                act.wait_ge(s["q_m"], 1)
                act.sem_inc(s["q_m"], -1)
                C(aq[:, :, 64:128], bank(4, 64)).then_inc(s["q_a"], 1)
                evac("s5")
                if nxt is not None:
                    J.act_split(act, 1 - e)
                for sa, xa, f1, f2 in (("s6a", "x4_a", "s6", "s7"), ("s8a", "x5_a", "s8", "s9")):
                    act.wait_ge(s[sa], 1)
                    act.sem_inc(s[sa], -1)
                    C(xn[:], bank(2)).then_inc(s[xa], 1)
                    evac(f1)
                    evac(f2)
                evac("wz")
                evac("g")
                evac("c0")
                act.wait_ge(s["y_m"], 1)
                act.sem_inc(s["y_m"], -1)
                act.wait_ge(s["y_st"], 16)
                act.sem_inc(s["y_st"], -16)
                C(yst[:], bk[0:64, 4, :].rearrange("p (h t) -> p h t", h=NH)).then_inc(s["y_a"], 1)
                act.drain().then_inc(s["y_ev"], 1)
                evac("c1")

            J.act_load(act, R_RG)
            J.act_split(act, 0)
            with act.Fori(0, NT // 2 - 1) as i:
                for e in two:
                    body(i * 2 + e, i * 256 + (R_RG + (1 + e) * 128), e)
            body(NT - 2, DIN - 128, 0)
            body(NT - 1, None, 1)


def phase_head_norm(nc, l, projT, par, consts, rope, fa):
    with ExitStack() as ctx:
        P = Phase(nc, ctx, "hn")
        tiles = [(r * 128, False) for r in range(4)] + [(R_SQ + r * 128, True) for r in range(3)]
        NX, NR = len(tiles), 2 * len(tiles)
        steps = [(4, False), (0, False), (4, True), (5, False), (1, False), (5, True), (6, False), (2, False), (6, True), (3, False)]
        stores = [j for j, turn in steps if turn or not tiles[j][1]]
        pars, gsc = P.sb("pars", [128, NPAR]), P.sb("gsc", [128, NX])
        gather, spread = P.sb("gather", [128, NX, NR]), P.sb("spread", [NR, NX, 128])
        perm = P.sb("perm", [128, 128])
        cs = P.sb("cs", [128, 2, T])
        x = [P.sb(f"x{j}", [128, T]) for j in range(NX)]
        sq = [P.sb(f"sq{q}", [128, T]) for q in range(2)]
        rs, sw = P.sb("rs", [NR, T]), P.sb("sw", [128, T])
        f, g, one, F4 = P.sb("f", [4, T]), P.sb("g", [4, T]), P.sb("one", [4, T]), P.sb("F4", [4, 4, T])
        bk = [P.ps(f"bk{q}", [128, T]) for q in range(2)]
        names = ("c_in", "rope_in", "f_in", "z_rdy", "e_rdy", "F_rdy", "F_st", "ss_rdy", "v_rdy", "r_rdy", "bk_rdy", "bk_free", "o_rdy", "st")
        s = {n: P.sem(n) for n in names}
        x_in = [P.sem(f"x_in{j}") for j in range(NX)]
        sq_rdy, sq_free = ([P.sem(f"{n}{q}") for q in range(2)] for n in ("sq_rdy", "sq_free"))
        block = ctx.enter_context(nc.Block())

        @block.sync
        def _(sp):
            sp.dma_start(f[:], projT[R_FF:R_FF + 4, PAD:PAD + T]).then_inc(s["f_in"], 16)
            sp.dma_start(pars[:], lay(par, l)).then_inc(s["c_in"], 16)
            sp.dma_start(gather[:], consts[:, C_GATHER:C_SPREAD].rearrange("p (j r) -> p j r", j=NX)).then_inc(s["c_in"], 16)
            sp.dma_start(spread[:], consts[0:NR, C_SPREAD:NCONST].rearrange("p (j c) -> p j c", j=NX)).then_inc(s["c_in"], 16)
            sp.dma_start(perm[:], consts[:, 896:1024]).then_inc(s["c_in"], 16)
            for j, (row, rot) in enumerate(tiles):
                sp.dma_start(x[j][:], projT[row:row + 128, PAD:PAD + T]).then_inc(x_in[j], 16)
            sp.dma_start(cs[:], rope.rearrange("p (k t) -> p k t", k=2)).then_inc(s["rope_in"], 16)
            sp.wait_ge(s["F_rdy"], 1)
            sp.sem_inc(s["F_rdy"], -1)
            sp.dma_start(fa.rearrange("(h k) t -> h k t", k=4), F4[:]).then_inc(s["F_st"], 16)
            for j in stores:
                sp.wait_ge(s["o_rdy"], 1)
                sp.sem_inc(s["o_rdy"], -1)
                sp.dma_start(projT[tiles[j][0]:tiles[j][0] + 128, PAD:PAD + T], x[j][:]).then_inc(s["st"], 16)
            sp.wait_ge(s["st"], 16 * NX)
            sp.wait_ge(s["F_st"], 16)

        @block.scalar
        def _(act):
            A = nc.scalar.activation
            for j in range(NX):
                act.wait_ge(x_in[j], 16)
                act.sem_inc(x_in[j], -16)
                act.wait_ge(sq_free[j % 2], 1)
                act.sem_inc(sq_free[j % 2], -1)
                A(sq[j % 2][:], x[j][:], ACT.Square).then_inc(sq_rdy[j % 2], 1)
                if j == 1:
                    act.wait_ge(s["z_rdy"], 1)
                    act.sem_inc(s["z_rdy"], -1)
                    A(g[:], g[:], ACT.Exp, scale=-1.0)
                    act.drain()
                    A(g[:], g[:], ACT.Ln, bias=1.0).then_inc(s["e_rdy"], 1)
            act.wait_ge(s["v_rdy"], 1)
            act.sem_inc(s["v_rdy"], -1)
            A(rs[:], rs[:], ACT.Ln)
            act.drain()
            A(rs[:], rs[:], ACT.Exp, scale=-0.5).then_inc(s["r_rdy"], 1)

        @block.tensor
        def _(pe):
            M = nc.tensor.matmul
            for q in range(2):
                pe.sem_inc(sq_free[q], 1)
            pe.wait_ge(s["c_in"], 64)
            for j in range(NX):
                pe.wait_ge(sq_rdy[j % 2], 1)
                pe.sem_inc(sq_rdy[j % 2], -1)
                for c in range(0, T, TB):
                    ins = M(bk[0][0:NR, c:c + TB], gather[:, j, :], sq[j % 2][:, c:c + TB], start=(j == 0), stop=(j == NX - 1))
                ins.then_inc(sq_free[j % 2], 1)
            pe.drain().then_inc(s["ss_rdy"], 1)
            pe.wait_ge(s["r_rdy"], 1)
            pe.sem_inc(s["r_rdy"], -1)
            for n, (j, turn) in enumerate(steps):
                pe.wait_ge(s["bk_free"], 1)
                pe.sem_inc(s["bk_free"], -1)
                for c in range(0, T, TB):
                    if turn:
                        ins = M(bk[n % 2][:, c:c + TB], perm[:], x[j][:, c:c + TB], start=True, stop=True)
                    else:
                        ins = M(bk[n % 2][:, c:c + TB], spread[:, j, :], rs[:, c:c + TB], start=True, stop=True)
                ins.then_inc(s["bk_rdy"], 1)

        @block.vector
        def _(v):
            V = nc.vector
            v.wait_ge(s["f_in"], 16)
            v.sem_inc(s["f_in"], -16)
            v.wait_ge(s["c_in"], 64)
            V.tensor_scalar(f[:], f[:], pars[0:4, C_BF:C_BF + 1], None, ALU.add)
            v.drain()
            V.scalar_tensor_tensor(g[:], f[:], -1.0, f[:], ALU.mult, ALU.max).then_inc(s["z_rdy"], 1)
            V.tensor_copy(gsc[:], pars[:, C_GN:C_GN + 7])
            v.drain()
            for c in (0, 4):
                V.tensor_scalar(gsc[:, c:c + 2], gsc[:, c:c + 2], HD ** -0.5, None, ALU.mult)
            V.memset(one[:], 1.0)
            V.memset(F4[:, 1:3, :], 1.0)
            v.wait_ge(s["e_rdy"], 1)
            v.sem_inc(s["e_rdy"], -1)
            V.scalar_tensor_tensor(f[:], f[:], 0.0, g[:], ALU.min, ALU.subtract)
            v.drain()
            V.tensor_tensor_scan(F4[:, 0, :], one[:], f[:], 0.0, ALU.mult, ALU.add)
            v.drain()
            V.tensor_scalar(F4[:, 3, :], F4[:, 0, :], -1.0, None, ALU.mult).then_inc(s["F_rdy"], 1)
            v.wait_ge(s["ss_rdy"], 1)
            v.sem_inc(s["ss_rdy"], -1)
            V.tensor_scalar(rs[:], bk[0][0:NR, :], 1.0 / HD, EPS, ALU.mult, ALU.add).then_inc(s["v_rdy"], 1)
            v.drain().then_inc(s["bk_free"], 2)
            for n, (j, turn) in enumerate(steps):
                v.wait_ge(s["bk_rdy"], 1)
                v.sem_inc(s["bk_rdy"], -1)
                if turn:
                    if j == 4:
                        v.wait_ge(s["rope_in"], 16)
                        v.sem_inc(s["rope_in"], -16)
                    v.drain()
                    V.tensor_tensor(sw[:], bk[n % 2][:], cs[:, 1, :], ALU.mult).then_inc(s["bk_free"], 1)
                    V.tensor_tensor(x[j][:], x[j][:], cs[:, 0, :], ALU.mult)
                    v.drain()
                    V.tensor_tensor(x[j][:], x[j][:], sw[:], ALU.add).then_inc(s["o_rdy"], 1)
                else:
                    V.scalar_tensor_tensor(x[j][:], x[j][:], gsc[:, j:j + 1], bk[n % 2][:], ALU.mult, ALU.mult).then_inc(s["bk_free"], 1)
                    if not tiles[j][1]:
                        v.drain().then_inc(s["o_rdy"], 1)


def phase_fox(nc, l, projT, fa, consts, mixT):
    with ExitStack() as ctx:
        P = Phase(nc, ctx, "fx")
        ident, cm = P.sb("ident", [128, 128]), P.sb("cm", [128, 128])
        identb, cmb = P.sb("identb", [128, 128], BF16), P.sb("cmb", [128, 128], BF16)
        two = range(2)
        q2, k2 = ([P.sb(f"{n}{e}", [66, T]) for e in two] for n in ("qs", "ks"))
        v2 = [P.sb(f"vc{e}", [64, T]) for e in two]
        vs = P.sb("vs", [128, NT, 2 * HD])
        UK = 8
        prob = [P.sb(f"prob{q}", [128, UK * 128]) for q in range(3)]
        pts = [P.sb(f"pts{q}", [128, UK, 128]) for q in range(2)]
        nm, nr = P.sb("nm", [128, 4, 2]), P.sb("nr", [128, 4])
        lr = P.sb("lr", [64, 128])
        yo = P.sb("yo", [64, T])
        S = P.ps("S", [128, 2, UK * 128])
        pt = [P.ps(f"pt{q}", [128, 4, 128]) for q in range(2)]
        O = P.ps("O", [128, 2, 512])
        names = ("c_in", "cb_rdy", "v_tr", "v_ev", "s_rdy", "m_rdy", "o_rdy", "o_free", "yo_rdy", "yo_st")
        s = {n: P.sem(n) for n in names}
        pt_rdy = [P.sem(f"pt_rdy{q}") for q in range(2)]
        pt_ev = [P.sem(f"pt_ev{q}") for q in range(2)]
        h_in, in_free = ([P.sem(f"{n}{e}") for e in two] for n in ("h_in", "in_free"))
        p_rdy = P.sem("p_rdy")
        block = ctx.enter_context(nc.Block())

        units = []
        for t in range(NT):
            parts = [(0, t + 1)] if t < UK else [(0, UK), (UK, t + 1)]
            units += [(t, p, a, b, p == len(parts) - 1) for p, (a, b) in enumerate(parts)]
        NU = len(units)
        assert NU % 6 == 0

        def groups(u):
            t, p, a, b, last = units[u]
            return [(g, a + 4 * g, min(a + 4 * g + 4, b)) for g in range((b - a + 3) // 4)]

        @block.sync
        def _(sp):
            sp.dma_start(ident[:], consts[:, 0:128]).then_inc(s["c_in"], 16)
            sp.dma_start(cm[:], consts[:, 1024:1152]).then_inc(s["c_in"], 16)

            def load(h, e):
                sp.wait_ge(in_free[e], 1)
                sp.sem_inc(in_free[e], -1)
                tok = slice(PAD, PAD + T)
                sp.dma_start(v2[e][:], projT[bass.ds(h * HD + R_FV, HD), tok]).then_inc(h_in[e], 16)
                sp.dma_start(q2[e][0:64, :], projT[bass.ds(h * HD, HD), tok]).then_inc(h_in[e], 16)
                sp.dma_start(k2[e][0:64, :], projT[bass.ds(h * HD + R_FK, HD), tok]).then_inc(h_in[e], 16)
                sp.dma_start(q2[e][64:66, :], fa[bass.ds(h * 4, 2), :]).then_inc(h_in[e], 16)
                sp.dma_start(k2[e][64:66, :], fa[bass.ds(h * 4 + 2, 2), :]).then_inc(h_in[e], 16)

            def store(h):
                sp.wait_ge(s["yo_rdy"], 1)
                sp.sem_inc(s["yo_rdy"], -1)
                sp.dma_start(mixT[bass.ds(h * HD, HD), :], yo[:]).then_inc(s["yo_st"], 16)

            load(0, 0)
            with sp.Fori(0, NH // 2 - 1) as i:
                for e in two:
                    load(i * 2 + (1 + e), 1 - e)
                    store(i * 2 + e)
            load(NH - 1, 1)
            store(NH - 2)
            store(NH - 1)
            sp.wait_ge(s["yo_st"], 16)

        @block.tensor
        def _(pe):
            M, Tr = nc.tensor.matmul, nc.tensor.transpose
            pe.wait_ge(s["c_in"], 32)
            pe.wait_ge(s["cb_rdy"], 1)

            def qk(u, qs, ks):
                t, p, a, b, last = units[u]
                n = (b - a) * 128
                for c in range(0, n, 512):
                    w = min(512, n - c)
                    ins = M(S[:, u % 2, c:c + w], qs[:, t * 128:(t + 1) * 128], ks[:, a * 128 + c:a * 128 + c + w], start=True, stop=(c + w < n or not last))
                if last:
                    ins = M(S[:, u % 2, n - 128:n], identb[:], cmb[:], start=False, stop=True)
                ins.then_inc(s["s_rdy"], 1)

            def transpose_p(u):
                for g, j0, j1 in groups(u):
                    a = units[u][2]
                    for j in range(j0, j1):
                        ins = Tr(pt[g][:, j - j0, :], prob[u % 3][:, (j - a) * 128:(j - a + 1) * 128], ident[:])
                    ins.then_inc(pt_rdy[g], 1)

            def pv(u):
                t, p, a, b, last = units[u]
                if p == 0:
                    pe.wait_ge(s["o_free"], 1)
                    pe.sem_inc(s["o_free"], -1)
                for j in range(a, b):
                    ins = M(O[:, t % 2, 0:128], vs[:, j, :], pts[u % 2][:, j - a, :], start=(j == 0), stop=(j == t))
                if last:
                    ins.then_inc(s["o_rdy"], 1)

            def head(qs, ks, vc, h_in):
                pe.wait_ge(h_in, 80)
                pe.sem_inc(h_in, -80)
                for j in range(NT):
                    ins = Tr(S[:, 0, j * HD:(j + 1) * HD], vc[:, j * 128:(j + 1) * 128], ident[0:64, 0:64])
                ins.then_inc(s["v_tr"], 1)
                pe.wait_ge(s["v_ev"], 1)
                pe.sem_inc(s["v_ev"], -1)
                qk(0, qs, ks)
                qk(1, qs, ks)
                for u in range(NU):
                    pe.wait_ge(p_rdy, 1)
                    pe.sem_inc(p_rdy, -1)
                    if u + 2 < NU:
                        qk(u + 2, qs, ks)
                    if u > 0:
                        for g, j0, j1 in groups(u - 1):
                            pe.wait_ge(pt_ev[g], 1)
                            pe.sem_inc(pt_ev[g], -1)
                    transpose_p(u)
                    if u > 0:
                        pv(u - 1)
                for g, j0, j1 in groups(NU - 1):
                    pe.wait_ge(pt_ev[g], 1)
                    pe.sem_inc(pt_ev[g], -1)
                pv(NU - 1)

            with pe.Fori(0, NH // 2) as i:
                for e in two:
                    head(q2[e], k2[e], v2[e], h_in[e])

        @block.vector
        def _(v):
            V = nc.vector
            v.wait_ge(s["c_in"], 32)
            V.tensor_copy(identb[:], ident[:])
            V.tensor_copy(cmb[:], cm[:])
            v.drain().then_inc(s["cb_rdy"], 1)
            for e in two:
                v.sem_inc(in_free[e], 1)
            v.sem_inc(s["o_free"], 2)
            v.sem_inc(s["yo_st"], 16)
            V.memset(vs[:, :, HD:2 * HD], 1.0)
            v.drain()

            def row_max(u):
                t, p, a, b, last = units[u]
                v.wait_ge(s["s_rdy"], 1)
                v.sem_inc(s["s_rdy"], -1)
                ins = V.tensor_reduce(nm[:, t % 4, p:p + 1], S[:, u % 2, 0:(b - a) * 128], AX.X, ALU.max, negate=True)
                if p == 1:
                    v.drain()
                    ins = V.tensor_tensor(nr[:, t % 4:t % 4 + 1], nm[:, t % 4, 0:1], nm[:, t % 4, 1:2], ALU.min)
                if last:
                    ins.then_inc(s["m_rdy"], 1)

            def out_row(t):
                if t == 0:
                    v.wait_ge(s["yo_st"], 16)
                    v.sem_inc(s["yo_st"], -16)
                v.wait_ge(s["o_rdy"], 1)
                v.sem_inc(s["o_rdy"], -1)
                v.drain()
                V.reciprocal(lr[:], O[64:128, t % 2, 0:128])
                v.drain()
                V.tensor_tensor(yo[:, t * 128:(t + 1) * 128], O[0:64, t % 2, 0:128], lr[:], ALU.mult).then_inc(s["o_free"], 1)

            def head(e):
                v.wait_ge(s["v_tr"], 1)
                v.sem_inc(s["v_tr"], -1)
                V.tensor_copy(vs[:, :, 0:HD], S[:, 0, 0:NT * HD].rearrange("p (j c) -> p j c", j=NT)).then_inc(s["v_ev"], 1)
                row_max(0)
                row_max(1)
                for u in range(NU):
                    if u + 2 < NU:
                        row_max(u + 2)
                    g, j0, j1 = groups(u)[0]
                    v.wait_ge(pt_rdy[g], 1)
                    v.sem_inc(pt_rdy[g], -1)
                    V.tensor_copy(pts[u % 2][:, 0:j1 - j0, :], pt[g][:, 0:j1 - j0, :]).then_inc(pt_ev[g], 1)
                    if u > 0 and units[u - 1][4]:
                        out_row(units[u - 1][0])
                out_row(NT - 1)
                v.drain().then_inc(s["yo_rdy"], 1)
                v.drain().then_inc(in_free[e], 1)

            with v.Fori(0, NH // 2) as i:
                for e in two:
                    head(e)

        @block.scalar
        def _(act):
            A = nc.scalar.activation

            def exps(u):
                t, p, a, b, last = units[u]
                if p == 0:
                    act.wait_ge(s["m_rdy"], 1)
                    act.sem_inc(s["m_rdy"], -1)
                n = (b - a) * 128
                A(prob[u % 3][:, 0:n], S[:, u % 2, 0:n], ACT.Exp, bias=nm[:, t % 4, 0:1] if t < UK else nr[:, t % 4:t % 4 + 1]).then_inc(p_rdy, 1)

            def head():
                exps(0)
                for u in range(NU):
                    if u + 1 < NU:
                        exps(u + 1)
                    for g, j0, j1 in groups(u)[1:]:
                        act.wait_ge(pt_rdy[g], 1)
                        act.sem_inc(pt_rdy[g], -1)
                        nc.scalar.copy(pts[u % 2][:, 4 * g:4 * g + j1 - j0, :], pt[g][:, 0:j1 - j0, :]).then_inc(pt_ev[g], 1)

            with act.Fori(0, NH) as h:
                head()


def phase_swa(nc, l, projT, par, consts, masks, mixT, w_out, wo_hi, wo_lo):
    with ExitStack() as ctx:
        P = Phase(nc, ctx, "sw")
        KW = 192
        ident, pars = P.sb("ident", [128, 128]), P.sb("pars", [128, NPAR])
        mks = P.sb("mks", [128, 2, KW])
        cur = P.sb("cur", [128, KW])
        two = range(2)
        q, k, vc = ([P.sb(f"{n}{e}", [64, w, c]) for e in two] for n, w, c in (("q", NH, 128), ("k", 2, KW), ("vc", 2, KW)))
        va, vb = [P.sb(f"va{e}", [128, 2, HD]) for e in two], [P.sb(f"vb{e}", [64, 2, HD]) for e in two]
        sc, pb = ([P.sb(f"{n}{e}", [128, NH, KW]) for e in two] for n in ("sc", "pb"))
        mx, nm, es, ls = ([P.sb(f"{n}{e}", [128, NH]) for e in two] for n in ("mx", "nm", "es", "ls"))
        pa_t, pb_t = P.sb("pa_t", [128, NH, 128]), P.sb("pb_t", [64, NH, 128])
        on, yo = [P.sb(f"on{e}", [128, NH * HD]) for e in two], [P.sb(f"yo{e}", [128, 2, 128]) for e in two]
        raw = [P.sb(f"raw{e}", [128, TB]) for e in two]
        S = P.ps("S", [128, 2, 512])
        TA, TB_, O, V_, OT = P.ps("TA", [128, 512]), P.ps("TB", [64, 512]), P.ps("O", [128, 512]), P.ps("V", [128, 512]), P.ps("OT", [128, 512])
        names = ("c_in", "s_rdy", "s_free", "v_tr", "v_ev", "m_rdy", "p_rdy", "t_rdy", "tt_rdy", "ta_d", "tb_a", "o_rdy", "on_rdy", "ot_rdy", "ot_free")
        s = {n: P.sem(n) for n in names}
        s_in, in_free, yo_rdy, yo_st, raw_in, raw_free = ([P.sem(f"{n}{e}") for e in two] for n in ("in", "in_free", "yo_rdy", "yo_st", "raw_in", "raw_free"))
        block = ctx.enter_context(nc.Block())

        assert KC == NT // 2

        def loop(eng, first, body):
            first()
            body(0, 0, True, before=False)
            body(1, 1, True)
            with eng.Fori(1, NT // 2 - 1) as i:
                body(i * 2, 0, True)
                body(i * 2 + 1, 1, True)
            body(NT - 2, 0, True)
            body(NT - 1, 1, False)

        @block.sync
        def _(sp):
            sp.dma_start(ident[:], consts[:, 0:128]).then_inc(s["c_in"], 16)
            sp.dma_start(pars[:], lay(par, l)).then_inc(s["c_in"], 16)
            sp.dma_start(mks[:], masks[:, 768:768 + 2 * KW].rearrange("p (k t) -> p k t", k=2)).then_inc(s["c_in"], 16)

            def load(t, e):
                sp.wait_ge(in_free[e], 1)
                sp.sem_inc(in_free[e], -1)
                sp.dma_start(q[e][:], projT[R_SQ:R_SQ + GW, bass.ds(t * 128 + PAD, 128)].rearrange("(h c) t -> c h t", c=64)).then_inc(s_in[e], 16)
                sp.dma_start(k[e][:], projT[R_SK:R_SK + 128, bass.ds(t * 128 + (PAD - CH), KW)].rearrange("(h c) t -> c h t", c=64)).then_inc(s_in[e], 16)
                sp.dma_start(vc[e][:], projT[R_SV:R_SV + 128, bass.ds(t * 128 + (PAD - CH), KW)].rearrange("(h c) t -> c h t", c=64)).then_inc(s_in[e], 16)

            def store(t, e):
                sp.wait_ge(yo_rdy[e], 1)
                sp.sem_inc(yo_rdy[e], -1)
                sp.dma_start(mixT[2 * GW:3 * GW, bass.ds(t * 128, 128)].rearrange("(k p) t -> p k t", p=128), yo[e][:]).then_inc(yo_st[e], 16)

            def weights(k, q):
                sp.wait_ge(raw_free[q], 1)
                sp.sem_inc(raw_free[q], -1)
                sp.dma_start(raw[q][:], lay(w_out, l)[bass.ds(k * 128, 128), q * TB:(q + 1) * TB]).then_inc(raw_in[q], 16)

            load(0, 0)
            load(1, 1)
            with sp.Fori(0, NT // 2 - 1) as i:
                for e in two:
                    load(i * 2 + (2 + e), e)
                    weights(i, e)
                    store(i * 2 + e, e)
            for e in two:
                weights(KC - 1, e)
                store(NT - 2 + e, e)
            for e in two:
                sp.wait_ge(yo_st[e], 16)

        @block.gpsimd
        def _(pool):
            for q in two:
                pool.sem_inc(raw_free[q], 1)
            with pool.Fori(0, KC) as k:
                for q in two:
                    hi, lo = (w[:, bass.ds(k, 1), q * TB:(q + 1) * TB].rearrange("p a n -> p (a n)") for w in (wo_hi, wo_lo))
                    pool.wait_ge(raw_in[q], 16)
                    pool.sem_inc(raw_in[q], -16)
                    nc.gpsimd.tensor_copy(hi, raw[q][:])
                    pool.drain()
                    nc.gpsimd.tensor_tensor(lo, raw[q][:], hi.bitcast(F32), ALU.subtract).then_inc(raw_free[q], 1)

        @block.tensor
        def _(pe):
            M, Tr = nc.tensor.matmul, nc.tensor.transpose
            pe.wait_ge(s["c_in"], 48)

            def scores(e, first=False):
                pe.wait_ge(s_in[e], 48)
                pe.sem_inc(s_in[e], -48)
                pe.wait_ge(s["s_free"], 1)
                pe.sem_inc(s["s_free"], -1)
                for h in range(NH):
                    ins = M(S[:, h // 2, (h % 2) * KW:(h % 2 + 1) * KW], q[e][:, h, :], k[e][:, h // 2, :], start=True, stop=True)
                ins.then_inc(s["s_rdy"], 1)
                if not first:
                    pe.wait_ge(s["v_ev"], 1)
                    pe.sem_inc(s["v_ev"], -1)
                for g in two:
                    Tr(V_[:, g * HD:(g + 1) * HD], vc[e][:, g, 0:128], ident[0:64, 0:64])
                for g in two:
                    ins = Tr(V_[0:64, 128 + g * HD:128 + (g + 1) * HD], vc[e][:, g, 128:KW], ident[0:64, 0:64])
                ins.then_inc(s["v_tr"], 1)

            def out_t(e):
                pe.wait_ge(s["on_rdy"], 1)
                pe.sem_inc(s["on_rdy"], -1)
                pe.wait_ge(s["ot_free"], 1)
                pe.sem_inc(s["ot_free"], -1)
                for p in two:
                    ins = Tr(OT[:, p * 128:(p + 1) * 128], on[e][:, p * 128:(p + 1) * 128], ident[:])
                ins.then_inc(s["ot_rdy"], 1)

            def body(t, e, nxt, before=True):
                pe.wait_ge(s["p_rdy"], 1)
                pe.sem_inc(s["p_rdy"], -1)
                for h in range(NH):
                    ins = Tr(TA[:, h * 128:(h + 1) * 128], pb[e][:, h, 0:128], ident[:])
                ins.then_inc(s["t_rdy"], 1)
                for h in range(NH):
                    ins = Tr(TB_[:, h * 128:(h + 1) * 128], pb[e][:, h, 128:KW], ident[:])
                ins.then_inc(s["tt_rdy"], 1)
                if nxt:
                    scores(1 - e)
                else:
                    pe.wait_ge(s["v_ev"], 1)
                    pe.sem_inc(s["v_ev"], -1)
                if before:
                    out_t(1 - e)
                pe.wait_ge(s["ta_d"], 1)
                pe.sem_inc(s["ta_d"], -1)
                pe.wait_ge(s["tb_a"], 1)
                pe.sem_inc(s["tb_a"], -1)
                for h in range(NH):
                    M(O[:, h * HD:(h + 1) * HD], pa_t[:, h, :], va[e][:, h // 2, :], start=True, stop=False)
                    ins = M(O[:, h * HD:(h + 1) * HD], pb_t[:, h, :], vb[e][:, h // 2, :], start=False, stop=True)
                ins.then_inc(s["o_rdy"], 1)
            loop(pe, lambda: scores(0, True), body)
            out_t(1)

        @block.vector
        def _(v):
            V = nc.vector
            v.wait_ge(s["c_in"], 48)
            V.tensor_copy(cur[:], mks[:, 0, :])
            for e in two:
                v.sem_inc(in_free[e], 1)
            v.sem_inc(s["s_free"], 1)
            v.drain()
            sink = pars[:, C_SINK:C_SINK + NH]

            def maxima(e):
                v.wait_ge(s["s_rdy"], 1)
                v.sem_inc(s["s_rdy"], -1)
                V.tensor_tensor(sc[e][:].rearrange("p (b h) k -> p b h k", b=2), S[:, :, 0:2 * KW].rearrange("p b (h k) -> p b h k", h=2),
                                cur[:].rearrange("p (a b k) -> p a b k", a=1, b=1).to_broadcast([128, 2, 2, KW]), ALU.add)
                v.drain().then_inc(s["s_free"], 1)
                V.tensor_copy(cur[:], mks[:, 1, :])
                V.tensor_reduce(mx[e][:], sc[e][:], AX.X, ALU.max)
                v.drain()
                V.tensor_tensor(mx[e][:], mx[e][:], sink, ALU.max)
                v.drain()
                V.tensor_scalar(nm[e][:], mx[e][:], -1.0, None, ALU.mult)
                V.tensor_tensor(es[e][:], sink, mx[e][:], ALU.subtract)
                v.drain().then_inc(s["m_rdy"], 1)
                v.wait_ge(s["v_tr"], 1)
                v.sem_inc(s["v_tr"], -1)
                V.tensor_copy(va[e][:], V_[:, 0:128].rearrange("p (g c) -> p g c", g=2)).then_inc(in_free[e], 1)
                V.tensor_copy(vb[e][:], V_[0:64, 128:256].rearrange("p (g c) -> p g c", g=2))
                v.drain().then_inc(s["v_ev"], 1)

            def body(t, e, nxt, before=True):
                v.wait_ge(s["t_rdy"], 1)
                v.sem_inc(s["t_rdy"], -1)
                V.tensor_copy(pa_t[:], TA[:].rearrange("p (h q) -> p h q", h=NH)).then_inc(s["ta_d"], 1)
                V.tensor_tensor(ls[e][:], ls[e][:], es[e][:], ALU.add)
                v.drain()
                V.reciprocal(ls[e][:], ls[e][:])
                v.drain()
                if nxt:
                    maxima(1 - e)
                v.wait_ge(s["o_rdy"], 1)
                v.sem_inc(s["o_rdy"], -1)
                V.tensor_tensor(on[e][:].rearrange("p (h c) -> p h c", h=NH), O[:, 0:NH * HD].rearrange("p (h c) -> p h c", h=NH),
                                ls[e][:].rearrange("p (h o) -> p h o", o=1).to_broadcast([128, NH, HD]), ALU.mult).then_inc(s["on_rdy"], 1)
            loop(v, lambda: maxima(0), body)

        @block.scalar
        def _(act):
            A = nc.scalar.activation
            for e in two:
                act.sem_inc(yo_st[e], 16)
            act.sem_inc(s["ot_free"], 1)

            def out_ev(e):
                act.wait_ge(s["ot_rdy"], 1)
                act.sem_inc(s["ot_rdy"], -1)
                act.wait_ge(yo_st[e], 16)
                act.sem_inc(yo_st[e], -16)
                nc.scalar.copy(yo[e][:], OT[:, 0:256].rearrange("p (k q) -> p k q", k=2)).then_inc(yo_rdy[e], 1)
                act.drain().then_inc(s["ot_free"], 1)

            def exps(e):
                act.wait_ge(s["m_rdy"], 1)
                act.sem_inc(s["m_rdy"], -1)
                A(es[e][:], es[e][:], ACT.Exp)
                for h in range(NH):
                    A(pb[e][:, h, :], sc[e][:, h, :], ACT.Exp, bias=nm[e][:, h:h + 1], accum_out=ls[e][:, h:h + 1])
                act.drain().then_inc(s["p_rdy"], 1)

            def body(t, e, nxt, before=True):
                act.wait_ge(s["tt_rdy"], 1)
                act.sem_inc(s["tt_rdy"], -1)
                nc.scalar.copy(pb_t[:], TB_[:].rearrange("p (h q) -> p h q", h=NH)).then_inc(s["tb_a"], 1)
                if before:
                    out_ev(1 - e)
                if nxt:
                    exps(1 - e)
            loop(act, lambda: exps(0), body)
            out_ev(1)


def phase_out(nc, l, projT, rw, par, consts, mixT, xT, wo_hi, wo_lo):
    with ExitStack() as ctx:
        P = Phase(nc, ctx, "ou")
        two = range(2)
        pars, bones = P.sb("pars", [128, NPAR]), P.sb("bones", [128, 128])
        y = [P.sb(f"y{q}", [128, KC, TB]) for q in two]
        g = P.sb("g", [128, KC, TB])
        cv = [P.sb(f"cv{q}", [128, 3, 2, TB + 2]) for q in two]
        bv = [P.sb(f"bv{q}", [128, 2, TB]) for q in two]
        th, sq = P.sb("th", [128, KC, TB]), P.sb("sq", [128, 2, TB])
        m_hi, m_lo = P.sb("m_hi", [128, KC, TB], F32R), P.sb("m_lo", [128, KC, TB], F32R)
        stage = [P.sb(f"stage{q}", [128, TB]) for q in two]
        pm, pv = P.ps("pm", [128, 2, TB]), P.ps("pv", [128, 2, TB])
        NA = 4
        acc = [P.ps(f"acc{q}", [128, TB]) for q in range(NA)]
        names = ("c_in", "th_rdy", "u_rdy", "pm_rdy", "sq_rdy", "pv_rdy", "v_rdy", "r_rdy", "mix_rdy", "hi_rdy", "lo_rdy", "m_free", "g_in", "g_free")
        s = {n: P.sem(n) for n in names}
        acc_rdy, acc_free = ([P.sem(f"{n}{q}") for q in range(NA)] for n in ("acc_rdy", "acc_free"))
        cv_in, y_in, y_free, stage_in, stage_rdy, stage_st = (
            [P.sem(f"{n}{q}") for q in two] for n in ("cv_in", "y_in", "y_free", "stage_in", "stage_rdy", "stage_st"))
        block = ctx.enter_context(nc.Block())
        assert NB % 2 == 0 and DM == 2 * TB

        def blocks(eng, body):
            with eng.Fori(0, NB // 2 - 1) as i:
                for q in two:
                    body(i * 2 + q, q, True, True)
            body(NB - 2, 0, True, False)
            body(NB - 1, 1, False, False)

        @block.sync
        def _(sp):
            sp.dma_start(pars[:], lay(par, l)).then_inc(s["c_in"], 16)
            sp.dma_start(bones[:], consts[:, 256:384]).then_inc(s["c_in"], 16)

            def load_block(i, q):
                cols = bass.ds(i * TB, TB)
                sp.wait_ge(y_free[q], 1)
                sp.sem_inc(y_free[q], -1)
                for n, r in enumerate((R_CB, R_CC, R_CX)):
                    sp.dma_start(cv[q][:, n], projT[r:r + GW, bass.ds(i * TB + (PAD - 2), TB + 2)].rearrange("(k p) t -> p k t", p=128)).then_inc(cv_in[q], 16)
                sp.dma_start(y[q][:, 0:6, :], mixT[0:768, cols].rearrange("(k p) t -> p k t", p=128)).then_inc(y_in[q], 16)
                sp.dma_start(bv[q][:], rw[5 * GW:6 * GW, cols].rearrange("(k p) t -> p k t", p=128)).then_inc(y_in[q], 16)

            def load_gates(i):
                sp.wait_ge(s["g_free"], 1)
                sp.sem_inc(s["g_free"], -1)
                for n, r in enumerate((R_FG, R_RG, R_SG, R_CG)):
                    sp.dma_start(g[:, 2 * n:2 * n + 2, :], projT[r:r + GW, bass.ds(i * TB + PAD, TB)].rearrange("(k p) t -> p k t", p=128)).then_inc(s["g_in"], 16)

            load_block(0, 0)
            load_gates(0)
            load_block(1, 1)

            def body(i, q, follows, load):
                cols = bass.ds(i * TB, TB)
                if follows:
                    load_gates(i + 1)
                for d in range(KC):
                    e = d % 2
                    sp.wait_ge(stage_st[e], 16)
                    sp.sem_inc(stage_st[e], -16)
                    sp.dma_start(stage[e][:], xT[d * 128:(d + 1) * 128, cols]).then_inc(stage_in[e], 16)
                    if d == 2 and load:
                        load_block(i + 2, q)
                    if d > 0:
                        sp.wait_ge(stage_rdy[1 - e], 1)
                        sp.sem_inc(stage_rdy[1 - e], -1)
                        sp.dma_start(xT[(d - 1) * 128:d * 128, cols], stage[1 - e][:]).then_inc(stage_st[1 - e], 16)
                sp.wait_ge(stage_rdy[1], 1)
                sp.sem_inc(stage_rdy[1], -1)
                sp.dma_start(xT[(KC - 1) * 128:KC * 128, cols], stage[1][:]).then_inc(stage_st[1], 16)
            blocks(sp, body)
            for q in two:
                sp.wait_ge(stage_st[q], 16)

        @block.scalar
        def _(act):
            A = nc.scalar.activation

            def gates():
                act.wait_ge(s["g_in"], 64)
                act.sem_inc(s["g_in"], -64)
                A(th[:], g[:], ACT.Tanh, scale=0.5).then_inc(s["th_rdy"], 1)
                act.wait_ge(s["v_rdy"], 1)
                act.sem_inc(s["v_rdy"], -1)
                A(sq[:], sq[:], ACT.Ln)
                act.drain()
                A(sq[:], sq[:], ACT.Exp, scale=-0.5).then_inc(s["r_rdy"], 1)

            act.sem_inc(s["g_free"], 1)
            gates()

            def body(i, q, follows, load):
                act.wait_ge(s["mix_rdy"], 1)
                act.sem_inc(s["mix_rdy"], -1)
                if follows:
                    act.sem_inc(s["g_free"], 1)
                for c in range(0, KC, 2):
                    act.wait_ge(s["m_free"], 1)
                    act.sem_inc(s["m_free"], -1)
                    A(m_hi[:, c:c + 2, :], y[q][:, c:c + 2, :], ACT.Copy).then_inc(s["hi_rdy"], 1)
                if follows:
                    gates()
            blocks(act, body)

        @block.gpsimd
        def _(pool):
            for q in two:
                pool.sem_inc(y_free[q], 1)

            def body(i, q, follows, load):
                for c in range(0, KC, 2):
                    pool.wait_ge(s["hi_rdy"], 1)
                    pool.sem_inc(s["hi_rdy"], -1)
                    nc.gpsimd.tensor_tensor(m_lo[:, c:c + 2, :], y[q][:, c:c + 2, :], m_hi[:, c:c + 2, :].bitcast(F32), ALU.subtract).then_inc(s["lo_rdy"], 1)
                pool.drain().then_inc(y_free[q], 1)
            blocks(pool, body)

        @block.tensor
        def _(pe):
            M = nc.tensor.matmul
            pe.wait_ge(s["c_in"], 32)

            def head_sums(q):
                pe.wait_ge(s["u_rdy"], 1)
                pe.sem_inc(s["u_rdy"], -1)
                for p in two:
                    ins = M(pm[:, p, :], bones[:], y[q][:, 2 + p, :], start=True, stop=True)
                ins.then_inc(s["pm_rdy"], 1)

            def head_squares():
                pe.wait_ge(s["sq_rdy"], 1)
                pe.sem_inc(s["sq_rdy"], -1)
                for p in two:
                    ins = M(pv[:, p, :], bones[:], sq[:, p, :], start=True, stop=True)
                ins.then_inc(s["pv_rdy"], 1)

            head_sums(0)
            head_squares()
            pe.sem_inc(s["m_free"], KC // 2 - 1)

            def body(i, q, follows, load):
                for d in range(KC):
                    a = acc[d % NA]
                    cs = slice(d * 128, (d + 1) * 128)
                    pe.wait_ge(acc_free[d % NA], 1)
                    pe.sem_inc(acc_free[d % NA], -1)
                    for k in range(KC):
                        if d == 0 and k % 2 == 0:
                            pe.wait_ge(s["lo_rdy"], 1)
                            pe.sem_inc(s["lo_rdy"], -1)
                        ins = M(a[:], wo_hi[:, k, cs], m_hi[:, k, :], start=(k == 0), stop=False)
                        if d == 0 and k == 0:
                            ins.then_inc(s["m_free"], 1)
                        M(a[:], wo_hi[:, k, cs], m_lo[:, k, :], start=False, stop=False)
                        ins = M(a[:], wo_lo[:, k, cs], m_hi[:, k, :], start=False, stop=(k == KC - 1))
                        if d == KC - 1 and k % 2 == 1 and k < KC - 1:
                            ins.then_inc(s["m_free"], 1)
                    ins.then_inc(acc_rdy[d % NA], 1)
                    if d == 0 and follows:
                        head_sums(1 - q)
                    if d == 2 and follows:
                        head_squares()
            blocks(pe, body)

        @block.vector
        def _(v):
            V = nc.vector
            v.wait_ge(s["c_in"], 32)
            for q in two:
                v.sem_inc(stage_st[q], 16)
            for q in range(NA):
                v.sem_inc(acc_free[q], 1)

            def add_x(d):
                e = d % 2
                v.wait_ge(acc_rdy[d % NA], 1)
                v.sem_inc(acc_rdy[d % NA], -1)
                v.wait_ge(stage_in[e], 16)
                v.sem_inc(stage_in[e], -16)
                V.tensor_tensor(stage[e][:], acc[d % NA][:], stage[e][:], ALU.add).then_inc(stage_rdy[e], 1)
                v.drain().then_inc(acc_free[d % NA], 1)

            def convolve(q):
                y_, cv_ = y[q], cv[q]
                v.wait_ge(cv_in[q], 48)
                v.sem_inc(cv_in[q], -48)
                V.tensor_tensor(cv_[:, 1], cv_[:, 1], cv_[:, 2], ALU.mult)
                v.drain()
                for p in two:
                    V.tensor_scalar(y_[:, 6 + p, :], cv_[:, 1, p, 2:TB + 2], pars[:, C_CW + 4 + p:C_CW + 5 + p], None, ALU.mult)
                for w in (1, 0):
                    v.drain()
                    for p in two:
                        V.scalar_tensor_tensor(y_[:, 6 + p, :], cv_[:, 1, p, w:TB + w], pars[:, C_CW + 2 * w + p:C_CW + 2 * w + p + 1], y_[:, 6 + p, :], ALU.mult, ALU.add)

            def mix(q, between, first=False):
                y_, g_, cv_ = y[q], g, cv[q]
                if first:
                    convolve(q)
                v.wait_ge(y_in[q], 32)
                v.sem_inc(y_in[q], -32)
                v.drain().then_inc(s["u_rdy"], 1)
                if not first:
                    convolve(q)
                v.wait_ge(s["pm_rdy"], 1)
                v.sem_inc(s["pm_rdy"], -1)
                V.scalar_tensor_tensor(y_[:, 2:4, :], pm[:], -1.0 / HD, y_[:, 2:4, :], ALU.mult, ALU.add)
                v.drain()
                V.tensor_tensor(sq[:], y_[:, 2:4, :], y_[:, 2:4, :], ALU.mult).then_inc(s["sq_rdy"], 1)
                between(0)
                V.tensor_tensor(y_[:, 6:8, :], y_[:, 6:8, :], cv_[:, 0, :, 2:TB + 2], ALU.mult)
                between(1)
                v.wait_ge(s["pv_rdy"], 1)
                v.sem_inc(s["pv_rdy"], -1)
                V.tensor_scalar(sq[:], pv[:], 1.0 / HD, LN_EPS, ALU.mult, ALU.add).then_inc(s["v_rdy"], 1)
                between(2)
                v.wait_ge(s["th_rdy"], 1)
                v.sem_inc(s["th_rdy"], -1)
                V.scalar_tensor_tensor(g_[:, 0:4, :], th[:, 0:4, :], 1.0, g_[:, 0:4, :], ALU.add, ALU.mult)
                V.scalar_tensor_tensor(g_[:, 4:8, :], th[:, 4:8, :], 1.0, g_[:, 4:8, :], ALU.add, ALU.mult)
                between(3)
                v.wait_ge(s["r_rdy"], 1)
                v.sem_inc(s["r_rdy"], -1)
                V.tensor_tensor(y_[:, 2:4, :], y_[:, 2:4, :], sq[:], ALU.mult)
                v.drain()
                for p in two:
                    V.tensor_scalar(y_[:, 2 + p, :], y_[:, 2 + p, :], pars[:, C_LG + p:C_LG + p + 1], pars[:, C_LB + p:C_LB + p + 1], ALU.mult, ALU.add)
                v.drain()
                V.tensor_tensor(y_[:, 2:4, :], y_[:, 2:4, :], bv[q][:], ALU.add)
                between(4)
                v.drain()
                V.scalar_tensor_tensor(y_[:, 0:4, :], g_[:, 0:4, :], 0.5, y_[:, 0:4, :], ALU.mult, ALU.mult)
                between(5)
                V.scalar_tensor_tensor(y_[:, 4:8, :], g_[:, 4:8, :], 0.5, y_[:, 4:8, :], ALU.mult, ALU.mult).then_inc(s["mix_rdy"], 1)
                between(6)
                between(7)

            mix(0, lambda d: None, first=True)

            def body(i, q, follows, load):
                if follows:
                    mix(1 - q, add_x)
                else:
                    for d in range(KC):
                        add_x(d)
            blocks(v, body)


def hybrid_trunk(nc, x, w_in, w_out, par, lora, consts, masks, rope, out, layers=L, debug=None):
    def dram(n, shape):
        return nc.dram_tensor(n, shape, F32, kind="ExternalOutput" if debug else "Internal").ap()

    xT, mixT = dram("xT", (DM, T)), dram("mixT", (DM, T))
    projT = dram("projT", (DIN, PAD + T))
    rw, pend, fa = dram("rw", (6 * GW, T)), dram("pend", (GW, T // CH)), dram("fa", (4 * NH, T))
    phase_transpose(nc, consts, x, xT, projT)
    with nc.Fori(0, layers) as l:
        with nc.sbuf_tensor("h_hi", [128, KC, T], F32R) as h_hi, nc.sbuf_tensor("h_lo", [128, KC, T], F32R) as h_lo:
            phase_project(nc, l, xT, w_in, par, consts, projT, h_hi, h_lo)
            phase_rwkv_prep(nc, l, projT, par, lora, consts, rw, pend, w_in, h_hi, h_lo)
            phase_rwkv_scan(nc, l, rw, pend, consts, masks, mixT, w_in, projT, h_hi, h_lo)
        phase_head_norm(nc, l, projT, par, consts, rope, fa)
        phase_fox(nc, l, projT, fa, consts, mixT)
        with nc.sbuf_tensor("wo_hi", [128, KC, DM], F32R) as wo_hi, nc.sbuf_tensor("wo_lo", [128, KC, DM], F32R) as wo_lo:
            phase_swa(nc, l, projT, par, consts, masks, mixT, w_out, wo_hi, wo_lo)
            phase_out(nc, l, projT, rw, par, consts, mixT, xT, wo_hi, wo_lo)
    phase_transpose(nc, consts, xT, out)


def constants():
    i = np.arange(128)
    eye = np.eye(128)
    same = lambda n: (i[:, None] // n) == (i[None, :] // n)
    reset = np.tile(np.where(np.arange(TB) % CH == 0, 0.0, 1.0), (128, 1))
    perm = np.zeros((128, 128))
    perm[i, i ^ 32] = 1.0
    causal = np.where(i[None, :] <= i[:, None], 0.0, -1e30)
    gather = (np.arange(14)[None, None, :] == 2 * np.arange(7)[None, :, None] + i[:, None, None] // 64) * 1.0
    spread = np.zeros((128, 7, 128))
    spread[0:14] = gather.transpose(2, 1, 0)
    consts = np.concatenate([eye, np.ones((128, 128)), same(64), reset, perm, causal, gather.reshape(128, -1), spread.reshape(128, -1)], 1)
    assert consts.shape[1] == NCONST
    low = i[None, :] < i[:, None]
    m = [low & same(16), low & same(32) & ~same(16), low & same(64) & ~same(32), (low & same(16)).T, (low & same(64)).T, ((low | (eye > 0)) & same(64)).T]
    k = np.arange(192)
    win = (k[None, :] // 64 == i[:, None] // 64) | (k[None, :] // 64 == i[:, None] // 64 + 1)
    w1 = np.where(win, 0.0, -1e30)
    w0 = np.where(win & (k[None, :] >= 64), 0.0, -1e30)
    masks = np.concatenate([a.astype(np.float32) for a in m] + [w0, w1], 1)
    half = HD // 2
    inv = np.float32(10000.0) ** (-np.arange(half, dtype=np.float32) / np.float32(half))
    ang = np.arange(T, dtype=np.float32)[None, :] * inv[:, None].astype(np.float32)
    cos, sin = np.cos(ang), np.sin(ang)
    rope = np.concatenate([np.tile(np.concatenate([cos, cos]), (2, 1)), np.tile(np.concatenate([-sin, sin]), (2, 1))], 1)
    return [np.ascontiguousarray(a, dtype=np.float32) for a in (consts, masks, rope)]


def pack_parameters(a):
    def cols(n):
        v = a[n].reshape(L, -1, 128)
        return v.transpose(0, 2, 1)

    def twice(n):
        return np.concatenate([a[n], a[n]], 1)[:, :, None]

    bf = np.zeros((L, 128, 1), a["fox_b_f"].dtype)
    bf[:, 0:NH, 0] = a["fox_b_f"]
    parts = [cols(n) for n in ("norm_g", "rwkv_mu", "rwkv_w0", "rwkv_a0", "rwkv_k_k", "rwkv_k_a", "rwkv_r_k", "rwkv_ln_g", "rwkv_ln_b")]
    parts += [twice("fox_q_norm")] * 2 + [twice("fox_k_norm")] * 2 + [twice("swa_q_norm")] * 2 + [twice("swa_k_norm")]
    parts += [cols("conv_w"), np.repeat(a["swa_sinks"][:, None, :], 128, 1), bf]
    return np.ascontiguousarray(np.concatenate(parts, 2))


LAYERS, DEBUG = L, None


def kernel(**inputs):
    import concourse.bacc as bacc
    from concourse.bass_utils import run_bass_kernel_spmd as run

    a = {n: np.ascontiguousarray(v) for n, v in inputs.items()}
    consts, masks, rope = constants()
    feeds = {
        "x": a["x"].reshape(T, DM), "w_in": a["w_in"], "w_out": a["w_out"], "par": pack_parameters(a),
        "lora": np.ascontiguousarray(np.concatenate([a["rwkv_w_up"], a["rwkv_a_up"]], 1)),
        "consts": consts, "masks": masks, "rope": rope,
    }
    nc = bacc.Bacc("TRN2", target_bir_lowering=False, num_devices=1)
    args = [nc.dram_tensor(n, v.shape, F32, kind="ExternalInput").ap() for n, v in feeds.items()]
    args.append(nc.dram_tensor("out", (T, DM), F32, kind="ExternalOutput").ap())
    hybrid_trunk(nc, *args, layers=LAYERS, debug=DEBUG)
    r = run(nc, [feeds], core_ids=[0])
    return r.results[0]["out"].reshape(1, T, DM)
```
